# Optimizing a Trainium2 kernel written in Bass

```python
import math
import jax, jax.numpy as jnp
from jax import lax
import numpy as np

D_MODEL = 1024
BATCH = 1
SEQ = 512
DEPTH = 2

N_MEM = 256
EPS = 1e-6

POOL_WINDOWS = (2, 4, 8, 16)
POOL_MAX_W = max(POOL_WINDOWS)
POOL_GROUPS = len(POOL_WINDOWS)
POOL_WIDTH = D_MODEL // 2
POOL_GROUP_DIM = POOL_WIDTH // POOL_GROUPS
SGU_WIDTH = D_MODEL // 2
SGU_GROUPS = 4
SGU_GROUP_DIM = SGU_WIDTH // SGU_GROUPS
SGU_CHUNK = 128
EVEN_IN = POOL_WIDTH + 2 * SGU_WIDTH

DIL_HEADS = 8
DIL_HEAD_DIM = 64
DIL_WIDTH = DIL_HEADS * DIL_HEAD_DIM
DIL_PAIRS = ((128, 1), (512, 4), (2048, 16))
DIL_BLOCK = 128
ROPE_THETA = 500000.0
ROPE_DIM = DIL_HEAD_DIM // 4
RET_HEADS = 4
RET_HEAD_DIM = 128
RET_WIDTH = RET_HEADS * RET_HEAD_DIM
RET_CHUNK = 128
RET_THETA = 10000.0
ODD_SIZES = (DIL_WIDTH, DIL_WIDTH, DIL_WIDTH, RET_WIDTH, RET_WIDTH, RET_WIDTH, RET_WIDTH)
ODD_IN = sum(ODD_SIZES)

XATTN_HEADS = 4
XATTN_HEAD_DIM = D_MODEL // XATTN_HEADS
D_FF = -(-8 * D_MODEL // (3 * 256)) * 256

N_EVEN = (DEPTH + 1) // 2
N_ODD = DEPTH // 2

kernel_name = "hybrid_pool_sgu_dilated_retention_block"

def rmsnorm(x, g):
    xf = x.astype(jnp.float32)
    y = xf * lax.rsqrt(jnp.mean(xf * xf, axis=-1, keepdims=True) + EPS)
    return (y * g.astype(jnp.float32)).astype(x.dtype)

def rotary(x, pos, rot_dim, theta):
    half = rot_dim // 2
    inv = 1.0 / jnp.power(jnp.float32(theta), jnp.arange(half, dtype=jnp.float32) / half)
    ang = pos.astype(jnp.float32)[:, None] * inv[None, :]
    cos = jnp.cos(ang)[None, :, None, :]
    sin = jnp.sin(ang)[None, :, None, :]
    xr = x[..., :rot_dim].astype(jnp.float32)
    x1, x2 = xr[..., :half], xr[..., half:]
    rot = jnp.concatenate([x1 * cos - x2 * sin, x1 * sin + x2 * cos], axis=-1).astype(x.dtype)
    return jnp.concatenate([rot, x[..., rot_dim:]], axis=-1)

def pool_mixer(a, w, scale):
    B, S, _ = a.shape
    ag = a.reshape(B, S, POOL_GROUPS, POOL_GROUP_DIM).astype(jnp.float32)
    cs = jnp.pad(jnp.cumsum(ag, axis=1), ((0, 0), (POOL_MAX_W, 0), (0, 0), (0, 0)))
    t = jnp.arange(S)
    outs = []
    for g, win in enumerate(POOL_WINDOWS):
        csg = cs[:, :, g]
        wsum = csg[:, POOL_MAX_W:] - csg[:, POOL_MAX_W - win:POOL_MAX_W - win + S]
        cnt = jnp.minimum(t + 1, win).astype(jnp.float32)[None, :, None]
        outs.append(wsum / cnt - ag[:, :, g])
    d = jnp.stack(outs, axis=2).astype(a.dtype)
    y = jnp.einsum('bsgc,gcd->bsgd', d, w)
    return y.reshape(B, S, POOL_WIDTH) * scale

def sgu_mixer(u, v, norm_g, w_s, b_s):
    B, S, _ = u.shape
    n = S // SGU_CHUNK
    vc = rmsnorm(v, norm_g).reshape(B, n, SGU_CHUNK, SGU_GROUPS, SGU_GROUP_DIM)
    causal = jnp.tril(jnp.ones((SGU_CHUNK, SGU_CHUNK), dtype=bool))
    ws = jnp.where(causal[None], w_s, jnp.zeros_like(w_s))
    mixed = jnp.einsum('gts,bnsgc->bntgc', ws, vc) + jnp.transpose(b_s)[None, None, :, :, None]
    return u * mixed.reshape(B, S, SGU_WIDTH)

def even_mixer(h, w_in, pool_w, pool_scale, sgu_norm, sgu_w, sgu_b, w_out):
    z = h @ w_in
    a = z[..., :POOL_WIDTH]
    uv = jax.nn.gelu(z[..., POOL_WIDTH:])
    u, v = uv[..., :SGU_WIDTH], uv[..., SGU_WIDTH:]
    ya = pool_mixer(a, pool_w, pool_scale)
    yb = sgu_mixer(u, v, sgu_norm, sgu_w, sgu_b)
    return jnp.concatenate([ya, yb], axis=-1) @ w_out

def dilated_branch(q, k, v, dil, steps):
    B, S, H, dh = q.shape
    L = -(-S // dil)
    L = -(-L // DIL_BLOCK) * DIL_BLOCK
    nb = L // DIL_BLOCK
    S_pad = L * dil
    pad = ((0, 0), (0, S_pad - S), (0, 0), (0, 0))

    def sub(t):
        t = jnp.pad(t, pad).reshape(B, L, dil, H, dh)
        return jnp.moveaxis(t, 2, 1).reshape(B, dil, nb, DIL_BLOCK, H, dh)

    def with_prev(t):
        prev = jnp.pad(t, ((0, 0), (0, 0), (1, 0), (0, 0), (0, 0), (0, 0)))[:, :, :-1]
        return jnp.concatenate([prev, t], axis=3)

    qs = sub(q)
    kk = with_prev(sub(k))
    vv = with_prev(sub(v))
    scores = jnp.einsum('brnqhd,brnkhd->brnhqk', qs, kk).astype(jnp.float32) * (dh ** -0.5)
    qi = jnp.arange(DIL_BLOCK)[:, None] + DIL_BLOCK
    ki = jnp.arange(2 * DIL_BLOCK)[None, :]
    dist = qi - ki
    band = (dist >= 0) & (dist <= steps)
    has_prev = (jnp.arange(nb) > 0)[:, None, None]
    mask = band[None] & (has_prev | (ki >= DIL_BLOCK)[None])
    scores = jnp.where(mask[None, None, :, None], scores, -jnp.inf)
    m = jnp.max(scores, axis=-1, keepdims=True)
    p = jnp.exp(scores - m)
    s = jnp.sum(p, axis=-1)
    o = jnp.einsum('brnhqk,brnkhd->brnqhd', p, vv.astype(jnp.float32))
    o = o / jnp.swapaxes(s, 3, 4)[..., None]
    lse = jnp.swapaxes(m[..., 0] + jnp.log(s), 3, 4)

    def unsub(t):
        t = t.reshape((B, dil, L) + t.shape[4:])
        t = jnp.moveaxis(t, 1, 2)
        return t.reshape((B, S_pad) + t.shape[3:])[:, :S]

    return unsub(o), unsub(lse)

def dilated_mixture(q, k, v, pos):
    q = rotary(q, pos, ROPE_DIM, ROPE_THETA)
    k = rotary(k, pos, ROPE_DIM, ROPE_THETA)
    outs, lses = [], []
    for window, dil in DIL_PAIRS:
        o, lse = dilated_branch(q, k, v, dil, window // dil)
        outs.append(o)
        lses.append(lse)
    wts = jax.nn.softmax(jnp.stack(lses, axis=0), axis=0)
    return jnp.einsum('gbsh,gbshd->bshd', wts, jnp.stack(outs, axis=0))

def retention(q, k, v, pos):
    B, S, H, dk = q.shape
    dv = v.shape[-1]
    C = RET_CHUNK
    n = S // C
    q = rotary(q, pos, dk, RET_THETA).astype(jnp.float32)
    k = rotary(k, pos, dk, RET_THETA).astype(jnp.float32) * (dk ** -0.5)
    v = v.astype(jnp.float32)
    gamma = 1.0 - jnp.power(2.0, -5.0 - jnp.arange(H, dtype=jnp.float32))
    log_g = jnp.log(gamma)
    qc = q.reshape(B, n, C, H, dk)
    kc = k.reshape(B, n, C, H, dk)
    vc = v.reshape(B, n, C, H, dv)
    idx = jnp.arange(C, dtype=jnp.float32)
    rel = idx[:, None] - idx[None, :]
    decay = jnp.where(rel[None] >= 0, jnp.exp(jnp.maximum(rel, 0.0)[None] * log_g[:, None, None]), 0.0)
    inner = jnp.einsum('bnihd,bnjhd->bnhij', qc, kc) * decay[None, None]
    y_inner = jnp.einsum('bnhij,bnjhe->bnihe', inner, vc)
    k_decay = jnp.exp((C - 1 - idx)[None, :] * log_g[:, None])
    q_decay = jnp.exp((idx + 1)[None, :] * log_g[:, None])
    chunk_kv = jnp.einsum('bnjhd,hj,bnjhe->bnhde', kc, k_decay, vc)
    g_chunk = jnp.exp(C * log_g)[None, :, None, None]

    def step(state, kv):
        return state * g_chunk + kv, state

    init = jnp.zeros((B, H, dk, dv), jnp.float32)
    _, prev = lax.scan(step, init, jnp.moveaxis(chunk_kv, 1, 0))
    prev = jnp.moveaxis(prev, 0, 1)
    y_cross = jnp.einsum('bnihd,bnhde,hi->bnihe', qc, prev, q_decay)
    y = (y_inner + y_cross).reshape(B, S, H, dv)
    mu = jnp.mean(y, axis=-1, keepdims=True)
    var = jnp.mean(jnp.square(y - mu), axis=-1, keepdims=True)
    return (y - mu) * lax.rsqrt(var + EPS)

def odd_mixer(h, pos, w_in, w_out):
    B, S, _ = h.shape
    z = h @ w_in
    cuts = [int(c) for c in np.cumsum(ODD_SIZES)[:-1]]
    cq, ck, cv, rq, rk, rv, rg = jnp.split(z, cuts, axis=-1)
    dshape = (B, S, DIL_HEADS, DIL_HEAD_DIM)
    rshape = (B, S, RET_HEADS, RET_HEAD_DIM)
    yc = dilated_mixture(cq.reshape(dshape), ck.reshape(dshape), cv.reshape(dshape), pos)
    yc = yc.reshape(B, S, DIL_WIDTH).astype(h.dtype)
    yr = retention(rq.reshape(rshape), rk.reshape(rshape), rv.reshape(rshape), pos)
    yd = jax.nn.silu(rg) * yr.reshape(B, S, RET_WIDTH).astype(h.dtype)
    return jnp.concatenate([yc, yd], axis=-1) @ w_out

def memory_cross_attention(h, mem_n, wq, wkv, wo):
    B, S, _ = h.shape
    M = mem_n.shape[1]
    q = (h @ wq).reshape(B, S, XATTN_HEADS, XATTN_HEAD_DIM)
    kv = (mem_n @ wkv).reshape(B, M, 2, XATTN_HEADS, XATTN_HEAD_DIM)
    k, v = kv[:, :, 0], kv[:, :, 1]
    s = jnp.einsum('bqhd,bkhd->bhqk', q, k).astype(jnp.float32) * (XATTN_HEAD_DIM ** -0.5)
    p = jax.nn.softmax(s, axis=-1).astype(v.dtype)
    o = jnp.einsum('bhqk,bkhd->bqhd', p, v).reshape(B, S, D_MODEL)
    return o @ wo

def swiglu(h, w_gate_up, w_down):
    gu = h @ w_gate_up
    g, u = gu[..., :D_FF], gu[..., D_FF:]
    return (jax.nn.silu(g) * u) @ w_down

def setup_inputs(seed: int = 0) -> dict:
    key = jax.random.key(seed)
    ks = iter(jax.random.split(key, 32))
    f32 = jnp.float32

    def normal(shape, fan_in):
        return jax.random.normal(next(ks), shape, f32) * (fan_in ** -0.5)

    def gain(shape):
        return 1.0 + 0.02 * jax.random.normal(next(ks), shape, f32)

    return {
        "x": jax.random.normal(next(ks), (BATCH, SEQ, D_MODEL), f32),
        "mem": jax.random.normal(next(ks), (BATCH, N_MEM, D_MODEL), f32),
        "even_mix_norm": gain((N_EVEN, D_MODEL)),
        "even_w_in": normal((N_EVEN, D_MODEL, EVEN_IN), D_MODEL),
        "pool_w": normal((N_EVEN, POOL_GROUPS, POOL_GROUP_DIM, POOL_GROUP_DIM), POOL_GROUP_DIM),
        "pool_scale": gain((N_EVEN, POOL_WIDTH)),
        "sgu_norm": gain((N_EVEN, SGU_WIDTH)),
        "sgu_w": normal((N_EVEN, SGU_GROUPS, SGU_CHUNK, SGU_CHUNK), SGU_CHUNK),
        "sgu_b": gain((N_EVEN, SGU_GROUPS, SGU_CHUNK)),
        "even_w_out": normal((N_EVEN, POOL_WIDTH + SGU_WIDTH, D_MODEL), POOL_WIDTH + SGU_WIDTH),
        "odd_mix_norm": gain((N_ODD, D_MODEL)),
        "odd_w_in": normal((N_ODD, D_MODEL, ODD_IN), D_MODEL),
        "odd_w_out": normal((N_ODD, DIL_WIDTH + RET_WIDTH, D_MODEL), DIL_WIDTH + RET_WIDTH),
        "xattn_norm": gain((DEPTH, D_MODEL)),
        "mem_norm": gain((DEPTH, D_MODEL)),
        "xattn_wq": normal((DEPTH, D_MODEL, D_MODEL), D_MODEL),
        "xattn_wkv": normal((DEPTH, D_MODEL, 2 * D_MODEL), D_MODEL),
        "xattn_wo": normal((DEPTH, D_MODEL, D_MODEL), D_MODEL),
        "ffn_norm": gain((DEPTH, D_MODEL)),
        "ffn_w_gate_up": normal((DEPTH, D_MODEL, 2 * D_FF), D_MODEL),
        "ffn_w_down": normal((DEPTH, D_FF, D_MODEL), D_FF),
        "final_norm": gain((D_MODEL,)),
    }

def reference(x, mem, even_mix_norm, even_w_in, pool_w, pool_scale, sgu_norm, sgu_w, sgu_b,
              even_w_out, odd_mix_norm, odd_w_in, odd_w_out, xattn_norm, mem_norm, xattn_wq,
              xattn_wkv, xattn_wo, ffn_norm, ffn_w_gate_up, ffn_w_down, final_norm):
    pos = jnp.arange(x.shape[1], dtype=jnp.int32)
    h = x
    for layer in range(DEPTH):
        i = layer // 2
        if layer % 2 == 0:
            h = h + even_mixer(rmsnorm(h, even_mix_norm[i]), even_w_in[i], pool_w[i], pool_scale[i],
                               sgu_norm[i], sgu_w[i], sgu_b[i], even_w_out[i])
        else:
            h = h + odd_mixer(rmsnorm(h, odd_mix_norm[i]), pos, odd_w_in[i], odd_w_out[i])
        h = h + memory_cross_attention(rmsnorm(h, xattn_norm[layer]), rmsnorm(mem, mem_norm[layer]),
                                       xattn_wq[layer], xattn_wkv[layer], xattn_wo[layer])
        h = h + swiglu(rmsnorm(h, ffn_norm[layer]), ffn_w_gate_up[layer], ffn_w_down[layer])
    return rmsnorm(h, final_norm)


_drawn_inputs = setup_inputs


def setup_inputs(seed=0):
    import zlib

    import numpy as np

    out = dict(_drawn_inputs(seed))
    spreads = {}
    factors = {'even_mix_norm': 3.057,
     'pool_scale': 4.463,
     'sgu_norm': 8.0,
     'sgu_b': 6.559,
     'odd_mix_norm': 4.555,
     'xattn_norm': 8.0,
     'mem_norm': 8.0,
     'ffn_norm': 3.24,
     'final_norm': 2.754}
    for name, (base, spread) in spreads.items():
        noise = np.random.default_rng([zlib.crc32(name.encode()), seed]).standard_normal(out[name].shape)
        drawn = base * np.exp(spread * noise) if base else spread * noise
        out[name] = __import__('jax').numpy.asarray(drawn.astype(out[name].dtype))
    for name, factor in factors.items():
        out[name] = (out[name] * factor).astype(out[name].dtype)
    return out
```

```python
from contextlib import ExitStack

import numpy as np

import concourse.bass as bass
from concourse import mybir

F32 = mybir.dt.float32
F32R = mybir.dt.float32r
ACT = mybir.ActivationFunctionType
ALU = mybir.AluOpType
AX = mybir.AxisListType

P = 128
D = 1024
S = 512
M = 256
KT = D // P
TT = S // P
MT = M // P
DFF = 2816
FT = DFF // P
EPS = 1e-6
LAYERS = 2
RING = 4
LEAD = 3
UW = 1024
WINDOWS = (2, 4, 8, 16)
PAD = 16
DIL_H, RET_H, X_H = 8, 4, 4
DH = 64
NEG = -1e30

U_V, U_A, U_U, U_OUT0 = 0, 4, 8, 12
U_DV, U_DQK, U_RV, U_RQK, U_RG, U_OUT1 = 0, 4, 12, 16, 24, 28
X_K, X_V, X_Q, X_O, X_END = 0, 8, 16, 24, 32
F_GU, F_DN, F_END = 0, 2 * FT, 2 * FT + 3 * KT
MIX_UNITS = (20, 36)
UNIT0 = [0, MIX_UNITS[0] + X_END + F_END]
UNITS = sum(MIX_UNITS) + LAYERS * (X_END + F_END)

A_MIX = (4 + 4 + 4 + 4 + 4 + 8, 4 + 8 + 4 + 4 + 8 + 4 + 4 + 8)
A_X = 8 + 4 + 8 + 8 + 8
A_F = 2 * FT + KT
ACC0 = [0, A_MIX[0] + A_X + A_F]

C_EVEN, C_ODD, C_XN, C_FN, C_MN, C_PS, C_ALL = 0, 8, 16, 32, 48, 64, 68


def aux_plan():
    who, at = [], {}

    def add(name, s):
        at[name] = len(who)
        who.extend(s)

    add("x", "v" * 8)
    add(("row", 0), "v")
    add("mem", "vvvv")
    for layer in range(LAYERS):
        if layer:
            add(("mean", 3 * layer), "v")
            add(("row", 3 * layer), "v")
            add("rotd", "v" * 8)
            order_dil(lambda h: add(("ds", h), "vvvv"), lambda h: add(("dt", h), "aaa"), lambda h: None)
            add("rotr", "v" * 8)
            order_ret(lambda h: add(("rs", h), "vvv"), lambda h: None, lambda h: add(("rt", h), "v"))
        add(("mean", 3 * layer + 1), "v")
        add(("row", 3 * layer + 1), "v")
        order_dil(lambda h: add(("xs", layer, h), "aa"), lambda h: add(("xt", layer, h), "aa"),
                  lambda h: None, X_H)
        add(("mean", 3 * layer + 2), "v")
        add(("row", 3 * layer + 2), "v")
    add(("mean", 6), "v")
    add("out", "v" * 8)
    return who, at


def order_dil(scores, turn, values, heads=DIL_H):
    scores(0)
    for h in range(heads):
        if h + 1 < heads:
            scores(h + 1)
        turn(h)
        values(h)


def order_ret(scores, values, turn):
    scores(0)
    for h in range(RET_H):
        if h + 1 < RET_H:
            scores(h + 1)
        values(h)
        if h:
            turn(h - 1)
    turn(RET_H - 1)


BLOCK = {0: (0, 512), 1: (512, 384), 3: (896, 128), 2: (1024, 256)}
ROWS = {0: (0, 128), 1: (128, 256), 2: (384, 384), 3: (768, 512)}


def program(nc, d):
    who, aux_at = aux_plan()

    with ExitStack() as ctx:
        def sem(name):
            return ctx.enter_context(nc.semaphore(name))

        def fixed(name, shape, dt=F32):
            return ctx.enter_context(nc.sbuf_tensor(name, shape, dt))

        base = (nc.sbuf_base + 31) // 32 * 32
        fixed("arena", [P, 88 * 256])

        def at(name, kib, shape, dt=F32):
            return nc.alloc_sbuf_tensor_at(name, shape, dt, offset=int(base + kib * 1024))

        act_hi = at("act_hi", 0, [P, FT, S], F32R)
        act_lo = at("act_lo", 44, [P, FT, S], F32R)
        y_hi = at("y_hi", 0, [P, KT, S], F32R)
        y_lo = at("y_lo", 16, [P, KT, S], F32R)
        x_tok = at("x_tok", 0, [P, TT, D])
        mem_tok = at("mem_tok", 16, [P, MT, D])
        vn = at("vn", 32, [P, TT, S])
        uu = at("uu", 40, [P, 4, S])
        a_pad = at("a_pad", 48, [P, 4, PAD + S])
        wsum = at("wsum", 56.5, [P, 3, PAD + S])
        dd = at("dd", 64, [P, 4, S])
        ws_t = at("ws_t", 72, [P, 4, P])
        pool_w = at("pool_w", 74, [P, 4, P])
        sgu_b = at("sgu_b", 76, [P, 4, P])
        sgu_g = at("sgu_g", 78, [P, S])
        junk = at("junk", 80, [P, D])
        mem_hi = at("mem_hi", 32, [P, KT, M], F32R)
        mem_lo = at("mem_lo", 40, [P, KT, M], F32R)
        xk = at("xk", 48, [P, KT, M])
        xv = at("xv", 56, [P, MT, D])
        xq = at("xq", 64, [P, KT, S])
        xp = at("xp", 80, [P, 2, TT, M])
        xpt = at("xpt", 32, [P, MT, S])
        cs_r = at("cs_r", 32, [P, 2, S])
        perm = at("perm", 36, [P, 2, P])
        band = at("band", 37, [P, S])
        tv = at("tv", 40, [P, TT, S])
        tq = at("tq", 48, [P, 8, S])
        cs_d = at("cs_d", 64, [P, 2, S])
        dp = at("dp", 64, [P, 2, 1280])
        dpt = at("dpt", 74, [P, 1280])
        gate = at("gate", 64, [P, 4, S])
        inner = at("inner", 72, [P, 2, 1280])
        decay012 = at("decay012", 82, [P, 3, S])
        decay3 = at("decay3", 37, [P, S])

        hT = fixed("hT", [P, KT, S])
        u_hi = fixed("u_hi", [P, KT, S], F32R)
        u_lo = fixed("u_lo", [P, KT, S], F32R)
        raw = fixed("raw", [P, RING, UW])
        w_hi = fixed("w_hi", [P, RING, UW], F32R)
        w_lo = fixed("w_lo", [P, RING, UW], F32R)
        memT = fixed("memT", [P, KT, M])
        tmp = fixed("tmp", [P, 4, S])
        diag = tmp[:, 3, :]
        fin_g = memT[:, 0:KT // 2, :].rearrange("p a b -> p (a b)")
        sqsum = fixed("sqsum", [P, S])
        rstd_row = fixed("rstd_row", [P, S])
        ident = fixed("ident", [P, P])
        ones = fixed("ones", [P, P])
        vecs = fixed("vecs", [P, C_ALL])
        invcnt = fixed("invcnt", [P, 4, PAD])
        mean_w = fixed("mean_w", [P, 1])
        mexp = fixed("mexp", [P, TT])
        ssq = fixed("ssq", [P, TT])
        ssq_m = fixed("ssq_m", [P, MT])
        ssq_v = fixed("ssq_v", [P, TT])
        var_e = fixed("var_e", [P, TT])
        var_m = fixed("var_m", [P, MT])
        var_v = fixed("var_v", [P, TT])
        rstd_tok = fixed("rstd_tok", [P, TT])
        rstd_m = fixed("rstd_m", [P, MT])
        rstd_v = fixed("rstd_v", [P, TT])
        nmax = fixed("nmax", [P, 2, TT])
        psums = fixed("psums", [P, 2, TT])
        pinv = fixed("pinv", [P, 2, TT])
        stats = fixed("stats", [P, TT, 6])
        mv = fixed("mv", [P, TT, 2])
        rvar = fixed("rvar", [P, 2, TT])
        rrstd = fixed("rrstd", [P, 2, TT])

        accs = [ctx.enter_context(nc.psum_tensor(f"acc{i}", [P, 512], F32)) for i in range(4)]
        auxs = [ctx.enter_context(nc.psum_tensor(f"aux{i}", [P, 512], F32)) for i in range(4)]

        raw_in = [sem(f"raw_in{i}") for i in range(RING)]
        hi_ready = sem("hi_ready")
        lo_ready = sem("lo_ready")
        unit_used = sem("unit_used")
        acc_done = sem("acc_done")
        acc_drained = sem("acc_drained")
        aux_done = sem("aux_done")
        aux_free_v = sem("aux_free_v")
        aux_free_a = sem("aux_free_a")
        x_in = sem("x_in")
        mem_in = sem("mem_in")
        c0_in = sem("c0_in")
        c1_in = sem("c1_in")
        c2_in = sem("c2_in")
        c3_in = sem("c3_in")
        fin_in = sem("fin_in")
        const_set = sem("const_set")
        ws_masked = sem("ws_masked")
        x_sq = sem("x_sq")
        sq_ready = sem("sq_ready")
        sq_added = sem("sq_added")
        uhi_ready = sem("uhi_ready")
        u_ready = sem("u_ready")
        var_ready = sem("var_ready")
        rstd_ready = sem("rstd_ready")
        diag_ready = sem("diag_ready")
        mem_n = sem("mem_n")
        mhi_ready = sem("mhi_ready")
        mlo_ready = sem("mlo_ready")
        part_hi = sem("part_hi")
        vgelu = sem("vgelu")
        vsq = sem("vsq")
        vn_ready = sem("vn_ready")
        ugelu = sem("ugelu")
        win_ready = sem("win_ready")
        win_step = sem("win_step")
        d_ready = sem("d_ready")
        silu_ready = sem("silu_ready")
        prod_ready = sem("prod_ready")
        ahi_ready = sem("ahi_ready")
        act_ready = sem("act_ready")
        rot_raw = sem("rot_raw")
        rot_ready = sem("rot_ready")
        dve_step = sem("dve_step")
        max_ready = sem("max_ready")
        exp_ready = sem("exp_ready")
        p_ready = sem("p_ready")
        pt_ready = sem("pt_ready")
        in_ready = sem("in_ready")
        rvar_ready = sem("rvar_ready")
        rrstd_ready = sem("rrstd_ready")
        y_full = sem("y_full")
        y_ready = sem("y_ready")
        out_in = sem("out_in")

        def lin(c, i, k):
            return c if i is None else i * k + c

        def acc_tile(layer, t):
            return ACC0[layer] + t

        def aux_free(eng, t):
            if t >= 4:
                w = who[t - 4]
                eng.wait_ge(aux_free_v if w == "v" else aux_free_a, who[:t - 3].count(w))

        def slot_free(eng, n, i=None):
            ends, count = used[n]
            eng.wait_ge(acc_done if ends else unit_used, lin(count, i, RING))

        def mix_acc(layer):
            return ACC0[layer]

        def x_acc(layer):
            return ACC0[layer] + A_MIX[layer]

        def f_acc(layer):
            return x_acc(layer) + A_X

        def x_unit(layer):
            return UNIT0[layer] + MIX_UNITS[layer]

        def f_unit(layer):
            return x_unit(layer) + X_END

        AV, AA, AU, ASGU, APOOL, AOUT0 = 0, 4, 8, 12, 16, 20
        BV, BQK, BD, BRV, BRQK, BRG, BR, BOUT1 = 0, 4, 12, 16, 20, 28, 32, 36
        AK, AXV, AQ, AXO, AO = 0, 8, 12, 20, 28
        AOUT = (AOUT0, BOUT1)

        PHX, PHM1 = (8, 24), 16
        XMAX, DMAX = (0, 2 * X_H + TT * DIL_H), 2 * X_H
        SILU = (0, FT + RET_H)
        ROUND = {0: 0, 1: 3, 2: 4, 3: 5, 4: 6, 5: 7, 6: 8}

        def freed_v(t):
            return who[:t + 1].count("v")

        def freed_a(t):
            return who[:t + 1].count("a")

        def decay(h):
            return decay012[:, h, :] if h < 3 else decay3[:, :]

        used, mid = [], [0]

        def rows_used(t, tiles, per=1):
            for j in range(tiles):
                for e in range(per):
                    mid[0] += e < per - 1
                    used.append((e == per - 1, t + j + 1 if e == per - 1 else mid[0]))

        def cols_used(t, tiles):
            for q in range(4):
                mid[0] += q < 3
                used.append((q == 3, t + tiles if q == 3 else mid[0]))

        for layer in range(LAYERS):
            a = mix_acc(layer)
            if layer == 0:
                cols_used(a + AV, TT)
                rows_used(a + AA, 8)
            else:
                cols_used(a + BV, TT)
                rows_used(a + BQK, 8)
                cols_used(a + BRV, TT)
                rows_used(a + BRQK, 12)
            rows_used(a + AOUT[layer], KT)
            a = x_acc(layer)
            rows_used(a + AK, KT)
            cols_used(a + AXV, MT)
            cols_used(a + AXV + MT, MT)
            rows_used(a + AQ, KT)
            rows_used(a + AO, KT)
            rows_used(f_acc(layer), 2 * FT)
            rows_used(f_acc(layer) + 2 * FT, KT, 3)
        assert len(used) == UNITS

        block = ctx.enter_context(nc.Block())

        @block.sync
        def _(sp):
            for j in range(RING):
                sp.dma_start(raw[:, j, :], d["weights"][j]).then_inc(raw_in[j], 16)
            with sp.Fori(1, UNITS // RING) as i:
                for j in range(RING):
                    sp.wait_ge(lo_ready, i * RING + (j - RING + 1))
                    sp.dma_start(raw[:, j, :], d["weights"][bass.ds(i * RING + j, 1)].rearrange("a p n -> p (a n)"))\
                        .then_inc(raw_in[j], 16)
            for t in range(TT):
                sp.wait_ge(aux_free_v, freed_v(aux_at["out"] + 2 * t + 1))
                sp.dma_start(d["out"][0, t * P:(t + 1) * P, :], x_tok[:, t, :]).then_inc(out_in, 16)
            sp.wait_ge(out_in, 16 * TT)

        @block.scalar
        def _(act):
            def split(n, i=None):
                if n >= UNITS:
                    return
                s = n % RING
                act.wait_ge(raw_in[s], lin(16 * (n // RING + 1), i, 16))
                if n >= RING:
                    slot_free(act, n - RING, i)
                act.activation(w_hi[:, s, :], raw[:, s, :], ACT.Copy).then_inc(hi_ready, 1)

            def residual(norm, j, gcol, t):
                act.wait_ge(acc_drained, t + 1)
                dst = sqsum[:, :] if j == 0 else tmp[:, j % 2, :]
                if j >= 3:
                    act.wait_ge(sq_added, 6 * (norm - 1) + j - 2)
                act.activation(dst, hT[:, j, :], ACT.Square).then_inc(sq_ready, 1)
                if gcol is not None:
                    act.activation(u_hi[:, j, :], hT[:, j, :], ACT.Copy, scale=vecs[:, gcol + j:gcol + j + 1])\
                        .then_inc(uhi_ready, 1)

            def mem_hi_part(layer, j):
                act.wait_ge(aux_free_v, freed_v(aux_at["mem"] + 3))
                act.activation(mem_hi[:, j, :], memT[:, j, :], ACT.Copy,
                               scale=vecs[:, C_MN + 8 * layer + j:C_MN + 8 * layer + j + 1]).then_inc(mhi_ready, 1)

            def y_hi_part(j, src, scale=1.0):
                act.activation(y_hi[:, j, :], src, ACT.Copy, scale=scale).then_inc(part_hi, 1)

            for t in range(TT):
                act.dma_start(x_tok[:, t, :], d["x"][0, t * P:(t + 1) * P, :]).then_inc(x_in, 16)
            act.dma_start(ident[:, :], d["ident"]).then_inc(x_in, 16)
            act.dma_start(vecs[:, :], d["vecs"]).then_inc(x_in, 16)
            act.dma_start(mem_tok[:, :, :], d["mem"].rearrange("a (t p) n -> p (a t) n", p=P)).then_inc(mem_in, 16)
            act.dma_start(sgu_g[:, :], d["sgu_g"]).then_inc(c0_in, 16)
            act.dma_start(sgu_b[:, :, :], d["sgu_b"].rearrange("p (g t) -> p g t", g=4)).then_inc(c0_in, 16)
            act.dma_start(ws_t[:, :, :], d["ws_t"]).then_inc(c0_in, 16)
            act.dma_start(pool_w[:, :, :], d["pool_w"]).then_inc(c0_in, 16)
            act.dma_start(invcnt[:, :, :], d["invcnt"].rearrange("p (g t) -> p g t", g=4)).then_inc(c0_in, 16)
            act.wait_ge(x_in, 16 * 6)
            for t in range(TT):
                if t:
                    act.wait_ge(x_sq, t)
                act.activation(junk[:, :], x_tok[:, t, :], ACT.Square, accum_out=ssq[:, t:t + 1]).then_inc(x_sq, 1)
            for n in range(LEAD):
                split(n)
            for j in range(KT):
                act.wait_ge(aux_free_v, freed_v(aux_at["x"] + j))
                act.activation(u_hi[:, j, :], hT[:, j, :], ACT.Copy, scale=vecs[:, C_EVEN + j:C_EVEN + j + 1])\
                    .then_inc(uhi_ready, 1)
            act.wait_ge(mem_in, 16)
            for t in range(MT):
                act.wait_ge(x_sq, TT + t)
                act.activation(junk[:, :], mem_tok[:, t, :], ACT.Square, accum_out=ssq_m[:, t:t + 1])\
                    .then_inc(x_sq, 1)

            a0 = mix_acc(0)
            for n in range(4):
                split(n + LEAD)
            for t in range(TT):
                act.wait_ge(acc_drained, a0 + AV + t + 1)
                act.activation(vn[:, t, :], vn[:, t, :], ACT.Gelu_apprx_tanh).then_inc(vgelu, 1)
                act.wait_ge(vgelu, t + 1)
                if t == 0:
                    act.wait_ge(x_sq, TT + MT)
                else:
                    act.wait_ge(vsq, t)
                act.activation(junk[:, 0:S], vn[:, t, :], ACT.Square, accum_out=ssq_v[:, t:t + 1]).then_inc(vsq, 1)
                split(t + 4 + LEAD)
            for g in range(4):
                split(g + 8 + LEAD)
                act.wait_ge(acc_drained, a0 + AU + g + 1)
                act.activation(uu[:, g, :], uu[:, g, :], ACT.Gelu_apprx_tanh).then_inc(ugelu, 1)
            for g in range(4):
                act.wait_ge(y_full, g + 1)
                y_hi_part(4 + g, tmp[:, g % 2, :])
            for g in range(4):
                act.wait_ge(acc_done, a0 + APOOL + g + 1)
                y_hi_part(g, accs[(a0 + APOOL + g) % 4][:, :], scale=vecs[:, C_PS + g:C_PS + g + 1])

            def out_phase(layer, norm, u0, a0, gcol, with_mem=False):
                for j in range(KT):
                    split(u0 + j + LEAD)
                    residual(norm, j, gcol, a0 + j)
                    if with_mem:
                        mem_hi_part(layer, j)

            def cross_attention(layer):
                a0, u0 = x_acc(layer), x_unit(layer)
                for n in range(X_O):
                    split(u0 + n + LEAD)

                def exps(h):
                    for q in range(TT):
                        act.wait_ge(max_ready, XMAX[layer] + 2 * h + q // 2 + 1)
                        t = aux_at["xs", layer, h] + q // 2
                        ins = act.activation(xp[:, h % 2, q, :], auxs[t % 4][:, (q % 2) * M:(q % 2 + 1) * M], ACT.Exp,
                                             bias=nmax[:, h % 2, q:q + 1], accum_out=psums[:, h % 2, q:q + 1])
                        if q % 2:
                            ins.then_inc(aux_free_a, 1)

                def turned(h):
                    for k in range(MT):
                        t = aux_at["xt", layer, h] + k
                        act.wait_ge(aux_done, t + 1)
                        act.activation(xpt[:, k, :], auxs[t % 4][:, :], ACT.Copy).then_inc(aux_free_a, 1)

                def parts(h):
                    for e in range(2):
                        t = a0 + AXO + 2 * h + e
                        act.wait_ge(acc_done, t + 1)
                        y_hi_part(2 * h + e, accs[t % 4][:, :])

                exps(0)
                for h in range(X_H):
                    if h + 1 < X_H:
                        exps(h + 1)
                    turned(h)
                    parts(h)
                out_phase(layer, 3 * layer + 2, u0 + X_O, a0 + AO, C_FN + 8 * layer)

            def ffn(layer):
                u0, a0 = f_unit(layer), f_acc(layer)
                pr0 = layer * FT
                if layer == LAYERS - 1:
                    act.dma_start(fin_g, d["final_g"]).then_inc(fin_in, 16)

                def group(g, i=None):
                    for e in range(2):
                        pair = 2 * g + e
                        n = u0 + 4 * g + 2 * e
                        if g or e:
                            act.wait_ge(prod_ready, lin(pr0 + pair, i, 2))
                        split(n + LEAD, i)
                        if g or e:
                            idx = pair - 1 if i is None else i * 2 + (pair - 1)
                            act.activation(act_hi[:, idx, :], tmp[:, 2 + (pair - 1) % 2, :], ACT.Copy).then_inc(ahi_ready, 1)
                        if not g and not e:
                            split(n + 1 + LEAD)
                        act.wait_ge(acc_drained, lin(a0 + 2 * pair + 1, i, 4))
                        act.activation(tmp[:, e, :], tmp[:, e, :], ACT.Silu).then_inc(silu_ready, 1)
                        if g or e:
                            split(n + 1 + LEAD, i)

                group(0)
                group(1)
                with act.Fori(0, FT // 2 - 2) as i:
                    group(2, i)
                act.wait_ge(prod_ready, pr0 + FT)
                act.activation(act_hi[:, FT - 1, :], tmp[:, 3, :], ACT.Copy).then_inc(ahi_ready, 1)
                norm = 3 * layer + 3
                for j in range(KT):
                    for e in range(3):
                        split(u0 + F_DN + 3 * j + e + LEAD)
                    residual(norm, j, C_ODD if layer == 0 else None, a0 + 2 * FT + j)

            def odd_mixer():
                a0, u0 = mix_acc(1), UNIT0[1]
                act.wait_ge(acc_done, a0)
                act.dma_start(cs_d[:, :, :], d["cs_d"]).then_inc(c1_in, 16)
                act.dma_start(perm[:, :, :], d["perm"]).then_inc(c1_in, 16)
                act.dma_start(band[:, :], d["band"]).then_inc(c1_in, 16)
                act.dma_start(cs_r[:, :, :], d["cs_r"]).then_inc(c2_in, 16)
                act.dma_start(decay012[:, :, :], d["decay"][:, 0:3, :]).then_inc(c2_in, 16)
                for n in range(12):
                    split(u0 + n + LEAD)

                def exps(h):
                    for i in range(TT):
                        act.wait_ge(max_ready, DMAX + 4 * h + i + 1)
                        o, w = ROWS[i]
                        act.activation(dp[:, h % 2, o:o + w], dp[:, h % 2, o:o + w], ACT.Exp,
                                       bias=nmax[:, h % 2, i:i + 1], accum_out=psums[:, h % 2, i:i + 1])\
                            .then_inc(exp_ready, 1)

                def turned(h):
                    for e, (o, w) in enumerate(((0, 512), (512, 512), (1024, 256))):
                        t = aux_at["dt", h] + e
                        act.wait_ge(aux_done, t + 1)
                        act.activation(dpt[:, o:o + w], auxs[t % 4][:, 0:w], ACT.Copy).then_inc(aux_free_a, 1)

                def parts(h):
                    t = a0 + BD + h // 2
                    act.wait_ge(acc_done, t + 1)
                    y_hi_part(h // 2, accs[t % 4][:, :])

                exps(0)
                for h in range(DIL_H):
                    if h + 1 < DIL_H:
                        exps(h + 1)
                    turned(h)
                    if h % 2:
                        parts(h)
                act.dma_start(decay3[:, :], d["decay"][:, 3, :]).then_inc(c3_in, 16)
                for n in range(12, 24):
                    split(u0 + n + LEAD)
                for h in range(RET_H):
                    split(u0 + U_RG + h + LEAD)
                    act.wait_ge(acc_drained, a0 + BRG + h + 1)
                    act.activation(gate[:, h, :], gate[:, h, :], ACT.Silu).then_inc(silu_ready, 1)
                for h in range(RET_H):
                    act.wait_ge(aux_free_v, freed_v(aux_at["rt", h]))
                    y_hi_part(4 + h, tmp[:, 2 + h % 2, :])

            out_phase(0, 1, U_OUT0, mix_acc(0) + AOUT0, C_XN, with_mem=True)
            cross_attention(0)
            ffn(0)
            odd_mixer()
            out_phase(1, 4, UNIT0[1] + U_OUT1, mix_acc(1) + BOUT1, C_XN + 8, with_mem=True)
            cross_attention(1)
            ffn(1)

        @block.gpsimd
        def _(pool):
            pool.memset(ones[:, :], 1.0).then_inc(const_set, 1)
            pool.memset(mean_w[:, :], 1.0 / D).then_inc(const_set, 1)
            pool.memset(mexp[:, :], -0.5).then_inc(const_set, 1)
            pool.memset(a_pad[:, :, 0:PAD], 0.0).then_inc(const_set, 1)
            pool.wait_ge(c0_in, 16 * 5)
            pool.affine_select(out=ws_t[:, :, :], in_=ws_t[:, :, :], compare_op=ALU.is_ge, fill=0.0, base=0,
                               pattern=[[0, 4], [1, P]], channel_multiplier=-1).then_inc(ws_masked, 1)
            pool.wait_ge(const_set, 4)

            def power(dst, src, n):
                pool.tensor_tensor(dst, src, mexp[:, 0:n], ALU.pow).then_inc(rstd_ready, 1)

            def norm_power(norm):
                pool.wait_ge(aux_free_v, freed_v(aux_at["mean", norm]))
                power(rstd_tok[:, :], var_e[:, :], TT)

            def add_squares(norm):
                for j in range(1, KT - 1):
                    n = 6 * (norm - 1) + j
                    pool.wait_ge(sq_ready, 8 * (norm - 1) + j + 1)
                    if j > 1:
                        pool.wait_ge(sq_added, n - 1)
                    pool.tensor_tensor(sqsum[:, :], sqsum[:, :], tmp[:, j % 2, :], ALU.add).then_inc(sq_added, 1)

            pool.wait_ge(var_ready, 1)
            power(rstd_tok[:, :], var_e[:, :], TT)
            pool.wait_ge(var_ready, 2)
            power(rstd_m[:, :], var_m[:, :], MT)
            steps = 0
            for g, win in enumerate(WINDOWS):
                pool.wait_ge(acc_drained, mix_acc(0) + AA + g + 1)
                if g == 0:
                    pool.wait_ge(var_ready, 3)
                    power(rstd_v[:, :], var_v[:, :], TT)
                if g:
                    pool.wait_ge(win_ready, g)
                src, width = a_pad[:, g, :], 1
                buf = 0
                while width < win:
                    last = 2 * width == win
                    if last and g >= 1:
                        pool.wait_ge(d_ready, g)
                    dst = wsum[:, 2 if last else buf, :]
                    lo = 2 * width - 1
                    ins = pool.tensor_tensor(dst[:, lo:PAD + S], src[:, lo:PAD + S],
                                             src[:, lo - width:PAD + S - width], ALU.add)
                    if last:
                        ins.then_inc(win_ready, 1)
                    else:
                        ins.then_inc(win_step, 1)
                        steps += 1
                        pool.wait_ge(win_step, steps)
                    src, buf, width = dst, 1 - buf, 2 * width
            for layer in range(LAYERS):
                if layer:
                    add_squares(3)
                    norm_power(3)
                    for h in range(RET_H):
                        pool.wait_ge(rvar_ready, h + 1)
                        pool.tensor_tensor(rrstd[:, h % 2, :], rvar[:, h % 2, :], mexp[:, :], ALU.pow)\
                            .then_inc(rrstd_ready, 1)
                for norm in (3 * layer + 1, 3 * layer + 2):
                    add_squares(norm)
                    norm_power(norm)
            add_squares(6)
            norm_power(6)

        @block.vector
        def _(dve):
            chain = [0]

            def step(ins):
                chain[0] += 1
                ins.then_inc(dve_step, 1)
                return chain[0]

            def split(n, i=None):
                if n >= UNITS:
                    return
                s = n % RING
                dve.wait_ge(hi_ready, lin(n + 1, i, RING))
                dve.tensor_tensor(w_lo[:, s, :], raw[:, s, :], w_hi[:, s, :].bitcast(F32), ALU.subtract)\
                    .then_inc(lo_ready, 1)

            def acc(t):
                return accs[t % 4]

            def u_lo_part(norm, j, gcol):
                dve.wait_ge(uhi_ready, 8 * norm + j + 1)
                dve.scalar_tensor_tensor(out=u_lo[:, j, :], in0=hT[:, j, :], scalar=vecs[:, gcol + j:gcol + j + 1],
                                         in1=u_hi[:, j, :].bitcast(F32), op0=ALU.mult, op1=ALU.subtract)\
                    .then_inc(u_ready, 1)

            def y_lo_part(j, src, count, ready, scale=None):
                dve.wait_ge(part_hi, count)
                if scale is None:
                    ins = dve.tensor_tensor(y_lo[:, j, :], src, y_hi[:, j, :].bitcast(F32), ALU.subtract)
                else:
                    ins = dve.scalar_tensor_tensor(out=y_lo[:, j, :], in0=src, scalar=scale,
                                                   in1=y_hi[:, j, :].bitcast(F32), op0=ALU.mult, op1=ALU.subtract)
                ins.then_inc(ready, 1)

            def mean_to_var(norm):
                t = aux_at["mean", norm]
                dve.wait_ge(aux_done, t + 1)
                dve.tensor_scalar(var_e[:, :], auxs[t % 4][:, 0:TT], EPS, None, ALU.add).then_inc(aux_free_v, 1)

            def make_diag(norm):
                dve.wait_ge(rstd_ready, ROUND[norm] + 1)
                for t in range(TT):
                    ins = dve.tensor_scalar(diag[:, t * P:(t + 1) * P], ident[:, :], rstd_tok[:, t:t + 1], None,
                                            ALU.mult)
                ins.then_inc(diag_ready, 1)

            def make_row(norm):
                t = aux_at["row", norm]
                dve.wait_ge(aux_done, t + 1)
                dve.tensor_copy(rstd_row[:, :], auxs[t % 4][:, :]).then_inc(aux_free_v, 1)
                dve.wait_ge(aux_free_v, freed_v(t))

            def scaled(t, dst, sems=None, f=None):
                dve.wait_ge(acc_done, t + 1)
                if f is None:
                    ins = dve.tensor_tensor(dst, acc(t)[:, :], rstd_row[:, :], ALU.mult)
                else:
                    ins = dve.scalar_tensor_tensor(out=dst, in0=acc(t)[:, :], scalar=f, in1=rstd_row[:, :],
                                                   op0=ALU.mult, op1=ALU.mult)
                ins.then_inc(acc_drained, 1)

            def scaled_tok(t, dst, i):
                dve.wait_ge(acc_done, t + 1)
                dve.tensor_scalar(dst, acc(t)[:, :], rstd_tok[:, i:i + 1], None, ALU.mult).then_inc(acc_drained, 1)

            def mem_lo_part(layer, j):
                c = C_MN + 8 * layer + j
                dve.wait_ge(mhi_ready, 8 * layer + j + 1)
                dve.scalar_tensor_tensor(out=mem_lo[:, j, :], in0=memT[:, j, :], scalar=vecs[:, c:c + 1],
                                         in1=mem_hi[:, j, :].bitcast(F32), op0=ALU.mult, op1=ALU.subtract)\
                    .then_inc(mlo_ready, 1)

            def residual_phase(layer, norm, a0, u0, per, gcol, with_mem=False):
                for j in range(KT):
                    for e in range(per):
                        split(u0 + per * j + e + LEAD)
                    dve.wait_ge(acc_done, a0 + j + 1)
                    dve.tensor_tensor(hT[:, j, :], hT[:, j, :], acc(a0 + j)[:, :], ALU.add).then_inc(acc_drained, 1)
                    if gcol is not None and j:
                        u_lo_part(norm, j - 1, gcol)
                    if with_mem:
                        mem_lo_part(layer, j)
                if gcol is not None:
                    u_lo_part(norm, KT - 1, gcol)

            for n in range(LEAD):
                split(n)
            dve.wait_ge(x_sq, TT)
            dve.tensor_scalar(var_e[:, 0:TT], ssq[:, 0:TT], 1.0 / D, EPS, ALU.mult, ALU.add).then_inc(var_ready, 1)
            for j in range(KT):
                t = aux_at["x"] + j
                dve.wait_ge(aux_done, t + 1)
                dve.tensor_copy(hT[:, j, :], auxs[t % 4][:, :]).then_inc(aux_free_v, 1)
                if j:
                    u_lo_part(0, j - 1, C_EVEN)
            u_lo_part(0, KT - 1, C_EVEN)
            make_diag(0)
            make_row(0)
            dve.wait_ge(x_sq, TT + MT)
            dve.tensor_scalar(var_m[:, :], ssq_m[:, :], 1.0 / D, EPS, ALU.mult, ALU.add).then_inc(var_ready, 1)
            dve.wait_ge(rstd_ready, 2)
            for t in range(MT):
                dve.tensor_scalar(mem_tok[:, t, :], mem_tok[:, t, :], rstd_m[:, t:t + 1], None, ALU.mult)\
                    .then_inc(mem_n, 1)

            a0 = mix_acc(0)
            for n in range(4):
                split(n + LEAD)
            for t in range(TT):
                scaled_tok(a0 + AV + t, vn[:, t, :], t)
            for t in range(4):
                k = aux_at["mem"] + t
                dve.wait_ge(aux_done, k + 1)
                dve.tensor_copy(memT[:, 2 * t:2 * t + 2, :], auxs[k % 4][:, :].rearrange("p (a b) -> p a b", a=2))\
                    .then_inc(aux_free_v, 1)

            def pooled(g):
                win = WINDOWS[g]
                dve.wait_ge(win_ready, g + 1)
                n1 = step(dve.tensor_tensor(tmp[:, 2, 0:PAD], wsum[:, 2, PAD:2 * PAD], invcnt[:, g, :], ALU.mult))
                dve.scalar_tensor_tensor(out=dd[:, g, PAD:S], in0=wsum[:, 2, 2 * PAD:PAD + S], scalar=1.0 / win,
                                         in1=a_pad[:, g, 2 * PAD:PAD + S], op0=ALU.mult, op1=ALU.subtract)
                dve.wait_ge(dve_step, n1)
                dve.tensor_tensor(dd[:, g, 0:PAD], tmp[:, 2, 0:PAD], a_pad[:, g, PAD:2 * PAD], ALU.subtract)\
                    .then_inc(d_ready, 1)

            dve.wait_ge(const_set, 4)
            dve.wait_ge(c0_in, 16 * 5)
            for g in range(4):
                split(4 + g + LEAD)
                scaled(a0 + AA + g, a_pad[:, g, PAD:PAD + S])
                if g == 0:
                    dve.wait_ge(vsq, TT)
                    dve.tensor_scalar(var_v[:, :], ssq_v[:, :], 1.0 / S, EPS, ALU.mult, ALU.add)\
                        .then_inc(var_ready, 1)
                if g == 1:
                    dve.wait_ge(rstd_ready, 3)
                    for t in range(TT):
                        dve.scalar_tensor_tensor(out=vn[:, t, :], in0=vn[:, t, :], scalar=rstd_v[:, t:t + 1],
                                                 in1=sgu_g[:, :], op0=ALU.mult, op1=ALU.mult).then_inc(vn_ready, 1)
            for g in range(4):
                split(8 + g + LEAD)
                scaled(a0 + AU + g, uu[:, g, :])
                pooled(g)
            for g in range(4):
                t = a0 + ASGU + g
                dve.wait_ge(acc_done, t + 1)
                if g >= 2:
                    dve.wait_ge(part_hi, g - 1)
                dve.tensor_tensor(tmp[:, g % 2, :].rearrange("p (n t) -> p n t", n=TT),
                                  acc(t)[:, :].rearrange("p (n t) -> p n t", n=TT),
                                  sgu_b[:, g:g + 1, :].broadcast_to([P, TT, P]), ALU.add).then_inc(acc_drained, 1)
                dve.wait_ge(acc_drained, t + 1)
                dve.wait_ge(ugelu, g + 1)
                dve.tensor_tensor(tmp[:, g % 2, :], tmp[:, g % 2, :], uu[:, g, :], ALU.mult).then_inc(y_full, 1)
                dve.wait_ge(y_full, g + 1)
                y_lo_part(4 + g, tmp[:, g % 2, :], g + 1, y_ready)
            for g in range(4):
                t = a0 + APOOL + g
                y_lo_part(g, acc(t)[:, :], 4 + g + 1, acc_drained, scale=vecs[:, C_PS + g:C_PS + g + 1])
            residual_phase(0, 1, a0 + AOUT0, U_OUT0, 1, C_XN, with_mem=True)

            def cross_attention(layer):
                norm = 3 * layer + 1
                a0, u0 = x_acc(layer), x_unit(layer)
                for j in range(KT):
                    split(u0 + j + LEAD)
                    if j == 0:
                        mean_to_var(norm)
                        make_diag(norm)
                    if j == 1:
                        make_row(norm)
                    t = a0 + AK + j
                    dve.wait_ge(acc_done, t + 1)
                    dve.tensor_copy(xk[:, j, :], acc(t)[:, 0:M]).then_inc(acc_drained, 1)
                for c in range(2):
                    for n in range(4):
                        split(u0 + X_V + 4 * c + n + LEAD)
                    for m in range(MT):
                        t = a0 + AXV + 2 * c + m
                        dve.wait_ge(acc_done, t + 1)
                        dve.tensor_copy(xv[:, m, c * S:(c + 1) * S], acc(t)[:, :]).then_inc(acc_drained, 1)
                for j in range(KT):
                    split(u0 + X_Q + j + LEAD)
                    scaled(a0 + AQ + j, xq[:, j, :], f=float(256) ** -0.5)

                def maxima(h):
                    for q in range(2):
                        t = aux_at["xs", layer, h] + q
                        dve.wait_ge(aux_done, t + 1)
                        dve.tensor_reduce(nmax[:, h % 2, 2 * q:2 * q + 2],
                                          auxs[t % 4][:, :].rearrange("p (a b) -> p a b", a=2), AX.X, ALU.max,
                                          negate=True).then_inc(max_ready, 1)

                def normalise(h):
                    dve.wait_ge(aux_free_a, freed_a(aux_at["xs", layer, h] + 1))
                    n = step(dve.reciprocal(pinv[:, h % 2, :], psums[:, h % 2, :]))
                    dve.wait_ge(dve_step, n)
                    for q in range(TT):
                        ins = dve.tensor_scalar(xp[:, h % 2, q, :], xp[:, h % 2, q, :], pinv[:, h % 2, q:q + 1],
                                                None, ALU.mult)
                    ins.then_inc(p_ready, 1)

                def parts(h):
                    for e in range(2):
                        t = a0 + AXO + 2 * h + e
                        y_lo_part(2 * h + e, acc(t)[:, :], PHX[layer] + 2 * h + e + 1, acc_drained)

                maxima(0)
                normalise(0)
                for h in range(X_H):
                    if h + 1 < X_H:
                        maxima(h + 1)
                        normalise(h + 1)
                    parts(h)
                residual_phase(layer, 3 * layer + 2, a0 + AO, u0 + X_O, 1, C_FN + 8 * layer)

            def ffn(layer):
                norm = 3 * layer + 2
                u0, a0 = f_unit(layer), f_acc(layer)
                pr0 = layer * FT

                def lo_of(pair, i=None):
                    dve.wait_ge(ahi_ready, lin(pr0 + pair + 1, i, 2))
                    idx = pair if i is None else i * 2 + pair
                    dve.tensor_tensor(act_lo[:, idx, :], tmp[:, 2 + pair % 2, :], act_hi[:, idx, :].bitcast(F32),
                                      ALU.subtract).then_inc(act_ready, 1)

                def group(g, i=None):
                    for e in range(2):
                        pair = 2 * g + e
                        n = u0 + 4 * g + 2 * e
                        tg = a0 + 4 * g + 2 * e
                        split(n + LEAD, i)
                        if pair == 0:
                            mean_to_var(norm)
                            make_diag(norm)
                            split(n + 1 + LEAD)
                            make_row(norm)
                        dve.wait_ge(acc_done, lin(tg + 1, i, 4))
                        dve.tensor_tensor(tmp[:, e, :], acc(tg)[:, :], rstd_row[:, :], ALU.mult)\
                            .then_inc(acc_drained, 1)
                        if pair >= 1:
                            lo_of(pair - 1, i)
                        if pair:
                            split(n + 1 + LEAD, i)
                        dve.wait_ge(acc_done, lin(tg + 2, i, 4))
                        dve.tensor_tensor(tmp[:, 2 + e, :], acc(tg + 1)[:, :], rstd_row[:, :], ALU.mult)\
                            .then_inc(acc_drained, 1)
                        dve.wait_ge(silu_ready, lin(SILU[layer] + pair + 1, i, 2))
                        dve.wait_ge(acc_drained, lin(tg + 2, i, 4))
                        dve.tensor_tensor(tmp[:, 2 + e, :], tmp[:, 2 + e, :], tmp[:, e, :], ALU.mult)\
                            .then_inc(prod_ready, 1)

                group(0)
                group(1)
                with dve.Fori(0, FT // 2 - 2) as i:
                    group(2, i)
                lo_of(FT - 1)
                residual_phase(layer, 3 * layer + 3, a0 + 2 * FT, u0 + F_DN, 3, C_ODD if layer == 0 else None)

            def odd_mixer():
                a0, u0 = mix_acc(1), UNIT0[1]

                def rotated(j, rots, cs, b):
                    t = aux_at[rots] + j
                    dve.wait_ge(acc_drained, a0 + b + j + 1)
                    n = step(dve.tensor_tensor(tq[:, j, :], tmp[:, j % 2, :], cs[:, 0, :], ALU.mult))
                    dve.wait_ge(aux_done, t + 1)
                    done = j + (8 if b == BRQK else 0)
                    if done:
                        dve.wait_ge(rot_ready, done)
                    dve.tensor_tensor(tmp[:, 2, :], auxs[t % 4][:, :], cs[:, 1, :], ALU.mult).then_inc(aux_free_v, 1)
                    dve.wait_ge(aux_free_v, freed_v(t))
                    dve.wait_ge(dve_step, n)
                    dve.tensor_tensor(tq[:, j, :], tq[:, j, :], tmp[:, 2, :], ALU.add).then_inc(rot_ready, 1)

                for n in range(4):
                    split(u0 + n + LEAD)
                    if n == 0:
                        mean_to_var(3)
                        make_diag(3)
                    if n == 1:
                        make_row(3)
                for t in range(TT):
                    scaled_tok(a0 + BV + t, tv[:, t, :], t)
                dve.wait_ge(c1_in, 16 * 3)
                for j in range(8):
                    split(u0 + U_DQK + j + LEAD)
                    scaled(a0 + BQK + j, tmp[:, j % 2, :])
                    if j:
                        rotated(j - 1, "rotd", cs_d, BQK)
                rotated(7, "rotd", cs_d, BQK)

                def masked(h):
                    for i in range(TT):
                        t = aux_at["ds", h] + i
                        o, w = ROWS[i]
                        dve.wait_ge(aux_done, t + 1)
                        dve.scalar_tensor_tensor(out=dp[:, h % 2, o:o + w], in0=auxs[t % 4][:, 0:w],
                                                 scalar=float(DH) ** -0.5, in1=band[:, S - w:S], op0=ALU.mult,
                                                 op1=ALU.add).then_inc(aux_free_v, 1)
                    for i in range(TT):
                        t = aux_at["ds", h] + i
                        o, w = ROWS[i]
                        dve.wait_ge(aux_free_v, freed_v(t))
                        dve.tensor_reduce(nmax[:, h % 2, i:i + 1], dp[:, h % 2, o:o + w], AX.X, ALU.max,
                                          negate=True).then_inc(max_ready, 1)

                def normalise(h):
                    dve.wait_ge(exp_ready, 4 * h + 4)
                    n = step(dve.reciprocal(pinv[:, h % 2, :], psums[:, h % 2, :]))
                    dve.wait_ge(dve_step, n)
                    for i in range(TT):
                        o, w = ROWS[i]
                        ins = dve.tensor_scalar(dp[:, h % 2, o:o + w], dp[:, h % 2, o:o + w],
                                                pinv[:, h % 2, i:i + 1], None, ALU.mult)
                    ins.then_inc(p_ready, 1)

                dve.wait_ge(rot_ready, 8)
                masked(0)
                for h in range(DIL_H):
                    if h + 1 < DIL_H:
                        masked(h + 1)
                    normalise(h)
                    if h % 2 == 0 and h:
                        t = a0 + BD + h // 2 - 1
                        y_lo_part(h // 2 - 1, acc(t)[:, :], PHM1 + h // 2, acc_drained)
                y_lo_part(3, acc(a0 + BD + 3)[:, :], PHM1 + 4, acc_drained)

                for n in range(4):
                    split(u0 + U_RV + n + LEAD)
                for t in range(TT):
                    scaled_tok(a0 + BRV + t, tv[:, t, :], t)
                dve.wait_ge(c2_in, 16 * 2)
                dve.wait_ge(c3_in, 16)
                for j in range(8):
                    split(u0 + U_RQK + j + LEAD)
                    scaled(a0 + BRQK + j, tmp[:, j % 2, :])
                    if j:
                        rotated(j - 1, "rotr", cs_r, BRQK)
                rotated(7, "rotr", cs_r, BRQK)
                for j in range(4):
                    split(u0 + U_RG + j + LEAD)
                    scaled(a0 + BRG + j, gate[:, j, :])

                def decayed(h):
                    for e, kts in enumerate(((0,), (1, 3), (2,))):
                        t = aux_at["rs", h] + e
                        dve.wait_ge(aux_done, t + 1)
                        for kt in kts:
                            o, w = BLOCK[kt]
                            c = 384 if kt == 3 else 0
                            ins = dve.tensor_tensor(inner[:, h % 2, o:o + w], auxs[t % 4][:, c:c + w],
                                                    decay(h)[:, 0:w], ALU.mult)
                        ins.then_inc(aux_free_v, 1)

                def head_norm(h):
                    t = a0 + BR + h
                    dve.wait_ge(acc_done, t + 1)
                    for i in range(TT):
                        n = step(dve.bn_stats(stats[:, i, :], acc(t)[:, i * P:(i + 1) * P]))
                    dve.wait_ge(dve_step, n)
                    for i in range(TT):
                        n = step(dve.bn_aggr(mv[:, i, :], stats[:, i, :]))
                    dve.wait_ge(dve_step, n)
                    dve.tensor_scalar(rvar[:, h % 2, :], mv[:, :, 1], EPS, None, ALU.add).then_inc(rvar_ready, 1)
                    dve.wait_ge(rrstd_ready, h + 1)
                    for i in range(TT):
                        ins = dve.tensor_scalar(tmp[:, h % 2, i * P:(i + 1) * P], acc(t)[:, i * P:(i + 1) * P],
                                                mv[:, i, 0:1], rrstd[:, h % 2, i:i + 1], ALU.subtract, ALU.mult)
                    ins.then_inc(acc_drained, 1)

                def gated(h):
                    t = aux_at["rt", h]
                    dve.wait_ge(aux_done, t + 1)
                    dve.wait_ge(silu_ready, FT + h + 1)
                    dve.tensor_tensor(tmp[:, 2 + h % 2, :], auxs[t % 4][:, :], gate[:, h, :], ALU.mult)\
                        .then_inc(aux_free_v, 1)

                decayed(0)
                for h in range(RET_H):
                    if h + 1 < RET_H:
                        decayed(h + 1)
                    head_norm(h)
                    if h:
                        gated(h - 1)
                        y_lo_part(4 + h - 1, tmp[:, 2 + (h - 1) % 2, :], PHM1 + 4 + h, y_ready)
                gated(3)
                y_lo_part(7, tmp[:, 3, :], PHM1 + 8, y_ready)
                residual_phase(1, 4, a0 + BOUT1, u0 + U_OUT1, 1, C_XN + 8, with_mem=True)

            cross_attention(0)
            ffn(0)
            odd_mixer()
            cross_attention(1)
            ffn(1)

            mean_to_var(6)
            dve.wait_ge(rstd_ready, ROUND[6] + 1)
            dve.wait_ge(fin_in, 16)
            for t in range(TT):
                for c in range(2):
                    k = aux_at["out"] + 2 * t + c
                    dve.wait_ge(aux_done, k + 1)
                    dve.scalar_tensor_tensor(out=x_tok[:, t, c * S:(c + 1) * S], in0=auxs[k % 4][:, :],
                                             scalar=rstd_tok[:, t:t + 1], in1=fin_g[:, c * S:(c + 1) * S],
                                             op0=ALU.mult, op1=ALU.mult).then_inc(aux_free_v, 1)

        @block.tensor
        def _(pe):
            def three(out, w_h, w_l, x_h, x_l, first, last):
                pe.matmul(out, w_h, x_h, start=first, stop=False)
                pe.matmul(out, w_h, x_l, start=False, stop=False)
                return pe.matmul(out, w_l, x_h, start=False, stop=last)

            def acc_free(t, i=None):
                if t >= 4:
                    pe.wait_ge(acc_drained, lin(t - 3, i, 4))

            def weights_in(n, i=None):
                pe.wait_ge(lo_ready, lin(n + 1, i, RING))

            def rows_unit(n, t, x_h, x_l, i=None, before=None, k0=0, kn=KT, last=True):
                out = accs[t % 4][:, 0:x_h.shape[2]]
                s = n % RING
                weights_in(n, i)
                if k0 == 0:
                    acc_free(t, i)
                for k in range(kn):
                    if before is not None:
                        before(k0 + k)
                    w = slice(k * P, (k + 1) * P)
                    ins = three(out, w_hi[:, s, w], w_lo[:, s, w], x_h[:, k0 + k, :], x_l[:, k0 + k, :],
                                k0 + k == 0, last and k == kn - 1)
                ins.then_inc(acc_done if last else unit_used, 1)

            def cols_units(n0, t0, x_h, x_l, tiles, before=None, after=None):
                for q in range(4):
                    n = n0 + q
                    s = n % RING
                    weights_in(n)
                    for kk in range(2):
                        k = 2 * q + kk
                        if before is not None:
                            before(k)
                        w = slice(kk * 512, (kk + 1) * 512)
                        for m in range(tiles):
                            if k == 0:
                                acc_free(t0 + m)
                            tok = slice(m * P, (m + 1) * P)
                            out = accs[(t0 + m) % 4][:, :]
                            pe.matmul(out, x_h[:, k, tok], w_hi[:, s, w], start=(k == 0), stop=False)
                            pe.matmul(out, x_h[:, k, tok], w_lo[:, s, w], start=False, stop=False)
                            ins = pe.matmul(out, x_l[:, k, tok], w_hi[:, s, w], start=False, stop=(k == KT - 1))
                            if k == KT - 1:
                                ins.then_inc(acc_done, 1)
                    if q < 3:
                        ins.then_inc(unit_used, 1)
                    if after is not None:
                        after(q)

            def mean(norm):
                t = aux_at["mean", norm]
                aux_free(pe, t)
                pe.wait_ge(sq_added, 6 * norm)
                pe.wait_ge(sq_ready, 8 * norm)
                for i in range(TT):
                    out, tok = auxs[t % 4][:, i:i + 1], slice(i * P, (i + 1) * P)
                    pe.matmul(out, sqsum[:, tok], mean_w[:, :], start=True, stop=False)
                    ins = pe.matmul(out, tmp[:, 1, tok], mean_w[:, :], start=False, stop=True)
                ins.then_inc(aux_done, 1)

            def row(norm):
                t = aux_at["row", norm]
                aux_free(pe, t)
                pe.wait_ge(diag_ready, norm + 1)
                pe.matmul(auxs[t % 4][:, :], ones[:, :], diag, start=True, stop=True).then_inc(aux_done, 1)

            def stats_after(norm):
                def f(q):
                    if q == 0:
                        mean(norm)
                    if q == 1:
                        row(norm)
                return f

            def u_in(norm):
                return lambda k: pe.wait_ge(u_ready, 8 * norm + k + 1)

            pe.wait_ge(x_in, 16 * 6)
            for j in range(KT):
                t = aux_at["x"] + j
                aux_free(pe, t)
                for i in range(TT):
                    ins = pe.transpose(auxs[t % 4][:, i * P:(i + 1) * P], x_tok[:, i, j * P:(j + 1) * P], ident[:, :])
                ins.then_inc(aux_done, 1)
            pe.wait_ge(const_set, 4)
            row(0)

            a0 = mix_acc(0)
            cols_units(U_V, a0 + AV, u_hi, u_lo, TT, before=u_in(0))
            pe.wait_ge(mem_n, MT)
            for t in range(4):
                k = aux_at["mem"] + t
                aux_free(pe, k)
                for e in range(2):
                    for m in range(MT):
                        c = e * M + m * P
                        j = 2 * t + e
                        ins = pe.transpose(auxs[k % 4][:, c:c + P], mem_tok[:, m, j * P:(j + 1) * P], ident[:, :])
                ins.then_inc(aux_done, 1)
            for g in range(8):
                rows_unit(U_A + g, a0 + AA + g, u_hi, u_lo)
            pe.wait_ge(vn_ready, TT)
            pe.wait_ge(ws_masked, 1)
            for g in range(4):
                t = a0 + ASGU + g
                acc_free(t)
                for n in range(TT):
                    ins = pe.matmul(accs[t % 4][:, n * P:(n + 1) * P], vn[:, n, g * P:(g + 1) * P], ws_t[:, g, :],
                                    start=True, stop=True)
                ins.then_inc(acc_done, 1)
            for g in range(4):
                t = a0 + APOOL + g
                acc_free(t)
                pe.wait_ge(d_ready, g + 1)
                pe.matmul(accs[t % 4][:, :], pool_w[:, g, :], dd[:, g, :], start=True, stop=True).then_inc(acc_done, 1)

            def out_proj(u0, t0, in_acc, gated0):
                def y_in(k):
                    if k < 4:
                        pe.wait_ge(acc_drained, in_acc + k + 1)
                    else:
                        pe.wait_ge(y_ready, gated0 + k - 3)
                for j in range(KT):
                    rows_unit(u0 + j, t0 + j, y_hi, y_lo, before=y_in if j == 0 else None)

            out_proj(U_OUT0, a0 + AOUT0, a0 + APOOL, 0)

            def cross_attention(layer):
                norm = 3 * layer + 1
                a0, u0 = x_acc(layer), x_unit(layer)
                for j in range(KT):
                    rows_unit(u0 + j, a0 + AK + j, mem_hi, mem_lo,
                              before=(lambda k: pe.wait_ge(mlo_ready, 8 * layer + k + 1)) if j == 0 else None)
                    stats_after(norm)(j)
                for c in range(2):
                    cols_units(u0 + X_V + 4 * c, a0 + AXV + 2 * c, mem_hi, mem_lo, MT)
                for j in range(KT):
                    rows_unit(u0 + X_Q + j, a0 + AQ + j, u_hi, u_lo, before=u_in(norm) if j == 0 else None)
                pe.wait_ge(acc_drained, a0 + AQ + KT)

                def scores(h):
                    for c in range(2):
                        t = aux_at["xs", layer, h] + c
                        aux_free(pe, t)
                        for e in range(2):
                            i = 2 * c + e
                            for k in range(2):
                                ins = pe.matmul(auxs[t % 4][:, e * M:(e + 1) * M],
                                                xq[:, 2 * h + k, i * P:(i + 1) * P], xk[:, 2 * h + k, :],
                                                start=(k == 0), stop=(k == 1))
                        ins.then_inc(aux_done, 1)

                def turn(h):
                    pe.wait_ge(p_ready, (X_H + DIL_H) * layer + h + 1)
                    for k in range(MT):
                        t = aux_at["xt", layer, h] + k
                        aux_free(pe, t)
                        for i in range(TT):
                            ins = pe.transpose(auxs[t % 4][:, i * P:(i + 1) * P], xp[:, h % 2, i, k * P:(k + 1) * P],
                                               ident[:, :])
                        ins.then_inc(aux_done, 1)

                def values(h):
                    pe.wait_ge(aux_free_a, freed_a(aux_at["xt", layer, h] + 1))
                    for e in range(2):
                        t = a0 + AXO + 2 * h + e
                        acc_free(t)
                        for k in range(MT):
                            ins = pe.matmul(accs[t % 4][:, :], xv[:, k, (2 * h + e) * P:(2 * h + e + 1) * P],
                                            xpt[:, k, :], start=(k == 0), stop=(k == MT - 1))
                        ins.then_inc(acc_done, 1)

                order_dil(scores, turn, values, X_H)
                for j in range(KT):
                    rows_unit(u0 + X_O + j, a0 + AO + j, y_hi, y_lo,
                              before=(lambda k: pe.wait_ge(acc_drained, a0 + AXO + k + 1)) if j == 0 else None)

            def ffn(layer):
                norm = 3 * layer + 2
                u0, a0 = f_unit(layer), f_acc(layer)

                def group(g, i=None):
                    for e in range(4):
                        rows_unit(u0 + 4 * g + e, a0 + 4 * g + e, u_hi, u_lo, i,
                                  before=u_in(norm) if g == 0 and e == 0 else None)
                        if g == 0:
                            stats_after(norm)(e)

                group(0)
                group(1)
                with pe.Fori(0, FT // 2 - 2) as i:
                    group(2, i)
                for j in range(KT):
                    for e, kn in enumerate((8, 8, 6)):
                        rows_unit(u0 + F_DN + 3 * j + e, a0 + 2 * FT + j, act_hi, act_lo, k0=8 * e, kn=kn,
                                  last=(e == 2),
                                  before=(lambda k: pe.wait_ge(act_ready, FT * layer + k + 1)) if j == 0 else None)

            def odd_mixer():
                a0, u0 = mix_acc(1), UNIT0[1]

                def rotate(j, b, rots, which):
                    t = aux_at[rots] + j
                    aux_free(pe, t)
                    pe.wait_ge(acc_drained, a0 + b + j + 1)
                    pe.matmul(auxs[t % 4][:, :], perm[:, which, :], tmp[:, j % 2, :], start=True, stop=True)\
                        .then_inc(aux_done, 1)

                cols_units(u0 + U_DV, a0 + BV, u_hi, u_lo, TT, before=u_in(3), after=stats_after(3))
                pe.wait_ge(c1_in, 16 * 3)
                for j in range(8):
                    rows_unit(u0 + U_DQK + j, a0 + BQK + j, u_hi, u_lo)
                    if j:
                        rotate(j - 1, BQK, "rotd", 0)
                rotate(7, BQK, "rotd", 0)
                pe.wait_ge(rot_ready, 8)

                def scores(h):
                    q0 = DH * (h % 2)
                    for i in range(TT):
                        t = aux_at["ds", h] + i
                        aux_free(pe, t)
                        pe.matmul(auxs[t % 4][:, 0:(i + 1) * P], tq[q0:q0 + DH, h // 2, i * P:(i + 1) * P],
                                  tq[q0:q0 + DH, 4 + h // 2, 0:(i + 1) * P], start=True, stop=True)\
                            .then_inc(aux_done, 1)

                def turn(h):
                    pe.wait_ge(p_ready, X_H + h + 1)
                    for e, kts in enumerate(((0,), (1, 3), (2,))):
                        t = aux_at["dt", h] + e
                        aux_free(pe, t)
                        for kt in kts:
                            c = 384 if kt == 3 else 0
                            for i in range(kt, TT):
                                o = ROWS[i][0] + kt * P
                                ins = pe.transpose(auxs[t % 4][:, c + (i - kt) * P:c + (i - kt + 1) * P],
                                                   dp[:, h % 2, o:o + P], ident[:, :])
                        ins.then_inc(aux_done, 1)

                def values(h):
                    t = a0 + BD + h // 2
                    q0 = DH * (h % 2)
                    if h % 2 == 0:
                        acc_free(t)
                    pe.wait_ge(aux_free_a, freed_a(aux_at["dt", h] + 2))
                    for kt in range(TT):
                        o, w = BLOCK[kt]
                        ins = pe.matmul(accs[t % 4][q0:q0 + DH, kt * P:S], tv[:, kt, h * DH:(h + 1) * DH],
                                        dpt[:, o:o + w], start=(kt == 0), stop=(kt == TT - 1))
                    if h % 2:
                        ins.then_inc(acc_done, 1)

                order_dil(scores, turn, values)

                cols_units(u0 + U_RV, a0 + BRV, u_hi, u_lo, TT)
                for j in range(8):
                    rows_unit(u0 + U_RQK + j, a0 + BRQK + j, u_hi, u_lo)
                    if j:
                        rotate(j - 1, BRQK, "rotr", 1)
                rotate(7, BRQK, "rotr", 1)
                for j in range(4):
                    rows_unit(u0 + U_RG + j, a0 + BRG + j, u_hi, u_lo)
                pe.wait_ge(rot_ready, 16)

                def ret_scores(h):
                    for e, kts in enumerate(((0,), (1, 3), (2,))):
                        t = aux_at["rs", h] + e
                        aux_free(pe, t)
                        for kt in kts:
                            c, w = (384 if kt == 3 else 0), BLOCK[kt][1]
                            ins = pe.matmul(auxs[t % 4][:, c:c + w], tq[:, 4 + h, kt * P:(kt + 1) * P],
                                            tq[:, h, kt * P:S], start=True, stop=True)
                        ins.then_inc(aux_done, 1)

                def ret_values(h):
                    t = a0 + BR + h
                    acc_free(t)
                    pe.wait_ge(aux_free_v, freed_v(aux_at["rs", h] + 2))
                    for i in range(TT):
                        for kt in range(i + 1):
                            o = BLOCK[kt][0] + (i - kt) * P
                            ins = pe.matmul(accs[t % 4][:, i * P:(i + 1) * P], inner[:, h % 2, o:o + P],
                                            tv[:, kt, h * P:(h + 1) * P], start=(kt == 0), stop=(kt == i))
                    ins.then_inc(acc_done, 1)

                def ret_turn(h):
                    t = aux_at["rt", h]
                    aux_free(pe, t)
                    pe.wait_ge(acc_drained, a0 + BR + h + 1)
                    for i in range(TT):
                        ins = pe.transpose(auxs[t % 4][:, i * P:(i + 1) * P], tmp[:, h % 2, i * P:(i + 1) * P],
                                           ident[:, :])
                    ins.then_inc(aux_done, 1)

                order_ret(ret_scores, ret_values, ret_turn)
                out_proj(u0 + U_OUT1, a0 + BOUT1, a0 + BD, 4)

            cross_attention(0)
            ffn(0)
            odd_mixer()
            cross_attention(1)
            ffn(1)
            pe.wait_ge(acc_drained, f_acc(1) + A_F)
            mean(6)
            for t in range(TT):
                for c in range(2):
                    k = aux_at["out"] + 2 * t + c
                    aux_free(pe, k)
                    for e in range(4):
                        ins = pe.transpose(auxs[k % 4][:, e * P:(e + 1) * P], hT[:, 4 * c + e, t * P:(t + 1) * P],
                                           ident[:, :])
                    ins.then_inc(aux_done, 1)


def rotary_tables(dims, half, theta):
    inv = (1.0 / np.power(np.float32(theta), np.arange(half, dtype=np.float32) / np.float32(half))).astype(np.float32)
    ang = (np.arange(S, dtype=np.float32)[:, None] * inv[None, :]).astype(np.float32).astype(np.float64)
    cs = np.zeros((dims, 2, S))
    cs[:, 0] = 1.0
    turn = np.zeros((dims, dims))
    for f in range(2 * half):
        cs[f, 0], cs[f, 1] = np.cos(ang[:, f % half]), np.sin(ang[:, f % half])
        turn[(f + half) % (2 * half), f] = -1.0 if f < half else 1.0
    return cs.astype(np.float32), turn.astype(np.float32)


def constants():
    cs64, turn64 = rotary_tables(DH, 8, 500000.0)
    cs_r, turn_r = rotary_tables(P, 64, 10000.0)
    perm = np.zeros((P, 2, P), np.float32)
    perm[0:DH, 0, 0:DH] = perm[DH:, 0, DH:] = turn64
    perm[:, 1] = turn_r
    dist = np.arange(P)[:, None] - np.arange(S)[None, :] + (S - P)
    past = dist >= 0
    count = (past & (dist <= 128)).astype(int) + (past & (dist % 4 == 0)) + (past & (dist % 16 == 0))
    band = np.where(count > 0, np.log(np.maximum(count, 1)), NEG).astype(np.float32)
    rel = np.arange(S)[None, :] - np.arange(P)[:, None]
    decay = np.stack([np.where(rel >= 0, (1 - 2.0 ** (-5 - h)) ** np.maximum(rel, 0), 0.0) * P ** -0.5
                      for h in range(RET_H)], axis=1).astype(np.float32)
    inv = np.stack([1.0 / np.minimum(np.arange(PAD) + 1, w) for w in WINDOWS]).astype(np.float32)
    return {
        "ident": np.eye(P, dtype=np.float32),
        "cs_d": np.ascontiguousarray(np.concatenate([cs64, cs64])),
        "cs_r": cs_r,
        "perm": perm,
        "band": band,
        "decay": np.ascontiguousarray(decay),
        "invcnt": np.ascontiguousarray(np.broadcast_to(inv.reshape(1, -1), (P, 4 * PAD))),
    }


def weight_units(w):
    def rows(a):
        k, m = a.shape[0] // P, a.shape[1] // P
        return a.reshape(k, P, m, P).transpose(2, 1, 0, 3).reshape(m, P, k * P)

    def cols(a):
        c = a.shape[1] // 512
        return a.reshape(4, 2, P, c, 512).transpose(3, 0, 2, 1, 4).reshape(4 * c, P, UW)

    out = np.zeros((UNITS, P, UW), np.float32)
    n = [0]

    def put(u):
        out[n[0]:n[0] + len(u), :, 0:u.shape[2]] = u
        n[0] += len(u)

    even, odd = w["even_w_in"][0], w["odd_w_in"][0]
    for layer in range(LAYERS):
        if layer == 0:
            put(cols(even[:, 1024:1536]))
            put(rows(even[:, 0:1024]))
            put(rows(w["even_w_out"][0]))
        else:
            put(cols(odd[:, 1024:1536]))
            put(rows(odd[:, 0:1024]))
            put(cols(odd[:, 2560:3072]))
            put(rows(odd[:, 1536:2560]))
            put(rows(odd[:, 3072:3584]))
            put(rows(w["odd_w_out"][0]))
        put(rows(w["xattn_wkv"][layer][:, 0:D]))
        put(cols(w["xattn_wkv"][layer][:, D:]))
        put(rows(w["xattn_wq"][layer]))
        put(rows(w["xattn_wo"][layer]))
        gu = rows(w["ffn_w_gate_up"][layer])
        put(gu.reshape(2, FT, P, UW).transpose(1, 0, 2, 3).reshape(2 * FT, P, UW))
        down = rows(w["ffn_w_down"][layer])
        for j in range(KT):
            for e in range(3):
                put(down[j:j + 1, :, e * UW:min((e + 1) * UW, DFF)])
    assert n[0] == UNITS
    return out


def kernel(**inputs):
    import concourse.bacc as bacc
    from concourse.bass_utils import run_bass_kernel_spmd

    w = {k: np.asarray(v) for k, v in inputs.items()}

    def columns(v):
        return v.reshape(-1, P).T

    arrays = dict(constants())
    arrays["x"] = np.ascontiguousarray(w["x"])
    arrays["mem"] = np.ascontiguousarray(w["mem"])
    arrays["weights"] = weight_units(w)
    arrays["vecs"] = np.ascontiguousarray(np.concatenate(
        [columns(w[k]) for k in ("even_mix_norm", "odd_mix_norm", "xattn_norm", "ffn_norm", "mem_norm", "pool_scale")],
        axis=1))
    arrays["ws_t"] = np.ascontiguousarray(w["sgu_w"][0].transpose(2, 0, 1))
    arrays["pool_w"] = np.ascontiguousarray(w["pool_w"][0].transpose(1, 0, 2))
    arrays["sgu_b"] = np.ascontiguousarray(np.broadcast_to(w["sgu_b"][0].reshape(1, -1), (P, 4 * P)))
    arrays["sgu_g"] = np.ascontiguousarray(np.broadcast_to(w["sgu_norm"][0][None], (P, S)))
    arrays["final_g"] = np.ascontiguousarray(np.broadcast_to(w["final_norm"][None], (P, D)))

    nc = bacc.Bacc("TRN2", target_bir_lowering=False, num_devices=1)
    named = {f"in_{k}": a for k, a in arrays.items()}
    d = {k: nc.dram_tensor(f"in_{k}", a.shape, F32, kind="ExternalInput").ap() for k, a in arrays.items()}
    d["out"] = nc.dram_tensor("out_h", (1, S, D), F32, kind="ExternalOutput").ap()
    program(nc, d)
    r = run_bass_kernel_spmd(nc, [named], core_ids=[0])
    return r.results[0]["out_h"]
```

```python
from contextlib import ExitStack

import numpy as np

import concourse.bass as bass
from concourse import mybir

F32 = mybir.dt.float32
F32R = mybir.dt.float32r
ACT = mybir.ActivationFunctionType
ALU = mybir.AluOpType
AX = mybir.AxisListType

P = 128
D = 1024
S = 512
M = 256
KT = D // P
TT = S // P
MT = M // P
DFF = 2816
FT = DFF // P
EPS = 1e-6
LAYERS = 2
RING = 4
LEAD = 3
UW = 1024
WINDOWS = (2, 4, 8, 16)
PAD = 16
DIL_H, RET_H, X_H = 8, 4, 4
DH = 64
NEG = -1e30

U_V, U_A, U_OUT0, U_MIX0 = 0, 4, 12, 20
U_DV, U_DQK, U_RV, U_RQK, U_RG, U_OUT1, U_MIX1 = 0, 4, 12, 16, 24, 28, 36
U_KV = 2 * KT
U_X = 2 * KT
F_DN, F_END = 2 * FT, 2 * FT + 3 * KT
KV_UNIT = (0, U_KV + U_MIX0 + U_X + F_END + U_MIX1)
MIX_UNIT = (U_KV, KV_UNIT[1] - U_MIX1)
X_UNIT = (U_KV + U_MIX0, KV_UNIT[1] + U_KV)
F_UNIT = tuple(u + U_X for u in X_UNIT)
UNITS = F_UNIT[1] + F_END

A_V, A_A, A_U, A_POOL, A_SGU, A_OUT0, A_MIX0 = 0, 4, 8, 12, 16, 20, 28
B_V, B_QK, B_RV, B_D, B_R, B_OUT1, B_MIX1 = 0, 4, 12, 16, 32, 36, 44
A_K, A_XV, A_KV = 0, 8, 12
A_Q, A_XO, A_O, A_X = 0, 8, 16, 24
A_DN, A_F = 2 * FT, 2 * FT + KT
KV_ACC = (0, A_KV + A_MIX0 + A_X + A_F + B_MIX1)
MIX_ACC = (A_KV, KV_ACC[1] - B_MIX1)
X_ACC = (A_KV + A_MIX0, KV_ACC[1] + A_KV)
F_ACC = tuple(a + A_X for a in X_ACC)

C_EVEN, C_ODD, C_XN, C_FN, C_MN, C_PS, C_ALL = 0, 8, 16, 32, 48, 64, 68


def aux_plan():
    who, at = [], {}

    def add(name, s):
        at[name] = len(who)
        who.extend(s)

    add("mem", "vvvv")
    add("mem row", "v")
    add("x", "a" * 8)
    add(("row", 0), "v")
    for layer in range(LAYERS):
        if layer:
            add(("mean", 3), "v")
            add(("row", 3), "v")
            add(("ds", 0), "vvvv")
            add(("ds", 1), "vvvv")
            for h in range(DIL_H):
                add(("dt", h), "aaa")
                if h + 2 < DIL_H:
                    add(("ds", h + 2), "vvvv")
            add(("rs", 0), "vvv")
            order_ret(lambda h: add(("rs", h), "vvv"), lambda h: None, lambda h: add(("rt", h), "v"))
        add(("mean", 3 * layer + 1), "v")
        add(("row", 3 * layer + 1), "v")
        add(("xs", layer, 0), "aa")
        add(("xs", layer, 1), "aa")
        order_x(lambda h: add(("xs", layer, h), "aa"), lambda h: add(("xt", layer, h), "aa"), lambda h: None)
        add(("mean", 3 * layer + 2), "v")
        add(("row", 3 * layer + 2), "v")
    add("out", "v" * 8)
    add(("mean", 6), "v")
    return who, at


def order_x(scores, turn, values):
    for h in range(X_H):
        turn(h)
        if h + 2 < X_H:
            scores(h + 2)
        values(h)


def order_ret(scores, values, turn):
    for h in range(RET_H):
        if h + 1 < RET_H:
            scores(h + 1)
        values(h)
        if h:
            turn(h - 1)
    turn(RET_H - 1)


def side_units(h):
    p = h // 2
    if h % 2 == 0:
        return (3 * p, 4 * p), None
    return (3 * p + 1, 4 * p + 1), (3 * p + 2, 4 * p + 3)


BLOCK = {0: (0, 512), 1: (512, 384), 3: (896, 128), 2: (1024, 256)}
ROWS = {0: (0, 128), 1: (128, 256), 2: (384, 384), 3: (768, 512)}


def program(nc, d):
    who, aux_at = aux_plan()

    with ExitStack() as ctx:
        def sem(name):
            return ctx.enter_context(nc.semaphore(name))

        def fixed(name, shape, dt=F32):
            return ctx.enter_context(nc.sbuf_tensor(name, shape, dt))

        base = (nc.sbuf_base + 31) // 32 * 32
        fixed("arena", [P, 120 * 256])

        def at(name, kib, shape, dt=F32):
            return nc.alloc_sbuf_tensor_at(name, shape, dt, offset=int(base + kib * 1024))

        act_hi = at("act_hi", 0, [P, FT, S], F32R)
        act_lo = at("act_lo", 44, [P, FT, S], F32R)
        y_hi = at("y_hi", 0, [P, KT, S], F32R)
        y_lo = at("y_lo", 16, [P, KT, S], F32R)
        x_tok = at("x_tok", 0, [P, TT, D])
        mem_tok = at("mem_tok", 16, [P, MT, D])
        vn = at("vn", 32, [P, TT, S])
        uu = at("uu", 40, [P, 4, S])
        a_pad = at("a_pad", 64, [P, 4, PAD + S])
        wsum = at("wsum", 8, [P, 3, PAD + S])
        ws_t = at("ws_t", 72.5, [P, 4, P])
        pool_w = at("pool_w", 74.5, [P, 4, P])
        sgu_b = at("sgu_b", 76.5, [P, 4, P])
        sgu_g = at("sgu_g", 78.5, [P, S])
        junk = at("junk", 84, [P, D])
        mem_hi = at("mem_hi", 32, [P, KT, M], F32R)
        mem_lo = at("mem_lo", 40, [P, KT, M], F32R)
        xk = at("xk", 48, [P, KT, M])
        xv = at("xv", 56, [P, MT, D])
        xq = at("xq", 64, [P, KT, S])
        xp = at("xp", 80, [P, 2, TT, M])
        xpt = at("xpt", 32, [P, MT, S])
        tq_d = at("tq_d", 8, [P, 4, S])
        tk_d = at("tk_d", 24, [P, 4, S])
        gate = at("gate", 8, [P, 4, S])
        cs_r = at("cs_r", 32, [P, 2, S])
        decay012 = at("decay012", 32, [P, 3, S])
        band = at("band", 38, [P, S])
        tv_d = at("tv_d", 40, [P, TT, S])
        tq = at("tq", 48, [P, 8, S])
        tv = at("tv", 64, [P, TT, S])
        cs_d = at("cs_d", 72, [P, 2, S])
        dp = at("dp", 72, [P, 2, 1280])
        inner = at("inner", 72, [P, 2, 1280])
        dpt = at("dpt", 82, [P, 1280])
        u_hi = at("u_hi", 88, [P, KT, S], F32R)
        u_lo = at("u_lo", 104, [P, KT, S], F32R)
        y_tok = at("y_tok", 88, [P, TT, D])

        hT = fixed("hT", [P, KT, S])
        raw = fixed("raw", [P, RING, UW])
        w_hi = fixed("w_hi", [P, RING, UW], F32R)
        w_lo = fixed("w_lo", [P, RING, UW], F32R)
        memT = fixed("memT", [P, KT, M])
        tmp = fixed("tmp", [P, 4, S])
        diag = tmp[:, 3, :]
        fin_g = memT[:, 0:KT // 2, :].rearrange("p a b -> p (a b)")
        sqsum = fixed("sqsum", [P, S])
        rstd_row = fixed("rstd_row", [P, S])
        rstd_mrow = fixed("rstd_mrow", [P, M])
        ident = fixed("ident", [P, P])
        ones = fixed("ones", [P, P])
        vecs = fixed("vecs", [P, C_ALL])
        invcnt = fixed("invcnt", [P, 4, PAD])
        mean_w = fixed("mean_w", [P, 1])
        mexp = fixed("mexp", [P, TT])
        ssq = fixed("ssq", [P, TT])
        ssq_m = fixed("ssq_m", [P, MT])
        ssq_v = fixed("ssq_v", [P, TT])
        var_e = fixed("var_e", [P, TT])
        var_m = fixed("var_m", [P, MT])
        var_v = fixed("var_v", [P, TT])
        rstd_tok = fixed("rstd_tok", [P, TT])
        rstd_m = fixed("rstd_m", [P, MT])
        rstd_v = fixed("rstd_v", [P, TT])
        nmax = fixed("nmax", [P, 2, TT])
        psums = fixed("psums", [P, 2, TT])
        pinv = fixed("pinv", [P, 2, TT])
        stats = fixed("stats", [P, TT, 6])
        mv = fixed("mv", [P, TT, 2])
        rvar = fixed("rvar", [P, 2, TT])
        rrstd = fixed("rrstd", [P, 2, TT])

        accs = [ctx.enter_context(nc.psum_tensor(f"acc{i}", [P, 512], F32)) for i in range(4)]
        auxs = [ctx.enter_context(nc.psum_tensor(f"aux{i}", [P, 512], F32)) for i in range(4)]

        raw_in = [sem(f"raw_in{i}") for i in range(RING)]
        hi_ready = sem("hi_ready")
        lo_ready = sem("lo_ready")
        unit_used = sem("unit_used")
        acc_done = sem("acc_done")
        acc_drained = sem("acc_drained")
        aux_done = sem("aux_done")
        aux_free_v = sem("aux_free_v")
        aux_free_a = sem("aux_free_a")
        x_in = sem("x_in")
        mem_in = sem("mem_in")
        c0_in = sem("c0_in")
        c1_in = sem("c1_in")
        c2_in = sem("c2_in")
        fin_in = sem("fin_in")
        const_set = sem("const_set")
        ws_masked = sem("ws_masked")
        x_sq = sem("x_sq")
        sq_ready = sem("sq_ready")
        sq_added = sem("sq_added")
        uhi_ready = sem("uhi_ready")
        u_ready = sem("u_ready")
        var_ready = sem("var_ready")
        rstd_ready = sem("rstd_ready")
        diag_ready = sem("diag_ready")
        mhi_ready = sem("mhi_ready")
        mlo_ready = sem("mlo_ready")
        part_hi = sem("part_hi")
        vgelu = sem("vgelu")
        vsq = sem("vsq")
        vn_ready = sem("vn_ready")
        ugelu = sem("ugelu")
        win_ready = sem("win_ready")
        win_step = sem("win_step")
        d_ready = sem("d_ready")
        silu_ready = sem("silu_ready")
        prod_ready = sem("prod_ready")
        ahi_ready = sem("ahi_ready")
        act_ready = sem("act_ready")
        shifted = sem("shifted")
        rot_half = sem("rot_half")
        rot_ready = sem("rot_ready")
        dve_step = sem("dve_step")
        max_ready = sem("max_ready")
        exp_ready = sem("exp_ready")
        p_ready = sem("p_ready")
        pt_ready = sem("pt_ready")
        in_ready = sem("in_ready")
        rvar_ready = sem("rvar_ready")
        rrstd_ready = sem("rrstd_ready")
        y_full = sem("y_full")
        y_ready = sem("y_ready")
        out_ready = sem("out_ready")
        out_in = sem("out_in")

        def lin(c, i, k):
            return c if i is None else i * k + c

        def aux_free(eng, t):
            if t >= 4:
                w = who[t - 4]
                eng.wait_ge(aux_free_v if w == "v" else aux_free_a, who[:t - 3].count(w))

        def slot_free(eng, n, i=None):
            ends, count = used[n]
            eng.wait_ge(acc_done if ends else unit_used, lin(count, i, RING))

        PHX, PHM1 = (8, 24), 16
        XMAX, DMAX = (0, 2 * X_H + TT * DIL_H), 2 * X_H
        SILU = (0, FT + RET_H)
        ROUND = {0: 1, 1: 3, 2: 4, 3: 5, 4: 6, 5: 7, 6: 8}

        def freed_v(t):
            return who[:t + 1].count("v")

        def freed_a(t):
            return who[:t + 1].count("a")

        def decay(h):
            return decay012[:, h, :] if h < 3 else sqsum[:, :]

        used, mid = [], [0]

        def rows_used(t, tiles, per=1):
            for j in range(tiles):
                for e in range(per):
                    mid[0] += e < per - 1
                    used.append((e == per - 1, t + j + 1 if e == per - 1 else mid[0]))

        def cols_used(t, tiles):
            for q in range(4):
                mid[0] += q < 3
                used.append((q == 3, t + tiles if q == 3 else mid[0]))

        def kv_used(a):
            rows_used(a + A_K, KT)
            cols_used(a + A_XV, MT)
            cols_used(a + A_XV + MT, MT)

        for layer in range(LAYERS):
            a = MIX_ACC[layer]
            if layer == 0:
                kv_used(KV_ACC[0])
                cols_used(a + A_V, TT)
                rows_used(a + A_A, 8)
                rows_used(a + A_OUT0, KT)
            else:
                cols_used(a + B_V, TT)
                rows_used(a + B_QK, 8)
                cols_used(a + B_RV, TT)
                for h in range(DIL_H):
                    for r in side_units(h):
                        if r is not None:
                            used.append((True, a + B_D + r[1] + 1))
                rows_used(a + B_OUT1, KT)
                kv_used(KV_ACC[1])
            rows_used(X_ACC[layer] + A_Q, KT)
            rows_used(X_ACC[layer] + A_O, KT)
            rows_used(F_ACC[layer], 2 * FT)
            rows_used(F_ACC[layer] + A_DN, KT, 3)
        assert len(used) == UNITS

        block = ctx.enter_context(nc.Block())

        @block.sync
        def _(sp):
            for j in range(RING):
                sp.dma_start(raw[:, j, :], d["weights"][j]).then_inc(raw_in[j], 16)
            with sp.Fori(1, UNITS // RING) as i:
                for j in range(RING):
                    sp.wait_ge(lo_ready, i * RING + (j - RING + 1))
                    sp.dma_start(raw[:, j, :], d["weights"][bass.ds(i * RING + j, 1)].rearrange("a p n -> p (a n)"))\
                        .then_inc(raw_in[j], 16)
            for t in range(TT):
                sp.wait_ge(out_ready, t + 1)
                sp.dma_start(d["out"][0, t * P:(t + 1) * P, :], y_tok[:, t, :]).then_inc(out_in, 16)
            sp.wait_ge(out_in, 16 * TT)

        @block.scalar
        def _(act):
            def split(n, i=None):
                if n >= UNITS:
                    return
                s = n % RING
                act.wait_ge(raw_in[s], lin(16 * (n // RING + 1), i, 16))
                if n >= RING:
                    slot_free(act, n - RING, i)
                act.activation(w_hi[:, s, :], raw[:, s, :], ACT.Copy).then_inc(hi_ready, 1)

            def residual(norm, j, gcol, t):
                act.wait_ge(acc_drained, t + 1)
                dst = sqsum[:, :] if j == 0 else tmp[:, j % 2, :]
                if j >= 3:
                    act.wait_ge(sq_added, 6 * (norm - 1) + j - 2)
                act.activation(dst, hT[:, j, :], ACT.Square).then_inc(sq_ready, 1)
                if gcol is not None:
                    act.activation(u_hi[:, j, :], hT[:, j, :], ACT.Copy, scale=vecs[:, gcol + j:gcol + j + 1])\
                        .then_inc(uhi_ready, 1)

            def mem_hi_part(layer, j):
                act.wait_ge(aux_free_v, freed_v(aux_at["mem"] + j // 2))
                act.activation(mem_hi[:, j, :], memT[:, j, :], ACT.Copy,
                               scale=vecs[:, C_MN + 8 * layer + j:C_MN + 8 * layer + j + 1]).then_inc(mhi_ready, 1)

            def y_hi_part(j, src, scale=1.0):
                act.activation(y_hi[:, j, :], src, ACT.Copy, scale=scale).then_inc(part_hi, 1)

            act.dma_start(ident[:, :], d["ident"]).then_inc(mem_in, 16)
            act.dma_start(mem_tok[:, :, :], d["mem"].rearrange("a (t p) n -> p (a t) n", p=P)).then_inc(mem_in, 16)
            act.dma_start(vecs[:, :], d["vecs"]).then_inc(mem_in, 16)
            for t in range(TT):
                act.dma_start(x_tok[:, t, :], d["x"][0, t * P:(t + 1) * P, :]).then_inc(x_in, 16)
            act.dma_start(sgu_g[:, :], d["sgu_g"]).then_inc(c0_in, 16)
            act.dma_start(sgu_b[:, :, :], d["sgu_b"].rearrange("p (g t) -> p g t", g=4)).then_inc(c0_in, 16)
            act.dma_start(ws_t[:, :, :], d["ws_t"]).then_inc(c0_in, 16)
            act.dma_start(pool_w[:, :, :], d["pool_w"]).then_inc(c0_in, 16)
            act.dma_start(invcnt[:, :, :], d["invcnt"].rearrange("p (g t) -> p g t", g=4)).then_inc(c0_in, 16)
            act.wait_ge(mem_in, 16 * 3)
            split(0)
            for j in range(KT):
                mem_hi_part(0, j)
            for n in range(1, LEAD):
                split(n)
            for t in range(MT):
                if t:
                    act.wait_ge(x_sq, t)
                act.activation(junk[:, :], mem_tok[:, t, :], ACT.Square, accum_out=ssq_m[:, t:t + 1]).then_inc(x_sq, 1)
            for j in range(KT):
                split(j + LEAD)
                if 2 <= j < 2 + TT:
                    act.wait_ge(x_in, 16 * TT)
                    act.wait_ge(x_sq, MT + j - 2)
                    act.activation(junk[:, :], x_tok[:, j - 2, :], ACT.Square, accum_out=ssq[:, j - 2:j - 1])\
                        .then_inc(x_sq, 1)
            for j in range(KT):
                split(KT + j + LEAD)
                t = aux_at["x"] + j
                act.wait_ge(aux_done, t + 1)
                act.activation(hT[:, j, :], auxs[t % 4][:, :], ACT.Copy).then_inc(aux_free_a, 1)
                act.wait_ge(aux_free_a, freed_a(t))
                act.activation(u_hi[:, j, :], hT[:, j, :], ACT.Copy, scale=vecs[:, C_EVEN + j:C_EVEN + j + 1])\
                    .then_inc(uhi_ready, 1)

            a0, u0 = MIX_ACC[0], MIX_UNIT[0]
            for n in range(4):
                split(u0 + n + LEAD)
            for t in range(TT):
                act.wait_ge(acc_drained, a0 + A_V + t + 1)
                act.activation(vn[:, t, :], vn[:, t, :], ACT.Gelu_apprx_tanh).then_inc(vgelu, 1)
                act.wait_ge(vgelu, t + 1)
                if t == 0:
                    act.wait_ge(x_sq, TT + MT)
                else:
                    act.wait_ge(vsq, t)
                act.activation(junk[:, 0:S], vn[:, t, :], ACT.Square, accum_out=ssq_v[:, t:t + 1]).then_inc(vsq, 1)
                split(u0 + t + 4 + LEAD)
            for g in range(4):
                split(u0 + g + 8 + LEAD)
                act.wait_ge(acc_drained, a0 + A_U + g + 1)
                act.activation(uu[:, g, :], uu[:, g, :], ACT.Gelu_apprx_tanh).then_inc(ugelu, 1)
            for g in range(4):
                act.wait_ge(acc_done, a0 + A_POOL + g + 1)
                y_hi_part(g, accs[(a0 + A_POOL + g) % 4][:, :], scale=vecs[:, C_PS + g:C_PS + g + 1])
            for g in range(4):
                act.wait_ge(y_full, g + 1)
                y_hi_part(4 + g, tmp[:, g % 2, :])

            def out_phase(layer, norm, u0, a0, gcol, with_mem=False):
                for j in range(KT):
                    split(u0 + j + LEAD)
                    residual(norm, j, gcol, a0 + j)
                    if with_mem:
                        mem_hi_part(layer, j)

            def cross_attention(layer):
                a0, u0 = X_ACC[layer], X_UNIT[layer]

                def exps(h):
                    for q in range(TT):
                        act.wait_ge(max_ready, XMAX[layer] + 2 * h + q // 2 + 1)
                        t = aux_at["xs", layer, h] + q // 2
                        ins = act.activation(xp[:, h % 2, q, :], auxs[t % 4][:, (q % 2) * M:(q % 2 + 1) * M], ACT.Exp,
                                             bias=nmax[:, h % 2, q:q + 1], accum_out=psums[:, h % 2, q:q + 1])
                        if q % 2:
                            ins.then_inc(aux_free_a, 1)

                def turned(h):
                    for k in range(MT):
                        t = aux_at["xt", layer, h] + k
                        act.wait_ge(aux_done, t + 1)
                        act.activation(xpt[:, k, :], auxs[t % 4][:, :], ACT.Copy).then_inc(aux_free_a, 1)

                def parts(h):
                    for e in range(2):
                        t = a0 + A_XO + 2 * h + e
                        act.wait_ge(acc_done, t + 1)
                        y_hi_part(2 * h + e, accs[t % 4][:, :])

                for j in range(KT):
                    split(u0 + j + LEAD)
                    if j in (4, 6):
                        exps(j // 2 - 2)
                for h in range(X_H):
                    turned(h)
                    if h + 2 < X_H:
                        exps(h + 2)
                    parts(h)
                out_phase(layer, 3 * layer + 2, u0 + KT, a0 + A_O, C_FN + 8 * layer)

            def ffn(layer):
                u0, a0 = F_UNIT[layer], F_ACC[layer]
                pr0 = layer * FT
                if layer == LAYERS - 1:
                    act.dma_start(fin_g, d["final_g"]).then_inc(fin_in, 16)

                def group(g, i=None):
                    for e in range(2):
                        pair = 2 * g + e
                        n = u0 + 4 * g + 2 * e
                        if g or e:
                            act.wait_ge(prod_ready, lin(pr0 + pair, i, 2))
                        split(n + LEAD, i)
                        if g or e:
                            idx = pair - 1 if i is None else i * 2 + (pair - 1)
                            act.activation(act_hi[:, idx, :], tmp[:, 2 + (pair - 1) % 2, :], ACT.Copy).then_inc(ahi_ready, 1)
                        if not g and not e:
                            split(n + 1 + LEAD)
                        act.wait_ge(acc_drained, lin(a0 + 2 * pair + 1, i, 4))
                        act.activation(tmp[:, e, :], tmp[:, e, :], ACT.Silu).then_inc(silu_ready, 1)
                        if g or e:
                            split(n + 1 + LEAD, i)

                group(0)
                group(1)
                with act.Fori(0, FT // 2 - 2) as i:
                    group(2, i)
                act.wait_ge(prod_ready, pr0 + FT)
                act.activation(act_hi[:, FT - 1, :], tmp[:, 3, :], ACT.Copy).then_inc(ahi_ready, 1)
                norm = 3 * layer + 3
                for j in range(KT):
                    for e in range(3):
                        split(u0 + F_DN + 3 * j + e + LEAD)
                    residual(norm, j, C_ODD if layer == 0 else None, a0 + A_DN + j)

            def odd_mixer():
                a0, u0 = MIX_ACC[1], MIX_UNIT[1]
                act.wait_ge(acc_done, a0)
                act.dma_start(cs_d[:, :, :], d["cs_d"]).then_inc(c1_in, 16)
                act.dma_start(cs_r[:, :, :], d["cs_r"]).then_inc(c1_in, 16)
                act.dma_start(band[:, :], d["band"]).then_inc(c1_in, 16)

                def partners(r, t, far):
                    act.wait_ge(acc_drained, t + 1)
                    if r >= 2:
                        act.wait_ge(rot_ready, r - 1)
                    for q in range(0, P, far):
                        o = q + far if q // far % 2 == 0 else q - far
                        ins = act.activation(tmp[q:q + far, 2 + r % 2, :], tmp[o:o + far, r % 2, :], ACT.Copy)
                    ins.then_inc(shifted, 1)

                def exps(h):
                    for i in range(TT):
                        act.wait_ge(max_ready, DMAX + 4 * h + i + 1)
                        o, w = ROWS[i]
                        act.activation(dp[:, h % 2, o:o + w], dp[:, h % 2, o:o + w], ACT.Exp,
                                       bias=nmax[:, h % 2, i:i + 1], accum_out=psums[:, h % 2, i:i + 1])\
                            .then_inc(exp_ready, 1)

                def turned(h):
                    for e, (o, w) in enumerate(((0, 512), (512, 512), (1024, 256))):
                        t = aux_at["dt", h] + e
                        act.wait_ge(aux_done, t + 1)
                        act.activation(dpt[:, o:o + w], auxs[t % 4][:, 0:w], ACT.Copy).then_inc(aux_free_a, 1)

                def side(place):
                    r, c = place
                    split(u0 + U_RQK + r + LEAD)
                    if r < 8:
                        partners(8 + r, a0 + B_D + c, DH)
                    else:
                        act.wait_ge(acc_drained, a0 + B_D + c + 1)
                        act.activation(gate[:, r - 8, :], gate[:, r - 8, :], ACT.Silu).then_inc(silu_ready, 1)

                for n in range(4):
                    split(u0 + n + LEAD)
                for j in range(8):
                    split(u0 + U_DQK + j + LEAD)
                    partners(j, a0 + B_QK + j, 32)
                for n in range(4):
                    split(u0 + U_RV + n + LEAD)
                    if n % 2:
                        exps(n // 2)
                for h in range(DIL_H):
                    turned(h)
                    first, second = side_units(h)
                    side(first)
                    if h % 2:
                        t = a0 + B_D + 2 * h
                        act.wait_ge(acc_done, t + 1)
                        y_hi_part(h // 2, accs[t % 4][:, :])
                    if h + 2 < DIL_H:
                        exps(h + 2)
                    if second:
                        side(second)
                    if h == 6:
                        act.wait_ge(rot_half, 16)
                        act.dma_start(decay012[:, :, :], d["decay"][:, 0:3, :]).then_inc(c2_in, 16)
                        act.dma_start(sqsum[:, :], d["decay"][:, 3, :]).then_inc(c2_in, 16)
                for h in range(RET_H):
                    act.wait_ge(aux_free_v, freed_v(aux_at["rt", h]))
                    y_hi_part(4 + h, tmp[:, 2 + h % 2, :])

            out_phase(0, 1, MIX_UNIT[0] + U_OUT0, MIX_ACC[0] + A_OUT0, C_XN)
            cross_attention(0)
            ffn(0)
            odd_mixer()
            out_phase(1, 4, MIX_UNIT[1] + U_OUT1, MIX_ACC[1] + B_OUT1, C_XN + 8, with_mem=True)
            for n in range(U_KV):
                split(KV_UNIT[1] + n + LEAD)
            cross_attention(1)
            ffn(1)

        @block.gpsimd
        def _(pool):
            pool.memset(ones[:, :], 1.0).then_inc(const_set, 1)
            pool.memset(mean_w[:, :], 1.0 / D).then_inc(const_set, 1)
            pool.memset(mexp[:, :], -0.5).then_inc(const_set, 1)
            pool.memset(a_pad[:, :, 0:PAD], 0.0).then_inc(const_set, 1)
            pool.wait_ge(const_set, 4)

            def power(dst, src, n):
                pool.tensor_tensor(dst, src, mexp[:, 0:n], ALU.pow).then_inc(rstd_ready, 1)

            def norm_power(norm):
                pool.wait_ge(aux_free_v, freed_v(aux_at["mean", norm]))
                power(rstd_tok[:, :], var_e[:, :], TT)

            def add_squares(norm):
                for j in range(1, KT - 1):
                    n = 6 * (norm - 1) + j
                    pool.wait_ge(sq_ready, 8 * (norm - 1) + j + 1)
                    if j > 1:
                        pool.wait_ge(sq_added, n - 1)
                    pool.tensor_tensor(sqsum[:, :], sqsum[:, :], tmp[:, j % 2, :], ALU.add).then_inc(sq_added, 1)

            pool.wait_ge(var_ready, 1)
            power(rstd_m[:, :], var_m[:, :], MT)
            pool.wait_ge(var_ready, 2)
            power(rstd_tok[:, :], var_e[:, :], TT)
            pool.wait_ge(c0_in, 16 * 5)
            pool.affine_select(out=ws_t[:, :, :], in_=ws_t[:, :, :], compare_op=ALU.is_ge, fill=0.0, base=0,
                               pattern=[[0, 4], [1, P]], channel_multiplier=-1).then_inc(ws_masked, 1)
            steps = 0
            for g, win in enumerate(WINDOWS):
                pool.wait_ge(acc_drained, MIX_ACC[0] + A_A + g + 1)
                if g == 0:
                    pool.wait_ge(var_ready, 3)
                    power(rstd_v[:, :], var_v[:, :], TT)
                if g:
                    pool.wait_ge(win_ready, g)
                src, width = a_pad[:, g, :], 1
                buf = 0
                while width < win:
                    last = 2 * width == win
                    if last and g >= 1:
                        pool.wait_ge(d_ready, g)
                    dst = wsum[:, 2 if last else buf, :]
                    lo = 2 * width - 1
                    ins = pool.tensor_tensor(dst[:, lo:PAD + S], src[:, lo:PAD + S],
                                             src[:, lo - width:PAD + S - width], ALU.add)
                    if last:
                        ins.then_inc(win_ready, 1)
                    else:
                        ins.then_inc(win_step, 1)
                        steps += 1
                        pool.wait_ge(win_step, steps)
                    src, buf, width = dst, 1 - buf, 2 * width
            for layer in range(LAYERS):
                if layer:
                    add_squares(3)
                    norm_power(3)
                    for r in range(16):
                        dst = (tq_d if r < 4 else tk_d)[:, r % 4, :] if r < 8 else tq[:, r - 8, :]
                        pool.wait_ge(rot_half, r + 1)
                        pool.tensor_tensor(dst, dst, tmp[:, 2 + r % 2, :], ALU.add).then_inc(rot_ready, 1)
                    for h in range(RET_H):
                        pool.wait_ge(rvar_ready, h + 1)
                        pool.tensor_tensor(rrstd[:, h % 2, :], rvar[:, h % 2, :], mexp[:, :], ALU.pow)\
                            .then_inc(rrstd_ready, 1)
                for norm in (3 * layer + 1, 3 * layer + 2):
                    add_squares(norm)
                    norm_power(norm)
            add_squares(6)
            norm_power(6)

        @block.vector
        def _(dve):
            chain = [0]

            def step(ins):
                chain[0] += 1
                ins.then_inc(dve_step, 1)
                return chain[0]

            def split(n, i=None):
                if n >= UNITS:
                    return
                s = n % RING
                dve.wait_ge(hi_ready, lin(n + 1, i, RING))
                dve.tensor_tensor(w_lo[:, s, :], raw[:, s, :], w_hi[:, s, :].bitcast(F32), ALU.subtract)\
                    .then_inc(lo_ready, 1)

            def acc(t):
                return accs[t % 4]

            def u_lo_part(norm, j, gcol):
                dve.wait_ge(uhi_ready, 8 * norm + j + 1)
                dve.scalar_tensor_tensor(out=u_lo[:, j, :], in0=hT[:, j, :], scalar=vecs[:, gcol + j:gcol + j + 1],
                                         in1=u_hi[:, j, :].bitcast(F32), op0=ALU.mult, op1=ALU.subtract)\
                    .then_inc(u_ready, 1)

            def y_lo_part(j, src, count, ready, scale=None):
                dve.wait_ge(part_hi, count)
                if scale is None:
                    ins = dve.tensor_tensor(y_lo[:, j, :], src, y_hi[:, j, :].bitcast(F32), ALU.subtract)
                else:
                    ins = dve.scalar_tensor_tensor(out=y_lo[:, j, :], in0=src, scalar=scale,
                                                   in1=y_hi[:, j, :].bitcast(F32), op0=ALU.mult, op1=ALU.subtract)
                ins.then_inc(ready, 1)

            def mean_to_var(norm):
                t = aux_at["mean", norm]
                dve.wait_ge(aux_done, t + 1)
                dve.tensor_scalar(var_e[:, :], auxs[t % 4][:, 0:TT], EPS, None, ALU.add).then_inc(aux_free_v, 1)

            def make_diag(norm):
                dve.wait_ge(rstd_ready, ROUND[norm] + 1)
                for t in range(TT):
                    ins = dve.tensor_scalar(diag[:, t * P:(t + 1) * P], ident[:, :], rstd_tok[:, t:t + 1], None,
                                            ALU.mult)
                ins.then_inc(diag_ready, 1)

            def make_row(norm):
                t = aux_at["row", norm]
                dve.wait_ge(aux_done, t + 1)
                dve.tensor_copy(rstd_row[:, :], auxs[t % 4][:, :]).then_inc(aux_free_v, 1)
                dve.wait_ge(aux_free_v, freed_v(t))

            def scaled(t, dst, sems=None, f=None):
                dve.wait_ge(acc_done, t + 1)
                if f is None:
                    ins = dve.tensor_tensor(dst, acc(t)[:, :], rstd_row[:, :], ALU.mult)
                else:
                    ins = dve.scalar_tensor_tensor(out=dst, in0=acc(t)[:, :], scalar=f, in1=rstd_row[:, :],
                                                   op0=ALU.mult, op1=ALU.mult)
                ins.then_inc(acc_drained, 1)

            def scaled_tok(t, dst, i):
                dve.wait_ge(acc_done, t + 1)
                dve.tensor_scalar(dst, acc(t)[:, :], rstd_tok[:, i:i + 1], None, ALU.mult).then_inc(acc_drained, 1)

            def mem_lo_part(layer, j):
                c = C_MN + 8 * layer + j
                dve.wait_ge(mhi_ready, 8 * layer + j + 1)
                dve.scalar_tensor_tensor(out=mem_lo[:, j, :], in0=memT[:, j, :], scalar=vecs[:, c:c + 1],
                                         in1=mem_hi[:, j, :].bitcast(F32), op0=ALU.mult, op1=ALU.subtract)\
                    .then_inc(mlo_ready, 1)

            def out_tile(j):
                k = aux_at["out"] + j
                if j == 0:
                    dve.wait_ge(fin_in, 16)
                w = slice(j * P, (j + 1) * P)
                dve.wait_ge(aux_done, k + 1)
                dve.tensor_tensor(y_tok[:, :, w], auxs[k % 4][:, :].rearrange("p (t f) -> p t f", t=TT),
                                  fin_g[:, w].rearrange("p (a f) -> p a f", a=1).broadcast_to([P, TT, P]),
                                  ALU.mult).then_inc(aux_free_v, 1)

            def residual_phase(layer, norm, a0, u0, per, gcol, with_mem=False):
                for j in range(KT):
                    for e in range(per):
                        split(u0 + per * j + e + LEAD)
                    dve.wait_ge(acc_done, a0 + j + 1)
                    dve.tensor_tensor(hT[:, j, :], hT[:, j, :], acc(a0 + j)[:, :], ALU.add).then_inc(acc_drained, 1)
                    if gcol is not None and j:
                        u_lo_part(norm, j - 1, gcol)
                    if norm == 6 and j:
                        out_tile(j - 1)
                    if with_mem:
                        mem_lo_part(layer, j)
                if gcol is not None:
                    u_lo_part(norm, KT - 1, gcol)

            def kv_drain(layer, j):
                t = KV_ACC[layer] + j
                dve.wait_ge(acc_done, t + 1)
                if j < KT:
                    ins = dve.tensor_tensor(xk[:, j, :], acc(t)[:, 0:M], rstd_mrow[:, :], ALU.mult)
                else:
                    c, m = (j - KT) // MT, (j - KT) % MT
                    ins = dve.tensor_scalar(xv[:, m, c * S:(c + 1) * S], acc(t)[:, :], rstd_m[:, m:m + 1], None,
                                            ALU.mult)
                ins.then_inc(acc_drained, 1)

            for t in range(4):
                k = aux_at["mem"] + t
                dve.wait_ge(aux_done, k + 1)
                dve.tensor_copy(memT[:, 2 * t:2 * t + 2, :], auxs[k % 4][:, :].rearrange("p (a b) -> p a b", a=2))\
                    .then_inc(aux_free_v, 1)
                if t == 0:
                    split(0)
            dve.wait_ge(aux_free_v, freed_v(aux_at["mem"] + 3))
            for j in range(KT):
                mem_lo_part(0, j)
            for n in range(1, LEAD):
                split(n)
            dve.wait_ge(x_sq, MT)
            dve.tensor_scalar(var_m[:, :], ssq_m[:, :], 1.0 / D, EPS, ALU.mult, ALU.add).then_inc(var_ready, 1)
            for j in range(KT):
                split(j + LEAD)
                if j == 0:
                    dve.wait_ge(rstd_ready, 1)
                    for t in range(MT):
                        ins = dve.tensor_scalar(diag[:, t * P:(t + 1) * P], ident[:, :], rstd_m[:, t:t + 1], None,
                                                ALU.mult)
                    ins.then_inc(diag_ready, 1)
                if j == 1:
                    t = aux_at["mem row"]
                    dve.wait_ge(aux_done, t + 1)
                    dve.tensor_copy(rstd_mrow[:, :], auxs[t % 4][:, 0:M]).then_inc(aux_free_v, 1)
                    dve.wait_ge(aux_free_v, freed_v(t))
                    kv_drain(0, 0)
                if j:
                    kv_drain(0, j)
                if j == 6:
                    dve.wait_ge(x_sq, MT + TT)
                    dve.tensor_scalar(var_e[:, 0:TT], ssq[:, 0:TT], 1.0 / D, EPS, ALU.mult, ALU.add)\
                        .then_inc(var_ready, 1)
                    make_diag(0)
            for j in range(KT):
                split(KT + j + LEAD)
                if j:
                    u_lo_part(0, j - 1, C_EVEN)
                if j % 4 == 3:
                    for m in range(MT):
                        kv_drain(0, KT + (j // 4) * MT + m)
            u_lo_part(0, KT - 1, C_EVEN)

            a0, u0 = MIX_ACC[0], MIX_UNIT[0]
            for n in range(4):
                split(u0 + n + LEAD)
                if n == 0:
                    make_row(0)
            for t in range(TT):
                scaled_tok(a0 + A_V + t, vn[:, t, :], t)

            def pooled(g):
                win = WINDOWS[g]
                dve.wait_ge(win_ready, g + 1)
                n1 = step(dve.tensor_tensor(tmp[:, 2, 0:PAD], wsum[:, 2, PAD:2 * PAD], invcnt[:, g, :], ALU.mult))
                dve.scalar_tensor_tensor(out=a_pad[:, g, 2 * PAD:PAD + S], in0=wsum[:, 2, 2 * PAD:PAD + S], scalar=1.0 / win,
                                         in1=a_pad[:, g, 2 * PAD:PAD + S], op0=ALU.mult, op1=ALU.subtract)
                dve.wait_ge(dve_step, n1)
                dve.tensor_tensor(a_pad[:, g, PAD:2 * PAD], tmp[:, 2, 0:PAD], a_pad[:, g, PAD:2 * PAD], ALU.subtract)\
                    .then_inc(d_ready, 1)

            dve.wait_ge(const_set, 4)
            dve.wait_ge(c0_in, 16 * 5)
            for g in range(4):
                split(u0 + 4 + g + LEAD)
                scaled(a0 + A_A + g, a_pad[:, g, PAD:PAD + S])
                if g == 0:
                    dve.wait_ge(vsq, TT)
                    dve.tensor_scalar(var_v[:, :], ssq_v[:, :], 1.0 / S, EPS, ALU.mult, ALU.add)\
                        .then_inc(var_ready, 1)
                if g == 1:
                    dve.wait_ge(rstd_ready, 3)
                    for t in range(TT):
                        dve.scalar_tensor_tensor(out=vn[:, t, :], in0=vn[:, t, :], scalar=rstd_v[:, t:t + 1],
                                                 in1=sgu_g[:, :], op0=ALU.mult, op1=ALU.mult).then_inc(vn_ready, 1)
            for g in range(4):
                split(u0 + 8 + g + LEAD)
                scaled(a0 + A_U + g, uu[:, g, :])
                pooled(g)
            for g in range(4):
                t = a0 + A_POOL + g
                y_lo_part(g, acc(t)[:, :], g + 1, acc_drained, scale=vecs[:, C_PS + g:C_PS + g + 1])
            for g in range(4):
                t = a0 + A_SGU + g
                dve.wait_ge(acc_done, t + 1)
                if g >= 2:
                    dve.wait_ge(y_ready, g - 1)
                dve.tensor_tensor(tmp[:, g % 2, :].rearrange("p (n t) -> p n t", n=TT),
                                  acc(t)[:, :].rearrange("p (n t) -> p n t", n=TT),
                                  sgu_b[:, g:g + 1, :].broadcast_to([P, TT, P]), ALU.add).then_inc(acc_drained, 1)
                dve.wait_ge(acc_drained, t + 1)
                dve.wait_ge(ugelu, g + 1)
                dve.tensor_tensor(tmp[:, g % 2, :], tmp[:, g % 2, :], uu[:, g, :], ALU.mult).then_inc(y_full, 1)
                if g:
                    y_lo_part(4 + g - 1, tmp[:, (g - 1) % 2, :], 4 + g, y_ready)
            y_lo_part(7, tmp[:, 1, :], 8, y_ready)
            residual_phase(0, 1, a0 + A_OUT0, u0 + U_OUT0, 1, C_XN)

            def cross_attention(layer):
                norm = 3 * layer + 1
                a0, u0 = X_ACC[layer], X_UNIT[layer]
                if layer:
                    for j in range(KT):
                        split(KV_UNIT[1] + j + LEAD)
                        if j == 0:
                            mean_to_var(norm)
                            make_diag(norm)
                        if j == 1:
                            make_row(norm)
                        kv_drain(1, j)
                    for j in range(KT):
                        split(KV_UNIT[1] + KT + j + LEAD)
                        if j % 4 == 3:
                            for m in range(MT):
                                kv_drain(1, KT + (j // 4) * MT + m)

                def maxima(h):
                    for q in range(2):
                        t = aux_at["xs", layer, h] + q
                        dve.wait_ge(aux_done, t + 1)
                        dve.tensor_reduce(nmax[:, h % 2, 2 * q:2 * q + 2],
                                          auxs[t % 4][:, :].rearrange("p (a b) -> p a b", a=2), AX.X, ALU.max,
                                          negate=True).then_inc(max_ready, 1)

                def normalise(h):
                    dve.wait_ge(aux_free_a, freed_a(aux_at["xs", layer, h] + 1))
                    n = step(dve.reciprocal(pinv[:, h % 2, :], psums[:, h % 2, :]))
                    dve.wait_ge(dve_step, n)
                    for q in range(TT):
                        ins = dve.tensor_scalar(xp[:, h % 2, q, :], xp[:, h % 2, q, :], pinv[:, h % 2, q:q + 1],
                                                None, ALU.mult)
                    ins.then_inc(p_ready, 1)

                def parts(h):
                    for e in range(2):
                        t = a0 + A_XO + 2 * h + e
                        y_lo_part(2 * h + e, acc(t)[:, :], PHX[layer] + 2 * h + e + 1, acc_drained)

                for j in range(KT):
                    if j != 1 or layer:
                        split(u0 + j + LEAD)
                    if j == 0 and not layer:
                        mean_to_var(norm)
                        make_diag(norm)
                        split(u0 + 1 + LEAD)
                        make_row(norm)
                    scaled(a0 + A_Q + j, xq[:, j, :], f=float(256) ** -0.5)
                    if j in (4, 6):
                        maxima(j // 2 - 2)
                        normalise(j // 2 - 2)
                for h in range(X_H):
                    if h + 2 < X_H:
                        maxima(h + 2)
                    parts(h)
                    if h + 2 < X_H:
                        normalise(h + 2)
                residual_phase(layer, 3 * layer + 2, a0 + A_O, u0 + KT, 1, C_FN + 8 * layer)

            def ffn(layer):
                norm = 3 * layer + 2
                u0, a0 = F_UNIT[layer], F_ACC[layer]
                pr0 = layer * FT

                def lo_of(pair, i=None):
                    dve.wait_ge(ahi_ready, lin(pr0 + pair + 1, i, 2))
                    idx = pair if i is None else i * 2 + pair
                    dve.tensor_tensor(act_lo[:, idx, :], tmp[:, 2 + pair % 2, :], act_hi[:, idx, :].bitcast(F32),
                                      ALU.subtract).then_inc(act_ready, 1)

                def group(g, i=None):
                    for e in range(2):
                        pair = 2 * g + e
                        n = u0 + 4 * g + 2 * e
                        tg = a0 + 4 * g + 2 * e
                        split(n + LEAD, i)
                        if pair == 0:
                            mean_to_var(norm)
                            make_diag(norm)
                            split(n + 1 + LEAD)
                            make_row(norm)
                        dve.wait_ge(acc_done, lin(tg + 1, i, 4))
                        dve.tensor_tensor(tmp[:, e, :], acc(tg)[:, :], rstd_row[:, :], ALU.mult)\
                            .then_inc(acc_drained, 1)
                        if pair >= 1:
                            lo_of(pair - 1, i)
                        if pair:
                            split(n + 1 + LEAD, i)
                        dve.wait_ge(acc_done, lin(tg + 2, i, 4))
                        dve.tensor_tensor(tmp[:, 2 + e, :], acc(tg + 1)[:, :], rstd_row[:, :], ALU.mult)\
                            .then_inc(acc_drained, 1)
                        dve.wait_ge(silu_ready, lin(SILU[layer] + pair + 1, i, 2))
                        dve.wait_ge(acc_drained, lin(tg + 2, i, 4))
                        dve.tensor_tensor(tmp[:, 2 + e, :], tmp[:, 2 + e, :], tmp[:, e, :], ALU.mult)\
                            .then_inc(prod_ready, 1)

                group(0)
                group(1)
                with dve.Fori(0, FT // 2 - 2) as i:
                    group(2, i)
                lo_of(FT - 1)
                residual_phase(layer, 3 * layer + 3, a0 + A_DN, u0 + F_DN, 3, C_ODD if layer == 0 else None)

            def odd_mixer():
                a0, u0 = MIX_ACC[1], MIX_UNIT[1]

                def rotate(r):
                    dst = (tq_d if r < 4 else tk_d)[:, r % 4, :] if r < 8 else tq[:, r - 8, :]
                    cs = cs_d if r < 8 else cs_r
                    dve.tensor_tensor(dst, tmp[:, r % 2, :], cs[:, 0, :], ALU.mult)
                    dve.wait_ge(shifted, r + 1)
                    dve.tensor_tensor(tmp[:, 2 + r % 2, :], tmp[:, 2 + r % 2, :], cs[:, 1, :], ALU.mult)\
                        .then_inc(rot_half, 1)

                def masked(h):
                    for i in range(TT):
                        t = aux_at["ds", h] + i
                        o, w = ROWS[i]
                        dve.wait_ge(aux_done, t + 1)
                        dve.scalar_tensor_tensor(out=dp[:, h % 2, o:o + w], in0=auxs[t % 4][:, 0:w],
                                                 scalar=float(DH) ** -0.5, in1=band[:, S - w:S], op0=ALU.mult,
                                                 op1=ALU.add).then_inc(aux_free_v, 1)
                    for i in range(TT):
                        t = aux_at["ds", h] + i
                        o, w = ROWS[i]
                        dve.wait_ge(aux_free_v, freed_v(t))
                        dve.tensor_reduce(nmax[:, h % 2, i:i + 1], dp[:, h % 2, o:o + w], AX.X, ALU.max,
                                          negate=True).then_inc(max_ready, 1)

                def normalise(h):
                    dve.wait_ge(exp_ready, 4 * h + 4)
                    n = step(dve.reciprocal(pinv[:, h % 2, :], psums[:, h % 2, :]))
                    dve.wait_ge(dve_step, n)
                    for i in range(TT):
                        o, w = ROWS[i]
                        ins = dve.tensor_scalar(dp[:, h % 2, o:o + w], dp[:, h % 2, o:o + w],
                                                pinv[:, h % 2, i:i + 1], None, ALU.mult)
                    ins.then_inc(p_ready, 1)

                def decayed(h):
                    for e, kts in enumerate(((0,), (1, 3), (2,))):
                        t = aux_at["rs", h] + e
                        dve.wait_ge(aux_done, t + 1)
                        for kt in kts:
                            o, w = BLOCK[kt]
                            c = 384 if kt == 3 else 0
                            ins = dve.tensor_tensor(inner[:, h % 2, o:o + w], auxs[t % 4][:, c:c + w],
                                                    decay(h)[:, 0:w], ALU.mult)
                        ins.then_inc(aux_free_v, 1)

                def side(place):
                    r, c = place
                    split(u0 + U_RQK + r + LEAD)
                    if r < 8:
                        dve.wait_ge(rot_half, 8 + r - 1)
                    scaled(a0 + B_D + c, tmp[:, r % 2, :] if r < 8 else gate[:, r - 8, :])
                    if 0 < r <= 8:
                        rotate(8 + r - 1)

                for n in range(4):
                    split(u0 + n + LEAD)
                    if n == 0:
                        mean_to_var(3)
                        make_diag(3)
                    if n == 1:
                        make_row(3)
                for t in range(TT):
                    scaled_tok(a0 + B_V + t, tv_d[:, t, :], t)
                dve.wait_ge(c1_in, 16 * 3)
                for j in range(8):
                    split(u0 + U_DQK + j + LEAD)
                    if j >= 2:
                        dve.wait_ge(rot_half, j - 1)
                    scaled(a0 + B_QK + j, tmp[:, j % 2, :])
                    if j:
                        rotate(j - 1)
                for n in range(4):
                    split(u0 + U_RV + n + LEAD)
                    if n == 0:
                        rotate(7)
                    if n == 1:
                        dve.wait_ge(rot_half, 8)
                        masked(0)
                    if n == 2:
                        normalise(0)
                    if n == 3:
                        masked(1)
                for t in range(TT):
                    scaled_tok(a0 + B_RV + t, tv[:, t, :], t)
                for h in range(DIL_H):
                    first, second = side_units(h)
                    if h + 1 < DIL_H:
                        normalise(h + 1)
                    side(first)
                    if h + 2 < DIL_H:
                        masked(h + 2)
                    if h % 2:
                        t = a0 + B_D + 2 * h
                        y_lo_part(h // 2, acc(t)[:, :], PHM1 + h // 2 + 1, acc_drained)
                    if h == DIL_H - 1:
                        dve.wait_ge(c2_in, 16 * 2)
                        decayed(0)
                    if second:
                        side(second)

                def head_norm(h):
                    t = a0 + B_R + h
                    dve.wait_ge(acc_done, t + 1)
                    for i in range(TT):
                        n = step(dve.bn_stats(stats[:, i, :], acc(t)[:, i * P:(i + 1) * P]))
                    dve.wait_ge(dve_step, n)
                    for i in range(TT):
                        n = step(dve.bn_aggr(mv[:, i, :], stats[:, i, :]))
                    dve.wait_ge(dve_step, n)
                    dve.tensor_scalar(rvar[:, h % 2, :], mv[:, :, 1], EPS, None, ALU.add).then_inc(rvar_ready, 1)
                    dve.wait_ge(rrstd_ready, h + 1)
                    for i in range(TT):
                        ins = dve.tensor_scalar(tmp[:, h % 2, i * P:(i + 1) * P], acc(t)[:, i * P:(i + 1) * P],
                                                mv[:, i, 0:1], rrstd[:, h % 2, i:i + 1], ALU.subtract, ALU.mult)
                    ins.then_inc(acc_drained, 1)

                def gated(h):
                    t = aux_at["rt", h]
                    dve.wait_ge(aux_done, t + 1)
                    dve.wait_ge(silu_ready, FT + h + 1)
                    dve.tensor_tensor(tmp[:, 2 + h % 2, :], auxs[t % 4][:, :], gate[:, h, :], ALU.mult)\
                        .then_inc(aux_free_v, 1)

                for h in range(RET_H):
                    if h + 1 < RET_H:
                        decayed(h + 1)
                    head_norm(h)
                    if h:
                        gated(h - 1)
                        y_lo_part(4 + h - 1, tmp[:, 2 + (h - 1) % 2, :], PHM1 + 4 + h, y_ready)
                gated(3)
                y_lo_part(7, tmp[:, 3, :], PHM1 + 8, y_ready)
                residual_phase(1, 4, a0 + B_OUT1, u0 + U_OUT1, 1, C_XN + 8, with_mem=True)

            cross_attention(0)
            ffn(0)
            odd_mixer()
            cross_attention(1)
            ffn(1)

            out_tile(KT - 1)
            mean_to_var(6)
            dve.wait_ge(rstd_ready, ROUND[6] + 1)
            dve.wait_ge(aux_free_v, freed_v(aux_at["mean", 6]))
            for t in range(TT):
                dve.tensor_scalar(y_tok[:, t, :], y_tok[:, t, :], rstd_tok[:, t:t + 1], None, ALU.mult)\
                    .then_inc(out_ready, 1)

        @block.tensor
        def _(pe):
            def three(out, w_h, w_l, x_h, x_l, first, last):
                pe.matmul(out, w_h, x_h, start=first, stop=False)
                pe.matmul(out, w_h, x_l, start=False, stop=False)
                return pe.matmul(out, w_l, x_h, start=False, stop=last)

            def acc_free(t, i=None):
                if t >= 4:
                    pe.wait_ge(acc_drained, lin(t - 3, i, 4))

            def weights_in(n, i=None):
                pe.wait_ge(lo_ready, lin(n + 1, i, RING))

            def rows_unit(n, t, x_h, x_l, i=None, before=None, k0=0, kn=KT, last=True):
                out = accs[t % 4][:, 0:x_h.shape[2]]
                s = n % RING
                weights_in(n, i)
                if k0 == 0:
                    acc_free(t, i)
                for k in range(kn):
                    if before is not None:
                        before(k0 + k)
                    w = slice(k * P, (k + 1) * P)
                    ins = three(out, w_hi[:, s, w], w_lo[:, s, w], x_h[:, k0 + k, :], x_l[:, k0 + k, :],
                                k0 + k == 0, last and k == kn - 1)
                ins.then_inc(acc_done if last else unit_used, 1)

            def cols_units(n0, t0, x_h, x_l, tiles, before=None, after=None):
                for q in range(4):
                    n = n0 + q
                    s = n % RING
                    weights_in(n)
                    for kk in range(2):
                        k = 2 * q + kk
                        if before is not None:
                            before(k)
                        w = slice(kk * 512, (kk + 1) * 512)
                        for m in range(tiles):
                            if k == 0:
                                acc_free(t0 + m)
                            tok = slice(m * P, (m + 1) * P)
                            out = accs[(t0 + m) % 4][:, :]
                            pe.matmul(out, x_h[:, k, tok], w_hi[:, s, w], start=(k == 0), stop=False)
                            pe.matmul(out, x_h[:, k, tok], w_lo[:, s, w], start=False, stop=False)
                            ins = pe.matmul(out, x_l[:, k, tok], w_hi[:, s, w], start=False, stop=(k == KT - 1))
                            if k == KT - 1:
                                ins.then_inc(acc_done, 1)
                    if q < 3:
                        ins.then_inc(unit_used, 1)
                    if after is not None:
                        after(q)

            def mean(norm):
                t = aux_at["mean", norm]
                aux_free(pe, t)
                pe.wait_ge(sq_added, 6 * norm)
                pe.wait_ge(sq_ready, 8 * norm)
                for i in range(TT):
                    out, tok = auxs[t % 4][:, i:i + 1], slice(i * P, (i + 1) * P)
                    pe.matmul(out, sqsum[:, tok], mean_w[:, :], start=True, stop=False)
                    ins = pe.matmul(out, tmp[:, 1, tok], mean_w[:, :], start=False, stop=True)
                ins.then_inc(aux_done, 1)

            def row(norm):
                t = aux_at["row", norm]
                aux_free(pe, t)
                pe.wait_ge(diag_ready, norm + 2)
                pe.matmul(auxs[t % 4][:, :], ones[:, :], diag, start=True, stop=True).then_inc(aux_done, 1)

            def stats_after(norm):
                def f(q):
                    if q == 0:
                        mean(norm)
                    if q == 1:
                        row(norm)
                return f

            def u_in(norm):
                return lambda k: pe.wait_ge(u_ready, 8 * norm + k + 1)

            def kv_proj(layer, after=None):
                a0, u0 = KV_ACC[layer], KV_UNIT[layer]
                for j in range(KT):
                    rows_unit(u0 + j, a0 + A_K + j, mem_hi, mem_lo,
                              before=(lambda k: pe.wait_ge(mlo_ready, 8 * layer + k + 1)) if j == 0 else None)
                    if after is not None:
                        after(j)
                for c in range(2):
                    cols_units(u0 + KT + 4 * c, a0 + A_XV + 2 * c, mem_hi, mem_lo, MT)

            pe.wait_ge(mem_in, 16 * 3)
            for t in range(4):
                k = aux_at["mem"] + t
                aux_free(pe, k)
                for e in range(2):
                    for m in range(MT):
                        c = e * M + m * P
                        j = 2 * t + e
                        ins = pe.transpose(auxs[k % 4][:, c:c + P], mem_tok[:, m, j * P:(j + 1) * P], ident[:, :])
                ins.then_inc(aux_done, 1)

            def turn_x(j):
                t = aux_at["x"] + j
                aux_free(pe, t)
                for i in range(TT):
                    ins = pe.transpose(auxs[t % 4][:, i * P:(i + 1) * P], x_tok[:, i, j * P:(j + 1) * P], ident[:, :])
                ins.then_inc(aux_done, 1)

            a0, u0 = KV_ACC[0], KV_UNIT[0]
            for j in range(KT):
                rows_unit(u0 + j, a0 + A_K + j, mem_hi, mem_lo,
                          before=(lambda k: pe.wait_ge(mlo_ready, k + 1)) if j == 0 else None)
                if j == 1:
                    t = aux_at["mem row"]
                    aux_free(pe, t)
                    pe.wait_ge(const_set, 4)
                    pe.wait_ge(diag_ready, 1)
                    pe.matmul(auxs[t % 4][:, 0:M], ones[:, :], diag[:, 0:M], start=True, stop=True)\
                        .then_inc(aux_done, 1)
            pe.wait_ge(x_in, 16 * TT)
            for j in range(4):
                turn_x(j)
            cols_units(u0 + KT, a0 + A_XV, mem_hi, mem_lo, MT)
            for j in range(4, 8):
                turn_x(j)
            cols_units(u0 + KT + 4, a0 + A_XV + 2, mem_hi, mem_lo, MT, after=lambda q: row(0) if q == 1 else None)

            a0, u0 = MIX_ACC[0], MIX_UNIT[0]
            cols_units(u0 + U_V, a0 + A_V, u_hi, u_lo, TT, before=u_in(0))
            for g in range(8):
                rows_unit(u0 + U_A + g, a0 + A_A + g, u_hi, u_lo)
            for g in range(4):
                t = a0 + A_POOL + g
                acc_free(t)
                pe.wait_ge(d_ready, g + 1)
                pe.matmul(accs[t % 4][:, :], pool_w[:, g, :], a_pad[:, g, PAD:PAD + S], start=True, stop=True)\
                    .then_inc(acc_done, 1)
            pe.wait_ge(vn_ready, TT)
            pe.wait_ge(ws_masked, 1)
            for g in range(4):
                t = a0 + A_SGU + g
                acc_free(t)
                for n in range(TT):
                    ins = pe.matmul(accs[t % 4][:, n * P:(n + 1) * P], vn[:, n, g * P:(g + 1) * P], ws_t[:, g, :],
                                    start=True, stop=True)
                ins.then_inc(acc_done, 1)

            def out_unit(u0, t0, j, k0, k1, before=None):
                n, t = u0 + j, t0 + j
                s = n % RING
                if k0 == 0:
                    weights_in(n)
                    acc_free(t)
                for k in range(k0, k1):
                    if before is not None:
                        before(k)
                    w = slice(k * P, (k + 1) * P)
                    ins = three(accs[t % 4][:, :], w_hi[:, s, w], w_lo[:, s, w], y_hi[:, k, :], y_lo[:, k, :],
                                k == 0, k == KT - 1)
                if k1 == KT:
                    ins.then_inc(acc_done, 1)

            def out_proj(u0, t0, y_in, begun):
                for j in range(KT):
                    out_unit(u0, t0, j, KT // 2 if j < begun else 0, KT, before=y_in if j == 0 else None)

            for j in range(3):
                out_unit(u0 + U_OUT0, a0 + A_OUT0, j, 0, KT // 2,
                         before=(lambda k: pe.wait_ge(acc_drained, a0 + A_POOL + k + 1)) if j == 0 else None)
            out_proj(u0 + U_OUT0, a0 + A_OUT0, lambda k: pe.wait_ge(y_ready, k - 3), begun=3)

            def cross_attention(layer):
                norm = 3 * layer + 1
                a0, u0 = X_ACC[layer], X_UNIT[layer]
                if layer:
                    kv_proj(1, after=stats_after(norm))

                def scores(h):
                    for c in range(2):
                        t = aux_at["xs", layer, h] + c
                        aux_free(pe, t)
                        for e in range(2):
                            i = 2 * c + e
                            for k in range(2):
                                ins = pe.matmul(auxs[t % 4][:, e * M:(e + 1) * M],
                                                xq[:, 2 * h + k, i * P:(i + 1) * P], xk[:, 2 * h + k, :],
                                                start=(k == 0), stop=(k == 1))
                        ins.then_inc(aux_done, 1)

                def turn(h):
                    pe.wait_ge(p_ready, (X_H + DIL_H) * layer + h + 1)
                    for k in range(MT):
                        t = aux_at["xt", layer, h] + k
                        aux_free(pe, t)
                        for i in range(TT):
                            ins = pe.transpose(auxs[t % 4][:, i * P:(i + 1) * P], xp[:, h % 2, i, k * P:(k + 1) * P],
                                               ident[:, :])
                        ins.then_inc(aux_done, 1)

                def values(h):
                    pe.wait_ge(aux_free_a, freed_a(aux_at["xt", layer, h] + 1))
                    for e in range(2):
                        t = a0 + A_XO + 2 * h + e
                        acc_free(t)
                        for k in range(MT):
                            ins = pe.matmul(accs[t % 4][:, :], xv[:, k, (2 * h + e) * P:(2 * h + e + 1) * P],
                                            xpt[:, k, :], start=(k == 0), stop=(k == MT - 1))
                        ins.then_inc(acc_done, 1)

                for j in range(KT):
                    rows_unit(u0 + j, a0 + A_Q + j, u_hi, u_lo, before=u_in(norm) if j == 0 else None)
                    if not layer:
                        stats_after(norm)(j)
                    if j in (3, 5):
                        pe.wait_ge(acc_drained, a0 + A_Q + j - 1)
                        scores((j - 3) // 2)
                pe.wait_ge(acc_drained, a0 + A_Q + KT)
                order_x(scores, turn, values)
                for j in range(KT):
                    rows_unit(u0 + KT + j, a0 + A_O + j, y_hi, y_lo,
                              before=(lambda k: pe.wait_ge(acc_drained, a0 + A_XO + k + 1)) if j == 0 else None)

            def turn_out(j):
                k = aux_at["out"] + j
                aux_free(pe, k)
                pe.wait_ge(acc_drained, F_ACC[1] + A_DN + j + 1)
                for t in range(TT):
                    ins = pe.transpose(auxs[k % 4][:, t * P:(t + 1) * P], hT[:, j, t * P:(t + 1) * P], ident[:, :])
                ins.then_inc(aux_done, 1)

            def ffn(layer):
                norm = 3 * layer + 2
                u0, a0 = F_UNIT[layer], F_ACC[layer]

                def group(g, i=None):
                    for e in range(4):
                        rows_unit(u0 + 4 * g + e, a0 + 4 * g + e, u_hi, u_lo, i,
                                  before=u_in(norm) if g == 0 and e == 0 else None)
                        if g == 0:
                            stats_after(norm)(e)

                group(0)
                group(1)
                with pe.Fori(0, FT // 2 - 2) as i:
                    group(2, i)
                for j in range(KT):
                    for e, kn in enumerate((8, 8, 6)):
                        rows_unit(u0 + F_DN + 3 * j + e, a0 + A_DN + j, act_hi, act_lo, k0=8 * e, kn=kn,
                                  last=(e == 2),
                                  before=(lambda k: pe.wait_ge(act_ready, FT * layer + k + 1)) if j == 0 else None)
                    if layer == LAYERS - 1 and j:
                        turn_out(j - 1)

            def odd_mixer():
                a0, u0 = MIX_ACC[1], MIX_UNIT[1]

                cols_units(u0 + U_DV, a0 + B_V, u_hi, u_lo, TT, before=u_in(3), after=stats_after(3))
                for j in range(8):
                    rows_unit(u0 + U_DQK + j, a0 + B_QK + j, u_hi, u_lo)

                def scores(h):
                    q0 = DH * (h % 2)
                    pe.wait_ge(rot_ready, 5 + h // 2)
                    for i in range(TT):
                        t = aux_at["ds", h] + i
                        aux_free(pe, t)
                        pe.matmul(auxs[t % 4][:, 0:(i + 1) * P], tq_d[q0:q0 + DH, h // 2, i * P:(i + 1) * P],
                                  tk_d[q0:q0 + DH, h // 2, 0:(i + 1) * P], start=True, stop=True)\
                            .then_inc(aux_done, 1)

                def turn(h):
                    pe.wait_ge(p_ready, X_H + h + 1)
                    for e, kts in enumerate(((0,), (1, 3), (2,))):
                        t = aux_at["dt", h] + e
                        aux_free(pe, t)
                        for kt in kts:
                            c = 384 if kt == 3 else 0
                            for i in range(kt, TT):
                                o = ROWS[i][0] + kt * P
                                ins = pe.transpose(auxs[t % 4][:, c + (i - kt) * P:c + (i - kt + 1) * P],
                                                   dp[:, h % 2, o:o + P], ident[:, :])
                        ins.then_inc(aux_done, 1)

                def values(h):
                    t = a0 + B_D + 4 * (h // 2) + 2
                    q0 = DH * (h % 2)
                    if h % 2 == 0:
                        acc_free(t)
                    pe.wait_ge(aux_free_a, freed_a(aux_at["dt", h] + 2))
                    for kt in range(TT):
                        o, w = BLOCK[kt]
                        ins = pe.matmul(accs[t % 4][q0:q0 + DH, kt * P:S], tv_d[:, kt, h * DH:(h + 1) * DH],
                                        dpt[:, o:o + w], start=(kt == 0), stop=(kt == TT - 1))
                    if h % 2:
                        ins.then_inc(acc_done, 1)

                def ret_scores(h):
                    for e, kts in enumerate(((0,), (1, 3), (2,))):
                        t = aux_at["rs", h] + e
                        aux_free(pe, t)
                        for kt in kts:
                            c, w = (384 if kt == 3 else 0), BLOCK[kt][1]
                            ins = pe.matmul(auxs[t % 4][:, c:c + w], tq[:, 4 + h, kt * P:(kt + 1) * P],
                                            tq[:, h, kt * P:S], start=True, stop=True)
                        ins.then_inc(aux_done, 1)

                def side(place):
                    r, c = place
                    rows_unit(u0 + U_RQK + r, a0 + B_D + c, u_hi, u_lo)

                cols_units(u0 + U_RV, a0 + B_RV, u_hi, u_lo, TT,
                           after=lambda q: scores(q // 2) if q % 2 == 0 else None)
                for h in range(DIL_H):
                    turn(h)
                    first, second = side_units(h)
                    side(first)
                    if h + 2 < DIL_H:
                        scores(h + 2)
                    values(h)
                    if h == DIL_H - 1:
                        pe.wait_ge(rot_ready, 16)
                        ret_scores(0)
                    if second:
                        side(second)

                def ret_values(h):
                    t = a0 + B_R + h
                    acc_free(t)
                    pe.wait_ge(aux_free_v, freed_v(aux_at["rs", h] + 2))
                    for i in range(TT):
                        for kt in range(i + 1):
                            o = BLOCK[kt][0] + (i - kt) * P
                            ins = pe.matmul(accs[t % 4][:, i * P:(i + 1) * P], inner[:, h % 2, o:o + P],
                                            tv[:, kt, h * P:(h + 1) * P], start=(kt == 0), stop=(kt == i))
                    ins.then_inc(acc_done, 1)

                def ret_turn(h):
                    t = aux_at["rt", h]
                    aux_free(pe, t)
                    pe.wait_ge(acc_drained, a0 + B_R + h + 1)
                    for i in range(TT):
                        ins = pe.transpose(auxs[t % 4][:, i * P:(i + 1) * P], tmp[:, h % 2, i * P:(i + 1) * P],
                                           ident[:, :])
                    ins.then_inc(aux_done, 1)

                def start_out(j):
                    out_unit(u0 + U_OUT1, a0 + B_OUT1, j, 0, KT // 2)

                def turn_and_start(h):
                    if h == 2:
                        start_out(1)
                    ret_turn(h)
                    if h in (1, 2):
                        start_out({1: 0, 2: 2}[h])

                order_ret(ret_scores, ret_values, turn_and_start)
                out_proj(u0 + U_OUT1, a0 + B_OUT1, lambda k: pe.wait_ge(y_ready, 4 + k - 3), begun=3)

            cross_attention(0)
            ffn(0)
            odd_mixer()
            cross_attention(1)
            ffn(1)
            turn_out(KT - 1)
            mean(6)


def rotary_tables(dims, half, theta, order):
    inv = (1.0 / np.power(np.float32(theta), np.arange(half, dtype=np.float32) / np.float32(half))).astype(np.float32)
    ang = (np.arange(S, dtype=np.float32)[:, None] * inv[None, :]).astype(np.float32).astype(np.float64)
    cs = np.zeros((dims, 2, S))
    cs[:, 0] = 1.0
    for f in range(2 * half):
        cs[f, 0], cs[f, 1] = np.cos(ang[:, f % half]), np.sin(ang[:, f % half]) * (-1.0 if f < half else 1.0)
    return cs[order].astype(np.float32)


DIL_ORDER = np.concatenate([np.arange(0, 8), np.arange(16, 40), np.arange(8, 16), np.arange(40, DH)])


def constants():
    cs64 = rotary_tables(DH, 8, 500000.0, DIL_ORDER)
    cs_r = rotary_tables(P, 64, 10000.0, np.arange(P))
    dist = np.arange(P)[:, None] - np.arange(S)[None, :] + (S - P)
    past = dist >= 0
    count = (past & (dist <= 128)).astype(int) + (past & (dist % 4 == 0)) + (past & (dist % 16 == 0))
    band = np.where(count > 0, np.log(np.maximum(count, 1)), NEG).astype(np.float32)
    rel = np.arange(S)[None, :] - np.arange(P)[:, None]
    decay = np.stack([np.where(rel >= 0, (1 - 2.0 ** (-5 - h)) ** np.maximum(rel, 0), 0.0) * P ** -0.5
                      for h in range(RET_H)], axis=1).astype(np.float32)
    inv = np.stack([1.0 / np.minimum(np.arange(PAD) + 1, w) for w in WINDOWS]).astype(np.float32)
    return {
        "ident": np.eye(P, dtype=np.float32),
        "cs_d": np.ascontiguousarray(np.concatenate([cs64, cs64])),
        "cs_r": cs_r,
        "band": band,
        "decay": np.ascontiguousarray(decay),
        "invcnt": np.ascontiguousarray(np.broadcast_to(inv.reshape(1, -1), (P, 4 * PAD))),
    }


def weight_units(w):
    def rows(a):
        k, m = a.shape[0] // P, a.shape[1] // P
        return a.reshape(k, P, m, P).transpose(2, 1, 0, 3).reshape(m, P, k * P)

    def cols(a):
        c = a.shape[1] // 512
        return a.reshape(4, 2, P, c, 512).transpose(3, 0, 2, 1, 4).reshape(4 * c, P, UW)

    out = np.zeros((UNITS, P, UW), np.float32)
    n = [0]

    def put(u):
        out[n[0]:n[0] + len(u), :, 0:u.shape[2]] = u
        n[0] += len(u)

    even, odd = w["even_w_in"][0], w["odd_w_in"][0]
    def put_kv(layer):
        put(rows(w["xattn_wkv"][layer][:, 0:D]))
        put(cols(w["xattn_wkv"][layer][:, D:]))

    for layer in range(LAYERS):
        if layer == 0:
            put_kv(0)
            put(cols(even[:, 1024:1536]))
            put(rows(even[:, 0:1024]))
            put(rows(w["even_w_out"][0]))
        else:
            put(cols(odd[:, 1024:1536]))
            put(rows(odd[:, 0:1024].reshape(D, -1, DH)[:, :, DIL_ORDER].reshape(D, 1024)))
            put(cols(odd[:, 2560:3072]))
            put(rows(odd[:, 1536:2560]))
            put(rows(odd[:, 3072:3584]))
            put(rows(w["odd_w_out"][0]))
            put_kv(1)
        put(rows(w["xattn_wq"][layer]))
        put(rows(w["xattn_wo"][layer]))
        gu = rows(w["ffn_w_gate_up"][layer])
        put(gu.reshape(2, FT, P, UW).transpose(1, 0, 2, 3).reshape(2 * FT, P, UW))
        down = rows(w["ffn_w_down"][layer])
        for j in range(KT):
            for e in range(3):
                put(down[j:j + 1, :, e * UW:min((e + 1) * UW, DFF)])
    assert n[0] == UNITS
    return out


def kernel(**inputs):
    import concourse.bacc as bacc
    from concourse.bass_utils import run_bass_kernel_spmd

    w = {k: np.asarray(v) for k, v in inputs.items()}

    def columns(v):
        return v.reshape(-1, P).T

    arrays = dict(constants())
    arrays["x"] = np.ascontiguousarray(w["x"])
    arrays["mem"] = np.ascontiguousarray(w["mem"])
    arrays["weights"] = weight_units(w)
    arrays["vecs"] = np.ascontiguousarray(np.concatenate(
        [columns(w[k]) for k in ("even_mix_norm", "odd_mix_norm", "xattn_norm", "ffn_norm", "mem_norm", "pool_scale")],
        axis=1))
    arrays["ws_t"] = np.ascontiguousarray(w["sgu_w"][0].transpose(2, 0, 1))
    arrays["pool_w"] = np.ascontiguousarray(w["pool_w"][0].transpose(1, 0, 2))
    arrays["sgu_b"] = np.ascontiguousarray(np.broadcast_to(w["sgu_b"][0].reshape(1, -1), (P, 4 * P)))
    arrays["sgu_g"] = np.ascontiguousarray(np.broadcast_to(w["sgu_norm"][0][None], (P, S)))
    arrays["final_g"] = np.ascontiguousarray(np.broadcast_to(w["final_norm"][None], (P, D)))

    nc = bacc.Bacc("TRN2", target_bir_lowering=False, num_devices=1)
    named = {f"in_{k}": a for k, a in arrays.items()}
    d = {k: nc.dram_tensor(f"in_{k}", a.shape, F32, kind="ExternalInput").ap() for k, a in arrays.items()}
    d["out"] = nc.dram_tensor("out_h", (1, S, D), F32, kind="ExternalOutput").ap()
    program(nc, d)
    r = run_bass_kernel_spmd(nc, [named], core_ids=[0])
    return r.results[0]["out_h"]
```

```python
from contextlib import ExitStack

import numpy as np

import concourse.bass as bass
from concourse import mybir

F32 = mybir.dt.float32
F32R = mybir.dt.float32r
ACT = mybir.ActivationFunctionType
ALU = mybir.AluOpType
AX = mybir.AxisListType

P = 128
D = 1024
S = 512
M = 256
KT = D // P
TT = S // P
MT = M // P
DFF = 2816
FT = DFF // P
EPS = 1e-6
LAYERS = 2
RING = 4
LEAD = 3
UW = 1024
WINDOWS = (2, 4, 8, 16)
PAD = 16
DIL_H, RET_H, X_H = 8, 4, 4
DH = 64
NEG = -1e30

U_V, U_A, U_OUT0, U_MIX0 = 0, 4, 12, 20
U_DV, U_DQK, U_RV, U_RQK, U_RG, U_OUT1, U_MIX1 = 0, 4, 12, 16, 24, 28, 36
U_KV = 2 * KT
U_X = 2 * KT
F_DN, F_END = 2 * FT, 2 * FT + 3 * KT
KV_UNIT = (0, U_KV + U_MIX0 + U_X + F_END + U_MIX1)
MIX_UNIT = (U_KV, KV_UNIT[1] - U_MIX1)
X_UNIT = (U_KV + U_MIX0, KV_UNIT[1] + U_KV)
F_UNIT = tuple(u + U_X for u in X_UNIT)
UNITS = F_UNIT[1] + F_END

A_V, A_A, A_U, A_POOL, A_SGU, A_OUT0, A_MIX0 = 0, 4, 8, 12, 16, 20, 28
B_V, B_QK, B_RV, B_D, B_R, B_OUT1, B_MIX1 = 0, 4, 12, 16, 32, 36, 44
A_K, A_XV, A_KV = 0, 8, 12
A_Q, A_XO, A_O, A_X = 0, 8, 16, 24
A_DN, A_F = 2 * FT, 2 * FT + KT
KV_ACC = (0, A_KV + A_MIX0 + A_X + A_F + B_MIX1)
MIX_ACC = (A_KV, KV_ACC[1] - B_MIX1)
X_ACC = (A_KV + A_MIX0, KV_ACC[1] + A_KV)
F_ACC = tuple(a + A_X for a in X_ACC)

C_EVEN, C_ODD, C_XN, C_FN, C_MN, C_PS, C_ALL = 0, 8, 16, 32, 48, 64, 68

X_ORDER = (("xs", 0), ("xs", 1), ("xt", 0), ("xs", 2), ("xt", 1), ("xs", 3), ("xt", 2), ("xt", 3))


def aux_plan():
    who, at = [], {}

    def add(name, s):
        at[name] = len(who)
        who.extend(s)

    add("mem", "vvvv")
    add("mem row", "v")
    add("x", "a" * 8)
    add(("row", 0), "v")
    for layer in range(LAYERS):
        if layer:
            add(("mean", 3), "v")
            add(("row", 3), "v")
            add(("ds", 0), "vvvv")
            add(("ds", 1), "vvvv")
            for h in range(DIL_H):
                add(("dt", h), "aaa")
                if h + 2 < DIL_H:
                    add(("ds", h + 2), "vvvv")
            add(("rs", 0), "vvv")
            order_ret(lambda h: add(("rs", h), "vvv"), lambda h: None, lambda h: add(("rt", h), "v"))
        add(("mean", 3 * layer + 1), "v")
        add(("row", 3 * layer + 1), "v")
        for name, h in X_ORDER:
            add((name, layer, h), "aa" if name == "xs" else "vv")
        add(("mean", 3 * layer + 2), "v")
        add(("row", 3 * layer + 2), "v")
    add("out", "v" * 8)
    add(("mean", 6), "v")
    return who, at


def order_ret(scores, values, turn):
    for h in range(RET_H):
        if h + 1 < RET_H:
            scores(h + 1)
        values(h)
        if h:
            turn(h - 1)
    turn(RET_H - 1)


def side_units(h):
    p = h // 2
    if h % 2 == 0:
        return (3 * p, 4 * p), None
    return (3 * p + 1, 4 * p + 1), (3 * p + 2, 4 * p + 3)


BLOCK = {0: (0, 512), 1: (512, 384), 3: (896, 128), 2: (1024, 256)}
ROWS = {0: (0, 128), 1: (128, 256), 2: (384, 384), 3: (768, 512)}


def program(nc, d):
    who, aux_at = aux_plan()

    with ExitStack() as ctx:
        def sem(name):
            return ctx.enter_context(nc.semaphore(name))

        def fixed(name, shape, dt=F32):
            return ctx.enter_context(nc.sbuf_tensor(name, shape, dt))

        base = (nc.sbuf_base + 31) // 32 * 32
        fixed("arena", [P, 120 * 256])

        def at(name, kib, shape, dt=F32):
            return nc.alloc_sbuf_tensor_at(name, shape, dt, offset=int(base + kib * 1024))

        act_hi = at("act_hi", 0, [P, FT, S], F32R)
        act_lo = at("act_lo", 44, [P, FT, S], F32R)
        y_hi = at("y_hi", 0, [P, KT, S], F32R)
        y_lo = at("y_lo", 16, [P, KT, S], F32R)
        x_tok = at("x_tok", 0, [P, TT, D])
        mem_tok = at("mem_tok", 56, [P, MT, D])
        wsum = at("wsum", 8, [P, 3, PAD + S])
        a_pad = at("a_pad", 23.75, [P, 4, PAD + S])
        vn = at("vn", 32, [P, TT, S])
        uu = at("uu", 40, [P, 4, S])
        ws_t = at("ws_t", 80, [P, 4, P])
        pool_w = at("pool_w", 82, [P, 4, P])
        sgu_b = at("sgu_b", 84, [P, 4, P])
        sgu_g = at("sgu_g", 86, [P, S])
        mem_hi = at("mem_hi", 32, [P, KT, M], F32R)
        mem_lo = at("mem_lo", 40, [P, KT, M], F32R)
        xq = at("xq", 16, [P, KT, S])
        xk = at("xk", 56, [P, KT, M])
        xk_hi = at("xk_hi", 48, [P, KT, M], F32R)
        xk_lo = at("xk_lo", 56, [P, KT, M], F32R)
        xv = at("xv", 72, [P, MT, D])
        xv_hi = at("xv_hi", 64, [P, MT, D], F32R)
        xv_lo = at("xv_lo", 72, [P, MT, D], F32R)
        xp = at("xp", 80, [P, 2, TT, M])
        xpt_hi = at("xpt_hi", 32, [P, 2, MT, S], F32R)
        xpt_lo = at("xpt_lo", 40, [P, 2, MT, S], F32R)
        tq_d = at("tq_d", 8, [P, 4, S])
        tk_d = at("tk_d", 24, [P, 4, S])
        gate = at("gate", 8, [P, 4, S])
        cs_r = at("cs_r", 32, [P, 2, S])
        decay012 = at("decay012", 32, [P, 3, S])
        band = at("band", 38, [P, S])
        tv_d = at("tv_d", 40, [P, TT, S])
        tq = at("tq", 48, [P, 8, S])
        tv = at("tv", 64, [P, TT, S])
        cs_d = at("cs_d", 72, [P, 2, S])
        dp = at("dp", 72, [P, 2, 1280])
        inner = at("inner", 72, [P, 2, 1280])
        dpt = at("dpt", 82, [P, 1280])
        u_hi = at("u_hi", 88, [P, KT, S], F32R)
        u_lo = at("u_lo", 104, [P, KT, S], F32R)
        y_tok = at("y_tok", 88, [P, TT, D])

        hT = fixed("hT", [P, KT, S])
        raw = fixed("raw", [P, RING, UW])
        w_hi = fixed("w_hi", [P, RING, UW], F32R)
        w_lo = fixed("w_lo", [P, RING, UW], F32R)
        memT = fixed("memT", [P, KT, M])
        tmp = fixed("tmp", [P, 4, S])
        junk = tmp[:, 0:2, :].rearrange("p a b -> p (a b)")
        fin_g = memT[:, 0:KT // 2, :].rearrange("p a b -> p (a b)")
        sqsum = fixed("sqsum", [P, S])
        rstd_row = fixed("rstd_row", [P, S])
        rstd_mrow = fixed("rstd_mrow", [P, M])
        ident = fixed("ident", [P, P])
        vecs = fixed("vecs", [P, C_ALL])
        invcnt = fixed("invcnt", [P, 4, PAD])
        mean_w = fixed("mean_w", [P, 1])
        mexp = fixed("mexp", [P, TT])
        ssq = fixed("ssq", [P, TT])
        ssq_m = fixed("ssq_m", [P, MT])
        ssq_v = fixed("ssq_v", [P, TT])
        var_e = fixed("var_e", [P, TT])
        var_m = fixed("var_m", [P, MT])
        var_v = fixed("var_v", [P, TT])
        rstd_tok = fixed("rstd_tok", [P, TT])
        rstd_m = fixed("rstd_m", [P, MT])
        rstd_v = fixed("rstd_v", [P, TT])
        nmax = fixed("nmax", [P, 2, TT])
        psums = fixed("psums", [P, 2, TT])
        pinv = fixed("pinv", [P, 2, TT])
        stats = fixed("stats", [P, TT, 6])
        mv = fixed("mv", [P, TT, 2])
        rvar = fixed("rvar", [P, 2, TT])
        rrstd = fixed("rrstd", [P, 2, TT])

        accs = [ctx.enter_context(nc.psum_tensor(f"acc{i}", [P, 512], F32)) for i in range(4)]
        auxs = [ctx.enter_context(nc.psum_tensor(f"aux{i}", [P, 512], F32)) for i in range(4)]

        raw_in = [sem(f"raw_in{i}") for i in range(RING)]
        hi_ready = sem("hi_ready")
        lo_ready = sem("lo_ready")
        unit_used = sem("unit_used")
        acc_done = sem("acc_done")
        acc_drained = sem("acc_drained")
        aux_done = sem("aux_done")
        aux_free_v = sem("aux_free_v")
        aux_free_a = sem("aux_free_a")
        mem_in = [sem(f"mem_in{q}") for q in range(4)]
        ident_in = sem("ident_in")
        vecs_in = sem("vecs_in")
        x_in = sem("x_in")
        c0_in = sem("c0_in")
        c1_in = sem("c1_in")
        c2_in = sem("c2_in")
        fin_in = sem("fin_in")
        const_set = sem("const_set")
        ws_masked = sem("ws_masked")
        x_sq = sem("x_sq")
        sq_ready = sem("sq_ready")
        sq_added = sem("sq_added")
        uhi_ready = sem("uhi_ready")
        u_ready = sem("u_ready")
        var_ready = sem("var_ready")
        rstd_ready = sem("rstd_ready")
        kvhi_ready = sem("kvhi_ready")
        kvlo_ready = sem("kvlo_ready")
        qhi_ready = sem("qhi_ready")
        qlo_ready = sem("qlo_ready")
        pthi_ready = sem("pthi_ready")
        mhi_ready = sem("mhi_ready")
        mlo_ready = sem("mlo_ready")
        part_hi = sem("part_hi")
        vgelu = sem("vgelu")
        vsq = sem("vsq")
        vn_ready = sem("vn_ready")
        ugelu = sem("ugelu")
        win_ready = sem("win_ready")
        win_step = sem("win_step")
        d_ready = sem("d_ready")
        silu_ready = sem("silu_ready")
        prod_ready = sem("prod_ready")
        ahi_ready = sem("ahi_ready")
        act_ready = sem("act_ready")
        shifted = sem("shifted")
        rot_half = sem("rot_half")
        rot_ready = sem("rot_ready")
        dve_step = sem("dve_step")
        max_ready = sem("max_ready")
        exp_ready = sem("exp_ready")
        p_ready = sem("p_ready")
        rvar_ready = sem("rvar_ready")
        rrstd_ready = sem("rrstd_ready")
        y_full = sem("y_full")
        y_ready = sem("y_ready")
        out_ready_v = sem("out_ready_v")
        out_ready_a = sem("out_ready_a")
        out_in = sem("out_in")

        def lin(c, i, k):
            return c if i is None else i * k + c

        def aux_free(eng, t):
            if t >= 4:
                w = who[t - 4]
                eng.wait_ge(aux_free_v if w == "v" else aux_free_a, who[:t - 3].count(w))

        def slot_free(eng, n, i=None):
            ends, count = used[n]
            eng.wait_ge(acc_done if ends else unit_used, lin(count, i, RING))

        PHX, PHM1 = (8, 24), 16
        XMAX, DMAX = (0, 2 * X_H + TT * DIL_H), 2 * X_H
        SILU = (0, FT + RET_H)
        ROUND = {0: 1, 1: 3, 2: 4, 3: 5, 4: 6, 5: 7, 6: 8}

        def kv_split_due(n):
            return {**{j + 1: (j,) for j in range(KT)}, 12: (8, 9), 16: (10, 11)}.get(n, ())

        def kv_tile(j, k, v):
            if j < KT:
                return k[:, j, :]
            c, m = (j - KT) // MT, (j - KT) % MT
            return v[:, m, c * S:(c + 1) * S]

        def freed_v(t):
            return who[:t + 1].count("v")

        def freed_a(t):
            return who[:t + 1].count("a")

        def decay(h):
            return decay012[:, h, :] if h < 3 else sqsum[:, :]

        used, mid = [], [0]

        def rows_used(t, tiles, per=1):
            for j in range(tiles):
                for e in range(per):
                    mid[0] += e < per - 1
                    used.append((e == per - 1, t + j + 1 if e == per - 1 else mid[0]))

        def cols_used(t, tiles):
            for q in range(4):
                mid[0] += q < 3
                used.append((q == 3, t + tiles if q == 3 else mid[0]))

        def kv_used(a):
            rows_used(a + A_K, KT)
            cols_used(a + A_XV, MT)
            cols_used(a + A_XV + MT, MT)

        for layer in range(LAYERS):
            a = MIX_ACC[layer]
            if layer == 0:
                kv_used(KV_ACC[0])
                cols_used(a + A_V, TT)
                rows_used(a + A_A, 8)
                rows_used(a + A_OUT0, KT)
            else:
                cols_used(a + B_V, TT)
                rows_used(a + B_QK, 8)
                cols_used(a + B_RV, TT)
                for h in range(DIL_H):
                    for r in side_units(h):
                        if r is not None:
                            used.append((True, a + B_D + r[1] + 1))
                rows_used(a + B_OUT1, KT)
                kv_used(KV_ACC[1])
            rows_used(X_ACC[layer] + A_Q, KT)
            rows_used(X_ACC[layer] + A_O, KT)
            rows_used(F_ACC[layer], 2 * FT)
            rows_used(F_ACC[layer] + A_DN, KT, 3)
        assert len(used) == UNITS

        mem_rows = d["mem"].rearrange("a (t p) n -> p (a t) n", p=P)
        block = ctx.enter_context(nc.Block())

        @block.sync
        def _(sp):
            for q in (0, 2):
                sp.dma_start(mem_tok[:, :, q * 256:(q + 1) * 256], mem_rows[:, :, q * 256:(q + 1) * 256])\
                    .then_inc(mem_in[q], 16)
            for j in range(RING):
                if j == 1:
                    for q in range(4):
                        sp.wait_ge(mem_in[q], 16)
                sp.dma_start(raw[:, j, :], d["weights"][j]).then_inc(raw_in[j], 16)
            with sp.Fori(1, UNITS // RING) as i:
                for j in range(RING):
                    sp.wait_ge(lo_ready, i * RING + (j - RING + 1))
                    sp.dma_start(raw[:, j, :], d["weights"][bass.ds(i * RING + j, 1)].rearrange("a p n -> p (a n)"))\
                        .then_inc(raw_in[j], 16)
            for t in range(TT):
                sp.wait_ge(out_ready_a if t % 2 else out_ready_v, t // 2 + 1)
                sp.dma_start(d["out"][0, t * P:(t + 1) * P, :], y_tok[:, t, :]).then_inc(out_in, 16)
            sp.wait_ge(out_in, 16 * TT)

        @block.scalar
        def _(act):
            def split(n, i=None):
                if n >= UNITS:
                    return
                s = n % RING
                act.wait_ge(raw_in[s], lin(16 * (n // RING + 1), i, 16))
                if n >= RING:
                    slot_free(act, n - RING, i)
                act.activation(w_hi[:, s, :], raw[:, s, :], ACT.Copy).then_inc(hi_ready, 1)

            def residual(norm, j, gcol, t):
                act.wait_ge(acc_drained, t + 1)
                dst = sqsum[:, :] if j == 0 else tmp[:, j % 2, :]
                if j >= 3:
                    act.wait_ge(sq_added, (KT - 1) * (norm - 1) + j - 2)
                act.activation(dst, hT[:, j, :], ACT.Square).then_inc(sq_ready, 1)
                if gcol is not None:
                    act.activation(u_hi[:, j, :], hT[:, j, :], ACT.Copy, scale=vecs[:, gcol + j:gcol + j + 1])\
                        .then_inc(uhi_ready, 1)

            def mem_hi_part(layer, j):
                act.wait_ge(aux_free_v, freed_v(aux_at["mem"] + j // 2))
                act.activation(mem_hi[:, j, :], memT[:, j, :], ACT.Copy,
                               scale=vecs[:, C_MN + 8 * layer + j:C_MN + 8 * layer + j + 1]).then_inc(mhi_ready, 1)

            def kv_hi_parts(layer, n):
                for j in kv_split_due(n):
                    act.wait_ge(acc_drained, KV_ACC[layer] + j + 1)
                    act.activation(kv_tile(j, xk_hi, xv_hi), kv_tile(j, xk, xv), ACT.Copy).then_inc(kvhi_ready, 1)

            def y_hi_part(j, src, scale=1.0):
                act.activation(y_hi[:, j, :], src, ACT.Copy, scale=scale).then_inc(part_hi, 1)

            act.dma_start(ident[:, :], d["ident"]).then_inc(ident_in, 16)
            act.dma_start(vecs[:, :], d["vecs"]).then_inc(vecs_in, 16)
            for q in (1, 3):
                act.dma_start(mem_tok[:, :, q * 256:(q + 1) * 256], mem_rows[:, :, q * 256:(q + 1) * 256])\
                    .then_inc(mem_in[q], 16)
            act.wait_ge(vecs_in, 16)
            for j in range(KT):
                if j == 2:
                    split(0)
                mem_hi_part(0, j)
            for n in range(1, LEAD):
                split(n)
            for t in range(MT):
                if t:
                    act.wait_ge(x_sq, t)
                act.activation(junk, mem_tok[:, t, :], ACT.Square, accum_out=ssq_m[:, t:t + 1]).then_inc(x_sq, 1)
            for t in range(TT):
                act.dma_start(x_tok[:, t, :], d["x"][0, t * P:(t + 1) * P, :]).then_inc(x_in, 16)
            for j in range(KT):
                split(j + LEAD)
                if j == 2:
                    kv_hi_parts(0, 1)
                if j >= 2:
                    kv_hi_parts(0, j)
                t = j - (KT - TT)
                if t >= 0:
                    act.wait_ge(x_in, 16 * TT)
                    act.wait_ge(x_sq, MT + t)
                    act.activation(junk, x_tok[:, t, :], ACT.Square, accum_out=ssq[:, t:t + 1]).then_inc(x_sq, 1)
            act.dma_start(sgu_g[:, :], d["sgu_g"]).then_inc(c0_in, 16)
            act.dma_start(sgu_b[:, :, :], d["sgu_b"].rearrange("p (g t) -> p g t", g=4)).then_inc(c0_in, 16)
            act.dma_start(ws_t[:, :, :], d["ws_t"]).then_inc(c0_in, 16)
            act.dma_start(pool_w[:, :, :], d["pool_w"]).then_inc(c0_in, 16)
            act.dma_start(invcnt[:, :, :], d["invcnt"].rearrange("p (g t) -> p g t", g=4)).then_inc(c0_in, 16)
            for j in range(KT):
                split(KT + j + LEAD)
                kv_hi_parts(0, KT + j)
                t = aux_at["x"] + j
                act.wait_ge(aux_done, t + 1)
                act.activation(hT[:, j, :], auxs[t % 4][:, :], ACT.Copy).then_inc(aux_free_a, 1)
                act.wait_ge(aux_free_a, freed_a(t))
                act.activation(u_hi[:, j, :], hT[:, j, :], ACT.Copy, scale=vecs[:, C_EVEN + j:C_EVEN + j + 1])\
                    .then_inc(uhi_ready, 1)
            kv_hi_parts(0, U_KV)

            a0, u0 = MIX_ACC[0], MIX_UNIT[0]
            for n in range(4):
                split(u0 + n + LEAD)
            for t in range(TT):
                act.wait_ge(acc_drained, a0 + A_V + t + 1)
                act.activation(vn[:, t, :], vn[:, t, :], ACT.Gelu_apprx_tanh).then_inc(vgelu, 1)
                act.wait_ge(vgelu, t + 1)
                if t == 0:
                    act.wait_ge(x_sq, TT + MT)
                else:
                    act.wait_ge(vsq, t)
                act.activation(junk[:, 0:S], vn[:, t, :], ACT.Square, accum_out=ssq_v[:, t:t + 1]).then_inc(vsq, 1)
                split(u0 + t + 4 + LEAD)
            for g in range(4):
                split(u0 + g + 8 + LEAD)
                act.wait_ge(acc_drained, a0 + A_U + g + 1)
                act.activation(uu[:, g, :], uu[:, g, :], ACT.Gelu_apprx_tanh).then_inc(ugelu, 1)
            for g in range(4):
                act.wait_ge(acc_done, a0 + A_POOL + g + 1)
                y_hi_part(g, accs[(a0 + A_POOL + g) % 4][:, :], scale=vecs[:, C_PS + g:C_PS + g + 1])
            for g in range(4):
                act.wait_ge(y_full, g + 1)
                y_hi_part(4 + g, tmp[:, g % 2, :])

            def out_phase(layer, norm, u0, a0, gcol, with_mem=False):
                for j in range(KT):
                    split(u0 + j + LEAD)
                    residual(norm, j, gcol, a0 + j)
                    if with_mem and j < KT // 2:
                        mem_hi_part(layer, 2 * j)
                        mem_hi_part(layer, 2 * j + 1)

            def cross_attention(layer):
                a0, u0 = X_ACC[layer], X_UNIT[layer]

                def exps(h):
                    for q in range(TT):
                        act.wait_ge(max_ready, XMAX[layer] + 2 * h + q // 2 + 1)
                        t = aux_at["xs", layer, h] + q // 2
                        ins = act.activation(xp[:, h % 2, q, :], auxs[t % 4][:, (q % 2) * M:(q % 2 + 1) * M], ACT.Exp,
                                             bias=nmax[:, h % 2, q:q + 1], accum_out=psums[:, h % 2, q:q + 1])
                        if q % 2:
                            ins.then_inc(aux_free_a, 1)

                def turned(h):
                    for k in range(MT):
                        t = aux_at["xt", layer, h] + k
                        act.wait_ge(aux_done, t + 1)
                        act.activation(xpt_hi[:, h % 2, k, :], auxs[t % 4][:, :], ACT.Copy).then_inc(pthi_ready, 1)

                def parts(h):
                    for e in range(2):
                        t = a0 + A_XO + 2 * h + e
                        act.wait_ge(acc_done, t + 1)
                        y_hi_part(2 * h + e, accs[t % 4][:, :])

                def q_hi_part(j):
                    act.wait_ge(acc_drained, a0 + A_Q + j + 1)
                    act.activation(y_hi[:, j, :], xq[:, j, :], ACT.Copy).then_inc(qhi_ready, 1)

                for j in range(KT):
                    if j >= 2:
                        q_hi_part(j - 1)
                    split(u0 + j + LEAD)
                    if j == 1:
                        q_hi_part(0)
                    if j == 6:
                        turned(0)
                    elif j >= 3 and j % 2:
                        exps(j // 2 - 1)
                q_hi_part(KT - 1)
                turned(1)
                exps(3)
                parts(0)
                turned(2)
                parts(1)
                turned(3)
                parts(2)
                parts(3)
                out_phase(layer, 3 * layer + 2, u0 + KT, a0 + A_O, C_FN + 8 * layer)

            def ffn(layer):
                u0, a0 = F_UNIT[layer], F_ACC[layer]
                pr0 = layer * FT
                if layer == LAYERS - 1:
                    act.dma_start(fin_g, d["final_g"]).then_inc(fin_in, 16)

                def group(g, i=None):
                    for e in range(2):
                        pair = 2 * g + e
                        n = u0 + 4 * g + 2 * e
                        if g or e:
                            act.wait_ge(prod_ready, lin(pr0 + pair, i, 2))
                        split(n + LEAD, i)
                        if g or e:
                            idx = pair - 1 if i is None else i * 2 + (pair - 1)
                            act.activation(act_hi[:, idx, :], tmp[:, 2 + (pair - 1) % 2, :], ACT.Copy)\
                                .then_inc(ahi_ready, 1)
                        if not g and not e:
                            split(n + 1 + LEAD)
                        act.wait_ge(acc_drained, lin(a0 + 2 * pair + 1, i, 4))
                        act.activation(tmp[:, e, :], tmp[:, e, :], ACT.Silu).then_inc(silu_ready, 1)
                        if g or e:
                            split(n + 1 + LEAD, i)

                group(0)
                group(1)
                with act.Fori(0, FT // 2 - 2) as i:
                    group(2, i)
                act.wait_ge(prod_ready, pr0 + FT)
                act.activation(act_hi[:, FT - 1, :], tmp[:, 3, :], ACT.Copy).then_inc(ahi_ready, 1)
                norm = 3 * layer + 3
                for j in range(KT):
                    for e in range(3):
                        split(u0 + F_DN + 3 * j + e + LEAD)
                    residual(norm, j, C_ODD if layer == 0 else None, a0 + A_DN + j)

            def odd_mixer():
                a0, u0 = MIX_ACC[1], MIX_UNIT[1]
                act.wait_ge(acc_done, a0)
                act.dma_start(cs_d[:, :, :], d["cs_d"]).then_inc(c1_in, 16)
                act.dma_start(cs_r[:, :, :], d["cs_r"]).then_inc(c1_in, 16)
                act.dma_start(band[:, :], d["band"]).then_inc(c1_in, 16)

                def partners(r, t, far):
                    act.wait_ge(acc_drained, t + 1)
                    if r >= 2:
                        act.wait_ge(rot_ready, r - 1)
                    for q in range(0, P, far):
                        o = q + far if q // far % 2 == 0 else q - far
                        ins = act.activation(tmp[q:q + far, 2 + r % 2, :], tmp[o:o + far, r % 2, :], ACT.Copy)
                    ins.then_inc(shifted, 1)

                def exps(h):
                    for i in range(TT):
                        act.wait_ge(max_ready, DMAX + 4 * h + i + 1)
                        o, w = ROWS[i]
                        act.activation(dp[:, h % 2, o:o + w], dp[:, h % 2, o:o + w], ACT.Exp,
                                       bias=nmax[:, h % 2, i:i + 1], accum_out=psums[:, h % 2, i:i + 1])\
                            .then_inc(exp_ready, 1)

                def turned(h):
                    for e, (o, w) in enumerate(((0, 512), (512, 512), (1024, 256))):
                        t = aux_at["dt", h] + e
                        act.wait_ge(aux_done, t + 1)
                        act.activation(dpt[:, o:o + w], auxs[t % 4][:, 0:w], ACT.Copy).then_inc(aux_free_a, 1)

                def side(place):
                    r, c = place
                    split(u0 + U_RQK + r + LEAD)
                    if r < 8:
                        partners(8 + r, a0 + B_D + c, DH)
                    else:
                        act.wait_ge(acc_drained, a0 + B_D + c + 1)
                        act.activation(gate[:, r - 8, :], gate[:, r - 8, :], ACT.Silu).then_inc(silu_ready, 1)

                for n in range(4):
                    split(u0 + n + LEAD)
                for j in range(8):
                    split(u0 + U_DQK + j + LEAD)
                    partners(j, a0 + B_QK + j, 32)
                for n in range(4):
                    split(u0 + U_RV + n + LEAD)
                    if n % 2:
                        exps(n // 2)
                for h in range(DIL_H):
                    turned(h)
                    first, second = side_units(h)
                    side(first)
                    if h % 2:
                        t = a0 + B_D + 2 * h
                        act.wait_ge(acc_done, t + 1)
                        y_hi_part(h // 2, accs[t % 4][:, :])
                    if h + 2 < DIL_H:
                        exps(h + 2)
                    if second:
                        side(second)
                    if h == 6:
                        act.wait_ge(rot_half, 16)
                        act.dma_start(decay012[:, :, :], d["decay"][:, 0:3, :]).then_inc(c2_in, 16)
                        act.dma_start(sqsum[:, :], d["decay"][:, 3, :]).then_inc(c2_in, 16)
                for h in range(RET_H):
                    act.wait_ge(aux_free_v, freed_v(aux_at["rt", h]))
                    y_hi_part(4 + h, tmp[:, 2 + h % 2, :])

            out_phase(0, 1, MIX_UNIT[0] + U_OUT0, MIX_ACC[0] + A_OUT0, C_XN)
            cross_attention(0)
            ffn(0)
            odd_mixer()
            out_phase(1, 4, MIX_UNIT[1] + U_OUT1, MIX_ACC[1] + B_OUT1, C_XN + 8, with_mem=True)
            for n in range(U_KV):
                split(KV_UNIT[1] + n + LEAD)
                kv_hi_parts(1, n)
            kv_hi_parts(1, U_KV)
            cross_attention(1)
            ffn(1)
            act.wait_ge(aux_free_v, freed_v(aux_at["mean", 6]))
            act.wait_ge(rstd_ready, ROUND[6] + 1)
            for t in range(1, TT, 2):
                act.activation(y_tok[:, t, :], y_tok[:, t, :], ACT.Copy, scale=rstd_tok[:, t:t + 1])\
                    .then_inc(out_ready_a, 1)

        @block.gpsimd
        def _(pool):
            pool.memset(mean_w[:, :], 1.0 / D).then_inc(const_set, 1)
            pool.memset(mexp[:, :], -0.5).then_inc(const_set, 1)
            pool.memset(a_pad[:, :, 0:PAD], 0.0).then_inc(const_set, 1)
            pool.wait_ge(const_set, 3)

            def power(dst, src, n):
                pool.tensor_tensor(dst, src, mexp[:, 0:n], ALU.pow).then_inc(rstd_ready, 1)

            def norm_power(norm):
                pool.wait_ge(aux_free_v, freed_v(aux_at["mean", norm]))
                power(rstd_tok[:, :], var_e[:, :], TT)

            def add_squares(norm):
                for j in range(1, KT):
                    n = (KT - 1) * (norm - 1) + j
                    pool.wait_ge(sq_ready, 8 * (norm - 1) + j + 1)
                    if j > 1:
                        pool.wait_ge(sq_added, n - 1)
                    pool.tensor_tensor(sqsum[:, :], sqsum[:, :], tmp[:, j % 2, :], ALU.add).then_inc(sq_added, 1)

            pool.wait_ge(var_ready, 1)
            power(rstd_m[:, :], var_m[:, :], MT)
            pool.wait_ge(var_ready, 2)
            power(rstd_tok[:, :], var_e[:, :], TT)
            pool.wait_ge(c0_in, 16 * 5)
            pool.affine_select(out=ws_t[:, :, :], in_=ws_t[:, :, :], compare_op=ALU.is_ge, fill=0.0, base=0,
                               pattern=[[0, 4], [1, P]], channel_multiplier=-1).then_inc(ws_masked, 1)
            steps = 0
            for g, win in enumerate(WINDOWS):
                pool.wait_ge(acc_drained, MIX_ACC[0] + A_A + g + 1)
                if g == 0:
                    pool.wait_ge(var_ready, 3)
                    power(rstd_v[:, :], var_v[:, :], TT)
                if g:
                    pool.wait_ge(win_ready, g)
                src, width = a_pad[:, g, :], 1
                buf = 0
                while width < win:
                    last = 2 * width == win
                    if last and g >= 1:
                        pool.wait_ge(d_ready, g)
                    dst = wsum[:, 2 if last else buf, :]
                    lo = 2 * width - 1
                    ins = pool.tensor_tensor(dst[:, lo:PAD + S], src[:, lo:PAD + S],
                                             src[:, lo - width:PAD + S - width], ALU.add)
                    if last:
                        ins.then_inc(win_ready, 1)
                    else:
                        ins.then_inc(win_step, 1)
                        steps += 1
                        pool.wait_ge(win_step, steps)
                    src, buf, width = dst, 1 - buf, 2 * width
            for layer in range(LAYERS):
                if layer:
                    add_squares(3)
                    norm_power(3)
                    for r in range(16):
                        dst = (tq_d if r < 4 else tk_d)[:, r % 4, :] if r < 8 else tq[:, r - 8, :]
                        pool.wait_ge(rot_half, r + 1)
                        pool.tensor_tensor(dst, dst, tmp[:, 2 + r % 2, :], ALU.add).then_inc(rot_ready, 1)
                    for h in range(RET_H):
                        pool.wait_ge(rvar_ready, h + 1)
                        pool.tensor_tensor(rrstd[:, h % 2, :], rvar[:, h % 2, :], mexp[:, :], ALU.pow)\
                            .then_inc(rrstd_ready, 1)
                for norm in (3 * layer + 1, 3 * layer + 2):
                    add_squares(norm)
                    norm_power(norm)
            add_squares(6)
            norm_power(6)

        @block.vector
        def _(dve):
            chain = [0]

            def step(ins):
                chain[0] += 1
                ins.then_inc(dve_step, 1)
                return chain[0]

            def split(n, i=None):
                if n >= UNITS:
                    return
                s = n % RING
                dve.wait_ge(hi_ready, lin(n + 1, i, RING))
                dve.tensor_tensor(w_lo[:, s, :], raw[:, s, :], w_hi[:, s, :].bitcast(F32), ALU.subtract)\
                    .then_inc(lo_ready, 1)

            def acc(t):
                return accs[t % 4]

            def u_lo_part(norm, j, gcol):
                dve.wait_ge(uhi_ready, 8 * norm + j + 1)
                dve.scalar_tensor_tensor(out=u_lo[:, j, :], in0=hT[:, j, :], scalar=vecs[:, gcol + j:gcol + j + 1],
                                         in1=u_hi[:, j, :].bitcast(F32), op0=ALU.mult, op1=ALU.subtract)\
                    .then_inc(u_ready, 1)

            def y_lo_part(j, src, count, ready, scale=None):
                dve.wait_ge(part_hi, count)
                if scale is None:
                    ins = dve.tensor_tensor(y_lo[:, j, :], src, y_hi[:, j, :].bitcast(F32), ALU.subtract)
                else:
                    ins = dve.scalar_tensor_tensor(out=y_lo[:, j, :], in0=src, scalar=scale,
                                                   in1=y_hi[:, j, :].bitcast(F32), op0=ALU.mult, op1=ALU.subtract)
                ins.then_inc(ready, 1)

            def mean_to_var(norm):
                t = aux_at["mean", norm]
                dve.wait_ge(aux_done, t + 1)
                dve.tensor_scalar(var_e[:, :], auxs[t % 4][:, 0:TT], EPS, None, ALU.add).then_inc(aux_free_v, 1)

            def make_row(norm):
                t = aux_at["row", norm]
                dve.wait_ge(aux_done, t + 1)
                dve.tensor_copy(rstd_row[:, :], auxs[t % 4][:, :]).then_inc(aux_free_v, 1)
                dve.wait_ge(aux_free_v, freed_v(t))

            def scaled(t, dst, sems=None, f=None):
                dve.wait_ge(acc_done, t + 1)
                if f is None:
                    ins = dve.tensor_tensor(dst, acc(t)[:, :], rstd_row[:, :], ALU.mult)
                else:
                    ins = dve.scalar_tensor_tensor(out=dst, in0=acc(t)[:, :], scalar=f, in1=rstd_row[:, :],
                                                   op0=ALU.mult, op1=ALU.mult)
                ins.then_inc(acc_drained, 1)

            def scaled_tok(t, dst, i):
                dve.wait_ge(acc_done, t + 1)
                dve.tensor_scalar(dst, acc(t)[:, :], rstd_tok[:, i:i + 1], None, ALU.mult).then_inc(acc_drained, 1)

            def mem_lo_part(layer, j):
                c = C_MN + 8 * layer + j
                dve.wait_ge(mhi_ready, 8 * layer + j + 1)
                dve.scalar_tensor_tensor(out=mem_lo[:, j, :], in0=memT[:, j, :], scalar=vecs[:, c:c + 1],
                                         in1=mem_hi[:, j, :].bitcast(F32), op0=ALU.mult, op1=ALU.subtract)\
                    .then_inc(mlo_ready, 1)

            def out_tile(j):
                k = aux_at["out"] + j
                if j == 0:
                    dve.wait_ge(fin_in, 16)
                w = slice(j * P, (j + 1) * P)
                dve.wait_ge(aux_done, k + 1)
                dve.tensor_tensor(y_tok[:, :, w], auxs[k % 4][:, :].rearrange("p (t f) -> p t f", t=TT),
                                  fin_g[:, w].rearrange("p (a f) -> p a f", a=1).broadcast_to([P, TT, P]),
                                  ALU.mult).then_inc(aux_free_v, 1)

            def residual_phase(layer, norm, a0, u0, per, gcol, with_mem=False):
                for j in range(KT):
                    for e in range(per):
                        split(u0 + per * j + e + LEAD)
                    dve.wait_ge(acc_done, a0 + j + 1)
                    dve.tensor_tensor(hT[:, j, :], hT[:, j, :], acc(a0 + j)[:, :], ALU.add).then_inc(acc_drained, 1)
                    if gcol is not None and j:
                        u_lo_part(norm, j - 1, gcol)
                    if norm == 6 and j:
                        out_tile(j - 1)
                    if with_mem and j < KT // 2:
                        mem_lo_part(layer, 2 * j)
                        mem_lo_part(layer, 2 * j + 1)
                if gcol is not None:
                    u_lo_part(norm, KT - 1, gcol)

            def kv_drain(layer, j):
                t = KV_ACC[layer] + j
                dve.wait_ge(acc_done, t + 1)
                if j < KT:
                    ins = dve.tensor_tensor(kv_tile(j, xk, xv), acc(t)[:, 0:M], rstd_mrow[:, :], ALU.mult)
                else:
                    m = (j - KT) % MT
                    ins = dve.tensor_scalar(kv_tile(j, xk, xv), acc(t)[:, :], rstd_m[:, m:m + 1], None, ALU.mult)
                ins.then_inc(acc_drained, 1)

            def kv_lo_parts(layer, n):
                for j in kv_split_due(n):
                    dve.wait_ge(kvhi_ready, A_KV * layer + j + 1)
                    dve.tensor_tensor(kv_tile(j, xk_lo, xv_lo), kv_tile(j, xk, xv),
                                      kv_tile(j, xk_hi, xv_hi).bitcast(F32), ALU.subtract).then_inc(kvlo_ready, 1)

            for t in range(4):
                k = aux_at["mem"] + t
                dve.wait_ge(aux_done, k + 1)
                dve.tensor_copy(memT[:, 2 * t:2 * t + 2, :], auxs[k % 4][:, :].rearrange("p (a b) -> p a b", a=2))\
                    .then_inc(aux_free_v, 1)
                if t == 2:
                    split(0)
            dve.wait_ge(aux_free_v, freed_v(aux_at["mem"] + 3))
            for j in range(KT):
                mem_lo_part(0, j)
            for n in range(1, LEAD):
                split(n)
            dve.wait_ge(x_sq, MT)
            dve.tensor_scalar(var_m[:, :], ssq_m[:, :], 1.0 / D, EPS, ALU.mult, ALU.add).then_inc(var_ready, 1)
            for j in range(KT):
                split(j + LEAD)
                if j == 2:
                    t = aux_at["mem row"]
                    dve.wait_ge(aux_done, t + 1)
                    dve.tensor_copy(rstd_mrow[:, :], auxs[t % 4][:, 0:M]).then_inc(aux_free_v, 1)
                    dve.wait_ge(aux_free_v, freed_v(t))
                    kv_drain(0, 0)
                    kv_drain(0, 1)
                if j == 2:
                    kv_lo_parts(0, 1)
                if j >= 2:
                    kv_drain(0, j)
                    kv_lo_parts(0, j)
            for j in range(KT):
                split(KT + j + LEAD)
                kv_lo_parts(0, KT + j)
                if j == 1:
                    dve.wait_ge(x_sq, MT + TT)
                    dve.tensor_scalar(var_e[:, 0:TT], ssq[:, 0:TT], 1.0 / D, EPS, ALU.mult, ALU.add)\
                        .then_inc(var_ready, 1)
                if j:
                    u_lo_part(0, j - 1, C_EVEN)
                if j % 4 == 3:
                    for m in range(MT):
                        kv_drain(0, KT + (j // 4) * MT + m)
            u_lo_part(0, KT - 1, C_EVEN)
            kv_lo_parts(0, U_KV)

            a0, u0 = MIX_ACC[0], MIX_UNIT[0]
            for n in range(4):
                split(u0 + n + LEAD)
                if n == 0:
                    make_row(0)
            for t in range(TT):
                scaled_tok(a0 + A_V + t, vn[:, t, :], t)

            def pooled(g):
                win = WINDOWS[g]
                dve.wait_ge(win_ready, g + 1)
                n1 = step(dve.tensor_tensor(tmp[:, 2, 0:PAD], wsum[:, 2, PAD:2 * PAD], invcnt[:, g, :], ALU.mult))
                dve.scalar_tensor_tensor(out=a_pad[:, g, 2 * PAD:PAD + S], in0=wsum[:, 2, 2 * PAD:PAD + S],
                                         scalar=1.0 / win, in1=a_pad[:, g, 2 * PAD:PAD + S], op0=ALU.mult, op1=ALU.subtract)
                dve.wait_ge(dve_step, n1)
                dve.tensor_tensor(a_pad[:, g, PAD:2 * PAD], tmp[:, 2, 0:PAD], a_pad[:, g, PAD:2 * PAD], ALU.subtract)\
                    .then_inc(d_ready, 1)

            dve.wait_ge(const_set, 3)
            dve.wait_ge(c0_in, 16 * 5)
            for g in range(4):
                split(u0 + 4 + g + LEAD)
                scaled(a0 + A_A + g, a_pad[:, g, PAD:PAD + S])
                if g == 0:
                    dve.wait_ge(vsq, TT)
                    dve.tensor_scalar(var_v[:, :], ssq_v[:, :], 1.0 / S, EPS, ALU.mult, ALU.add)\
                        .then_inc(var_ready, 1)
                if g == 1:
                    dve.wait_ge(rstd_ready, 3)
                    for t in range(TT):
                        dve.scalar_tensor_tensor(out=vn[:, t, :], in0=vn[:, t, :], scalar=rstd_v[:, t:t + 1],
                                                 in1=sgu_g[:, :], op0=ALU.mult, op1=ALU.mult).then_inc(vn_ready, 1)
            for g in range(4):
                split(u0 + 8 + g + LEAD)
                scaled(a0 + A_U + g, uu[:, g, :])
                pooled(g)
            for g in range(4):
                t = a0 + A_POOL + g
                y_lo_part(g, acc(t)[:, :], g + 1, acc_drained, scale=vecs[:, C_PS + g:C_PS + g + 1])
            for g in range(4):
                t = a0 + A_SGU + g
                dve.wait_ge(acc_done, t + 1)
                if g >= 2:
                    dve.wait_ge(y_ready, g - 1)
                dve.tensor_tensor(tmp[:, g % 2, :].rearrange("p (n t) -> p n t", n=TT),
                                  acc(t)[:, :].rearrange("p (n t) -> p n t", n=TT),
                                  sgu_b[:, g:g + 1, :].broadcast_to([P, TT, P]), ALU.add).then_inc(acc_drained, 1)
                dve.wait_ge(acc_drained, t + 1)
                dve.wait_ge(ugelu, g + 1)
                dve.tensor_tensor(tmp[:, g % 2, :], tmp[:, g % 2, :], uu[:, g, :], ALU.mult).then_inc(y_full, 1)
                if g:
                    y_lo_part(4 + g - 1, tmp[:, (g - 1) % 2, :], 4 + g, y_ready)
            y_lo_part(7, tmp[:, 1, :], 8, y_ready)
            residual_phase(0, 1, a0 + A_OUT0, u0 + U_OUT0, 1, C_XN)

            def cross_attention(layer):
                norm = 3 * layer + 1
                a0, u0 = X_ACC[layer], X_UNIT[layer]
                if layer:
                    for j in range(KT):
                        split(KV_UNIT[1] + j + LEAD)
                        kv_drain(1, j)
                        kv_lo_parts(1, j)
                        if j == 2:
                            mean_to_var(norm)
                        if j == 5:
                            make_row(norm)
                    for j in range(KT):
                        split(KV_UNIT[1] + KT + j + LEAD)
                        kv_lo_parts(1, KT + j)
                        if j % 4 == 3:
                            for m in range(MT):
                                kv_drain(1, KT + (j // 4) * MT + m)

                    kv_lo_parts(1, U_KV)

                def q_lo_part(j):
                    dve.wait_ge(qhi_ready, KT * layer + j + 1)
                    dve.tensor_tensor(y_lo[:, j, :], xq[:, j, :], y_hi[:, j, :].bitcast(F32), ALU.subtract)\
                        .then_inc(qlo_ready, 1)

                def turned(h):
                    for k in range(MT):
                        t = aux_at["xt", layer, h] + k
                        dve.wait_ge(pthi_ready, MT * (X_H * layer + h) + k + 1)
                        dve.tensor_tensor(xpt_lo[:, h % 2, k, :], auxs[t % 4][:, :],
                                          xpt_hi[:, h % 2, k, :].bitcast(F32), ALU.subtract).then_inc(aux_free_v, 1)

                def maxima(h):
                    for q in range(2):
                        t = aux_at["xs", layer, h] + q
                        dve.wait_ge(aux_done, t + 1)
                        dve.tensor_reduce(nmax[:, h % 2, 2 * q:2 * q + 2],
                                          auxs[t % 4][:, :].rearrange("p (a b) -> p a b", a=2), AX.X, ALU.max,
                                          negate=True).then_inc(max_ready, 1)

                def normalise(h):
                    dve.wait_ge(aux_free_a, freed_a(aux_at["xs", layer, h] + 1))
                    n = step(dve.reciprocal(pinv[:, h % 2, :], psums[:, h % 2, :]))
                    dve.wait_ge(dve_step, n)
                    for q in range(TT):
                        ins = dve.tensor_scalar(xp[:, h % 2, q, :], xp[:, h % 2, q, :], pinv[:, h % 2, q:q + 1],
                                                None, ALU.mult)
                    ins.then_inc(p_ready, 1)

                def parts(h):
                    for e in range(2):
                        t = a0 + A_XO + 2 * h + e
                        y_lo_part(2 * h + e, acc(t)[:, :], PHX[layer] + 2 * h + e + 1, acc_drained)

                for j in range(KT):
                    if j:
                        q_lo_part(j - 1)
                    if j != 1 or layer:
                        split(u0 + j + LEAD)
                    if j == 0 and not layer:
                        mean_to_var(norm)
                        split(u0 + 1 + LEAD)
                        make_row(norm)
                    if j >= 3 and j % 2:
                        maxima(j // 2 - 1)
                    if j == 6:
                        turned(0)
                    scaled(a0 + A_Q + j, xq[:, j, :], f=float(256) ** -0.5)
                    if j in (3, 5):
                        normalise(j // 2 - 1)
                q_lo_part(KT - 1)
                turned(1)
                normalise(2)
                maxima(3)
                parts(0)
                normalise(3)
                turned(2)
                parts(1)
                turned(3)
                parts(2)
                parts(3)
                residual_phase(layer, 3 * layer + 2, a0 + A_O, u0 + KT, 1, C_FN + 8 * layer)

            def ffn(layer):
                norm = 3 * layer + 2
                u0, a0 = F_UNIT[layer], F_ACC[layer]
                pr0 = layer * FT

                def lo_of(pair, i=None):
                    dve.wait_ge(ahi_ready, lin(pr0 + pair + 1, i, 2))
                    idx = pair if i is None else i * 2 + pair
                    dve.tensor_tensor(act_lo[:, idx, :], tmp[:, 2 + pair % 2, :], act_hi[:, idx, :].bitcast(F32),
                                      ALU.subtract).then_inc(act_ready, 1)

                def group(g, i=None):
                    for e in range(2):
                        pair = 2 * g + e
                        n = u0 + 4 * g + 2 * e
                        tg = a0 + 4 * g + 2 * e
                        split(n + LEAD, i)
                        if pair == 0:
                            mean_to_var(norm)
                            split(n + 1 + LEAD)
                            make_row(norm)
                        dve.wait_ge(acc_done, lin(tg + 1, i, 4))
                        dve.tensor_tensor(tmp[:, e, :], acc(tg)[:, :], rstd_row[:, :], ALU.mult)\
                            .then_inc(acc_drained, 1)
                        if pair >= 1:
                            lo_of(pair - 1, i)
                        if pair:
                            split(n + 1 + LEAD, i)
                        dve.wait_ge(acc_done, lin(tg + 2, i, 4))
                        dve.tensor_tensor(tmp[:, 2 + e, :], acc(tg + 1)[:, :], rstd_row[:, :], ALU.mult)\
                            .then_inc(acc_drained, 1)
                        dve.wait_ge(silu_ready, lin(SILU[layer] + pair + 1, i, 2))
                        dve.wait_ge(acc_drained, lin(tg + 2, i, 4))
                        dve.tensor_tensor(tmp[:, 2 + e, :], tmp[:, 2 + e, :], tmp[:, e, :], ALU.mult)\
                            .then_inc(prod_ready, 1)

                group(0)
                group(1)
                with dve.Fori(0, FT // 2 - 2) as i:
                    group(2, i)
                lo_of(FT - 1)
                residual_phase(layer, 3 * layer + 3, a0 + A_DN, u0 + F_DN, 3, C_ODD if layer == 0 else None)

            def odd_mixer():
                a0, u0 = MIX_ACC[1], MIX_UNIT[1]

                def rotate(r):
                    dst = (tq_d if r < 4 else tk_d)[:, r % 4, :] if r < 8 else tq[:, r - 8, :]
                    cs = cs_d if r < 8 else cs_r
                    dve.tensor_tensor(dst, tmp[:, r % 2, :], cs[:, 0, :], ALU.mult)
                    dve.wait_ge(shifted, r + 1)
                    dve.tensor_tensor(tmp[:, 2 + r % 2, :], tmp[:, 2 + r % 2, :], cs[:, 1, :], ALU.mult)\
                        .then_inc(rot_half, 1)

                def masked(h):
                    for i in range(TT):
                        t = aux_at["ds", h] + i
                        o, w = ROWS[i]
                        dve.wait_ge(aux_done, t + 1)
                        dve.scalar_tensor_tensor(out=dp[:, h % 2, o:o + w], in0=auxs[t % 4][:, 0:w],
                                                 scalar=float(DH) ** -0.5, in1=band[:, S - w:S], op0=ALU.mult,
                                                 op1=ALU.add).then_inc(aux_free_v, 1)
                    for i in range(TT):
                        t = aux_at["ds", h] + i
                        o, w = ROWS[i]
                        dve.wait_ge(aux_free_v, freed_v(t))
                        dve.tensor_reduce(nmax[:, h % 2, i:i + 1], dp[:, h % 2, o:o + w], AX.X, ALU.max,
                                          negate=True).then_inc(max_ready, 1)

                def normalise(h):
                    dve.wait_ge(exp_ready, 4 * h + 4)
                    n = step(dve.reciprocal(pinv[:, h % 2, :], psums[:, h % 2, :]))
                    dve.wait_ge(dve_step, n)
                    for i in range(TT):
                        o, w = ROWS[i]
                        ins = dve.tensor_scalar(dp[:, h % 2, o:o + w], dp[:, h % 2, o:o + w],
                                                pinv[:, h % 2, i:i + 1], None, ALU.mult)
                    ins.then_inc(p_ready, 1)

                def decayed(h):
                    for e, kts in enumerate(((0,), (1, 3), (2,))):
                        t = aux_at["rs", h] + e
                        dve.wait_ge(aux_done, t + 1)
                        for kt in kts:
                            o, w = BLOCK[kt]
                            c = 384 if kt == 3 else 0
                            ins = dve.tensor_tensor(inner[:, h % 2, o:o + w], auxs[t % 4][:, c:c + w],
                                                    decay(h)[:, 0:w], ALU.mult)
                        ins.then_inc(aux_free_v, 1)

                def side(place):
                    r, c = place
                    split(u0 + U_RQK + r + LEAD)
                    if r < 8:
                        dve.wait_ge(rot_half, 8 + r - 1)
                    scaled(a0 + B_D + c, tmp[:, r % 2, :] if r < 8 else gate[:, r - 8, :])
                    if 0 < r <= 8:
                        rotate(8 + r - 1)

                for n in range(4):
                    split(u0 + n + LEAD)
                    if n == 0:
                        mean_to_var(3)
                    if n == 1:
                        make_row(3)
                for t in range(TT):
                    scaled_tok(a0 + B_V + t, tv_d[:, t, :], t)
                dve.wait_ge(c1_in, 16 * 3)
                for j in range(8):
                    split(u0 + U_DQK + j + LEAD)
                    if j >= 2:
                        dve.wait_ge(rot_half, j - 1)
                    scaled(a0 + B_QK + j, tmp[:, j % 2, :])
                    if j:
                        rotate(j - 1)
                for n in range(4):
                    split(u0 + U_RV + n + LEAD)
                    if n == 0:
                        rotate(7)
                    if n == 1:
                        dve.wait_ge(rot_half, 8)
                        masked(0)
                    if n == 2:
                        normalise(0)
                    if n == 3:
                        masked(1)
                for t in range(TT):
                    scaled_tok(a0 + B_RV + t, tv[:, t, :], t)
                for h in range(DIL_H):
                    first, second = side_units(h)
                    if h + 1 < DIL_H:
                        normalise(h + 1)
                    side(first)
                    if h + 2 < DIL_H:
                        masked(h + 2)
                    if h % 2:
                        t = a0 + B_D + 2 * h
                        y_lo_part(h // 2, acc(t)[:, :], PHM1 + h // 2 + 1, acc_drained)
                    if h == DIL_H - 1:
                        dve.wait_ge(c2_in, 16 * 2)
                        decayed(0)
                    if second:
                        side(second)

                def head_stats(h):
                    t = a0 + B_R + h
                    dve.wait_ge(acc_done, t + 1)
                    for i in range(TT):
                        n = step(dve.bn_stats(stats[:, i, :], acc(t)[:, i * P:(i + 1) * P]))
                    dve.wait_ge(dve_step, n)
                    for i in range(TT):
                        n = step(dve.bn_aggr(mv[:, i, :], stats[:, i, :]))
                    dve.wait_ge(dve_step, n)
                    dve.tensor_scalar(rvar[:, h % 2, :], mv[:, :, 1], EPS, None, ALU.add).then_inc(rvar_ready, 1)

                def head_scale(h):
                    t = a0 + B_R + h
                    dve.wait_ge(rrstd_ready, h + 1)
                    for i in range(TT):
                        ins = dve.tensor_scalar(tmp[:, h % 2, i * P:(i + 1) * P], acc(t)[:, i * P:(i + 1) * P],
                                                mv[:, i, 0:1], rrstd[:, h % 2, i:i + 1], ALU.subtract, ALU.mult)
                    ins.then_inc(acc_drained, 1)

                def gated(h):
                    t = aux_at["rt", h]
                    dve.wait_ge(aux_done, t + 1)
                    dve.wait_ge(silu_ready, FT + h + 1)
                    dve.tensor_tensor(tmp[:, 2 + h % 2, :], auxs[t % 4][:, :], gate[:, h, :], ALU.mult)\
                        .then_inc(aux_free_v, 1)

                for h in range(RET_H):
                    if h + 1 < RET_H:
                        decayed(h + 1)
                    head_stats(h)
                    if h:
                        gated(h - 1)
                    head_scale(h)
                    if h:
                        y_lo_part(4 + h - 1, tmp[:, 2 + (h - 1) % 2, :], PHM1 + 4 + h, y_ready)
                gated(3)
                y_lo_part(7, tmp[:, 3, :], PHM1 + 8, y_ready)
                residual_phase(1, 4, a0 + B_OUT1, u0 + U_OUT1, 1, C_XN + 8, with_mem=True)

            cross_attention(0)
            ffn(0)
            odd_mixer()
            cross_attention(1)
            ffn(1)

            out_tile(KT - 1)
            mean_to_var(6)
            dve.wait_ge(rstd_ready, ROUND[6] + 1)
            dve.wait_ge(aux_free_v, freed_v(aux_at["mean", 6]))
            for t in range(0, TT, 2):
                dve.tensor_scalar(y_tok[:, t, :], y_tok[:, t, :], rstd_tok[:, t:t + 1], None, ALU.mult)\
                    .then_inc(out_ready_v, 1)

        @block.tensor
        def _(pe):
            def three(out, w_h, w_l, x_h, x_l, first, last):
                pe.matmul(out, w_h, x_h, start=first, stop=False)
                pe.matmul(out, w_h, x_l, start=False, stop=False)
                return pe.matmul(out, w_l, x_h, start=False, stop=last)

            def acc_free(t, i=None):
                if t >= 4:
                    pe.wait_ge(acc_drained, lin(t - 3, i, 4))

            def weights_in(n, i=None):
                pe.wait_ge(lo_ready, lin(n + 1, i, RING))

            def rows_unit(n, t, x_h, x_l, i=None, before=None, k0=0, kn=KT, last=True):
                out = accs[t % 4][:, 0:x_h.shape[2]]
                s = n % RING
                weights_in(n, i)
                if k0 == 0:
                    acc_free(t, i)
                for k in range(kn):
                    if before is not None:
                        before(k0 + k)
                    w = slice(k * P, (k + 1) * P)
                    ins = three(out, w_hi[:, s, w], w_lo[:, s, w], x_h[:, k0 + k, :], x_l[:, k0 + k, :],
                                k0 + k == 0, last and k == kn - 1)
                ins.then_inc(acc_done if last else unit_used, 1)

            def cols_units(n0, t0, x_h, x_l, tiles, before=None, after=None):
                for q in range(4):
                    n = n0 + q
                    s = n % RING
                    weights_in(n)
                    for kk in range(2):
                        k = 2 * q + kk
                        if before is not None:
                            before(k)
                        w = slice(kk * 512, (kk + 1) * 512)
                        for m in range(tiles):
                            if k == 0:
                                acc_free(t0 + m)
                            tok = slice(m * P, (m + 1) * P)
                            out = accs[(t0 + m) % 4][:, :]
                            pe.matmul(out, x_h[:, k, tok], w_hi[:, s, w], start=(k == 0), stop=False)
                            pe.matmul(out, x_h[:, k, tok], w_lo[:, s, w], start=False, stop=False)
                            ins = pe.matmul(out, x_l[:, k, tok], w_hi[:, s, w], start=False, stop=(k == KT - 1))
                            if k == KT - 1:
                                ins.then_inc(acc_done, 1)
                    if q < 3:
                        ins.then_inc(unit_used, 1)
                    if after is not None:
                        after(q)

            def mean(norm):
                t = aux_at["mean", norm]
                aux_free(pe, t)
                pe.wait_ge(sq_added, (KT - 1) * norm)
                for i in range(TT):
                    ins = pe.matmul(auxs[t % 4][:, i:i + 1], sqsum[:, i * P:(i + 1) * P], mean_w[:, :],
                                    start=True, stop=True)
                ins.then_inc(aux_done, 1)

            def row(norm):
                t = aux_at["row", norm]
                aux_free(pe, t)
                pe.wait_ge(rstd_ready, ROUND[norm] + 1)
                for i in range(TT):
                    ins = pe.transpose(auxs[t % 4][:, i * P:(i + 1) * P], rstd_tok[:, i:i + 1].broadcast_to([P, P]),
                                       ident[:, :])
                ins.then_inc(aux_done, 1)

            def stats_after(norm, first=0, second=1):
                def f(q):
                    if q == first:
                        mean(norm)
                    if q == second:
                        row(norm)
                return f

            def u_in(norm):
                return lambda k: pe.wait_ge(u_ready, 8 * norm + k + 1)

            def kv_proj(layer, after=None):
                a0, u0 = KV_ACC[layer], KV_UNIT[layer]
                for j in range(KT):
                    rows_unit(u0 + j, a0 + A_K + j, mem_hi, mem_lo,
                              before=(lambda k: pe.wait_ge(mlo_ready, 8 * layer + k + 1)) if j == 0 else None)
                    if after is not None:
                        after(j)
                for c in range(2):
                    cols_units(u0 + KT + 4 * c, a0 + A_XV + 2 * c, mem_hi, mem_lo, MT)

            pe.wait_ge(ident_in, 16)
            for t in range(4):
                pe.wait_ge(mem_in[t], 16)
                k = aux_at["mem"] + t
                aux_free(pe, k)
                for e in range(2):
                    for m in range(MT):
                        c = e * M + m * P
                        j = 2 * t + e
                        ins = pe.transpose(auxs[k % 4][:, c:c + P], mem_tok[:, m, j * P:(j + 1) * P], ident[:, :])
                ins.then_inc(aux_done, 1)

            def turn_x(j):
                t = aux_at["x"] + j
                aux_free(pe, t)
                for i in range(TT):
                    ins = pe.transpose(auxs[t % 4][:, i * P:(i + 1) * P], x_tok[:, i, j * P:(j + 1) * P], ident[:, :])
                ins.then_inc(aux_done, 1)

            a0, u0 = KV_ACC[0], KV_UNIT[0]
            for j in range(KT):
                rows_unit(u0 + j, a0 + A_K + j, mem_hi, mem_lo,
                          before=(lambda k: pe.wait_ge(mlo_ready, k + 1)) if j == 0 else None)
                if j == 2:
                    t = aux_at["mem row"]
                    aux_free(pe, t)
                    pe.wait_ge(rstd_ready, 1)
                    for m in range(MT):
                        ins = pe.transpose(auxs[t % 4][:, m * P:(m + 1) * P],
                                           rstd_m[:, m:m + 1].broadcast_to([P, P]), ident[:, :])
                    ins.then_inc(aux_done, 1)
            pe.wait_ge(x_in, 16 * TT)
            for j in range(4):
                turn_x(j)
            cols_units(u0 + KT, a0 + A_XV, mem_hi, mem_lo, MT)
            for j in range(4, 8):
                turn_x(j)
            cols_units(u0 + KT + 4, a0 + A_XV + 2, mem_hi, mem_lo, MT, after=lambda q: row(0) if q == 1 else None)

            a0, u0 = MIX_ACC[0], MIX_UNIT[0]
            cols_units(u0 + U_V, a0 + A_V, u_hi, u_lo, TT, before=u_in(0))
            for g in range(8):
                rows_unit(u0 + U_A + g, a0 + A_A + g, u_hi, u_lo)
            for g in range(4):
                t = a0 + A_POOL + g
                acc_free(t)
                pe.wait_ge(d_ready, g + 1)
                pe.matmul(accs[t % 4][:, :], pool_w[:, g, :], a_pad[:, g, PAD:PAD + S], start=True, stop=True)\
                    .then_inc(acc_done, 1)
            pe.wait_ge(vn_ready, TT)
            pe.wait_ge(ws_masked, 1)
            for g in range(4):
                t = a0 + A_SGU + g
                acc_free(t)
                for n in range(TT):
                    ins = pe.matmul(accs[t % 4][:, n * P:(n + 1) * P], vn[:, n, g * P:(g + 1) * P], ws_t[:, g, :],
                                    start=True, stop=True)
                ins.then_inc(acc_done, 1)

            def out_unit(u0, t0, j, k0, k1, before=None):
                n, t = u0 + j, t0 + j
                s = n % RING
                if k0 == 0:
                    weights_in(n)
                    acc_free(t)
                for k in range(k0, k1):
                    if before is not None:
                        before(k)
                    w = slice(k * P, (k + 1) * P)
                    ins = three(accs[t % 4][:, :], w_hi[:, s, w], w_lo[:, s, w], y_hi[:, k, :], y_lo[:, k, :],
                                k == 0, k == KT - 1)
                if k1 == KT:
                    ins.then_inc(acc_done, 1)

            def out_proj(u0, t0, y_in):
                for j in range(3):
                    out_unit(u0, t0, j, KT // 2, KT - 1, before=y_in if j == 0 else None)
                for j in range(3):
                    out_unit(u0, t0, j, KT - 1, KT, before=y_in if j == 0 else None)
                for j in range(3, KT):
                    out_unit(u0, t0, j, 0, KT)

            for j in range(3):
                out_unit(u0 + U_OUT0, a0 + A_OUT0, j, 0, KT // 2,
                         before=(lambda k: pe.wait_ge(acc_drained, a0 + A_POOL + k + 1)) if j == 0 else None)
            out_proj(u0 + U_OUT0, a0 + A_OUT0, lambda k: pe.wait_ge(y_ready, k - 3))

            def cross_attention(layer):
                norm = 3 * layer + 1
                a0, u0 = X_ACC[layer], X_UNIT[layer]
                if layer:
                    kv_proj(1, after=stats_after(norm, 2, 5))

                def scores(h):
                    pe.wait_ge(qlo_ready, KT * layer + 2 * h + 2)
                    for c in range(2):
                        t = aux_at["xs", layer, h] + c
                        aux_free(pe, t)
                        for e in range(2):
                            i = 2 * c + e
                            for k in range(2):
                                f, tok = 2 * h + k, slice(i * P, (i + 1) * P)
                                ins = three(auxs[t % 4][:, e * M:(e + 1) * M], y_hi[:, f, tok], y_lo[:, f, tok],
                                            xk_hi[:, f, :], xk_lo[:, f, :], k == 0, k == 1)
                        ins.then_inc(aux_done, 1)

                def turn(h):
                    pe.wait_ge(p_ready, (X_H + DIL_H) * layer + h + 1)
                    for k in range(MT):
                        t = aux_at["xt", layer, h] + k
                        aux_free(pe, t)
                        for i in range(TT):
                            ins = pe.transpose(auxs[t % 4][:, i * P:(i + 1) * P], xp[:, h % 2, i, k * P:(k + 1) * P],
                                               ident[:, :])
                        ins.then_inc(aux_done, 1)

                def values(h, halves=(0, 1)):
                    pe.wait_ge(aux_free_v, freed_v(aux_at["xt", layer, h] + 1))
                    for e in halves:
                        t = a0 + A_XO + 2 * h + e
                        acc_free(t)
                        for k in range(MT):
                            w = slice((2 * h + e) * P, (2 * h + e + 1) * P)
                            ins = three(accs[t % 4][:, :], xv_hi[:, k, w], xv_lo[:, k, w],
                                        xpt_hi[:, h % 2, k, :], xpt_lo[:, h % 2, k, :], k == 0, k == MT - 1)
                        ins.then_inc(acc_done, 1)

                for j in range(KT):
                    rows_unit(u0 + j, a0 + A_Q + j, u_hi, u_lo, before=u_in(norm) if j == 0 else None)
                    if not layer:
                        stats_after(norm)(j)
                    if j == 2:
                        pe.wait_ge(kvlo_ready, A_KV * (layer + 1))
                    if j in (2, 4, 6):
                        scores(j // 2 - 1)
                    if j == 5:
                        turn(0)
                turn(1)
                values(0, (0,))
                scores(3)
                values(0, (1,))
                turn(2)
                values(1)
                turn(3)
                values(2)
                values(3)
                for j in range(KT):
                    rows_unit(u0 + KT + j, a0 + A_O + j, y_hi, y_lo,
                              before=(lambda k: pe.wait_ge(acc_drained, a0 + A_XO + k + 1)) if j == 0 else None)

            def turn_out(j):
                k = aux_at["out"] + j
                aux_free(pe, k)
                pe.wait_ge(acc_drained, F_ACC[1] + A_DN + j + 1)
                for t in range(TT):
                    ins = pe.transpose(auxs[k % 4][:, t * P:(t + 1) * P], hT[:, j, t * P:(t + 1) * P], ident[:, :])
                ins.then_inc(aux_done, 1)

            def ffn(layer):
                norm = 3 * layer + 2
                u0, a0 = F_UNIT[layer], F_ACC[layer]

                def group(g, i=None):
                    for e in range(4):
                        rows_unit(u0 + 4 * g + e, a0 + 4 * g + e, u_hi, u_lo, i,
                                  before=u_in(norm) if g == 0 and e == 0 else None)
                        if g == 0:
                            stats_after(norm)(e)

                group(0)
                group(1)
                with pe.Fori(0, FT // 2 - 2) as i:
                    group(2, i)
                for j in range(KT):
                    for e, kn in enumerate((8, 8, 6)):
                        rows_unit(u0 + F_DN + 3 * j + e, a0 + A_DN + j, act_hi, act_lo, k0=8 * e, kn=kn,
                                  last=(e == 2),
                                  before=(lambda k: pe.wait_ge(act_ready, FT * layer + k + 1)) if j == 0 else None)
                    if layer == LAYERS - 1 and j:
                        turn_out(j - 1)

            def odd_mixer():
                a0, u0 = MIX_ACC[1], MIX_UNIT[1]

                cols_units(u0 + U_DV, a0 + B_V, u_hi, u_lo, TT, before=u_in(3), after=stats_after(3))
                for j in range(8):
                    rows_unit(u0 + U_DQK + j, a0 + B_QK + j, u_hi, u_lo)

                def scores(h):
                    q0 = DH * (h % 2)
                    pe.wait_ge(rot_ready, 5 + h // 2)
                    for i in range(TT):
                        t = aux_at["ds", h] + i
                        aux_free(pe, t)
                        pe.matmul(auxs[t % 4][:, 0:(i + 1) * P], tq_d[q0:q0 + DH, h // 2, i * P:(i + 1) * P],
                                  tk_d[q0:q0 + DH, h // 2, 0:(i + 1) * P], start=True, stop=True)\
                            .then_inc(aux_done, 1)

                def turn(h):
                    pe.wait_ge(p_ready, X_H + h + 1)
                    for e, kts in enumerate(((0,), (1, 3), (2,))):
                        t = aux_at["dt", h] + e
                        aux_free(pe, t)
                        for kt in kts:
                            c = 384 if kt == 3 else 0
                            for i in range(kt, TT):
                                o = ROWS[i][0] + kt * P
                                ins = pe.transpose(auxs[t % 4][:, c + (i - kt) * P:c + (i - kt + 1) * P],
                                                   dp[:, h % 2, o:o + P], ident[:, :])
                        ins.then_inc(aux_done, 1)

                def values(h):
                    t = a0 + B_D + 4 * (h // 2) + 2
                    q0 = DH * (h % 2)
                    if h % 2 == 0:
                        acc_free(t)
                    pe.wait_ge(aux_free_a, freed_a(aux_at["dt", h] + 2))
                    for kt in range(TT):
                        o, w = BLOCK[kt]
                        ins = pe.matmul(accs[t % 4][q0:q0 + DH, kt * P:S], tv_d[:, kt, h * DH:(h + 1) * DH],
                                        dpt[:, o:o + w], start=(kt == 0), stop=(kt == TT - 1))
                    if h % 2:
                        ins.then_inc(acc_done, 1)

                def ret_scores(h):
                    for e, kts in enumerate(((0,), (1, 3), (2,))):
                        t = aux_at["rs", h] + e
                        aux_free(pe, t)
                        for kt in kts:
                            c, w = (384 if kt == 3 else 0), BLOCK[kt][1]
                            ins = pe.matmul(auxs[t % 4][:, c:c + w], tq[:, 4 + h, kt * P:(kt + 1) * P],
                                            tq[:, h, kt * P:S], start=True, stop=True)
                        ins.then_inc(aux_done, 1)

                def side(place):
                    r, c = place
                    rows_unit(u0 + U_RQK + r, a0 + B_D + c, u_hi, u_lo)

                cols_units(u0 + U_RV, a0 + B_RV, u_hi, u_lo, TT,
                           after=lambda q: scores(q // 2) if q % 2 == 0 else None)
                for h in range(DIL_H):
                    turn(h)
                    first, second = side_units(h)
                    side(first)
                    if h + 2 < DIL_H:
                        scores(h + 2)
                    values(h)
                    if h == DIL_H - 1:
                        pe.wait_ge(rot_ready, 16)
                        ret_scores(0)
                    if second:
                        side(second)

                def ret_values(h):
                    t = a0 + B_R + h
                    acc_free(t)
                    pe.wait_ge(aux_free_v, freed_v(aux_at["rs", h] + 2))
                    for i in range(TT):
                        for kt in range(i + 1):
                            o = BLOCK[kt][0] + (i - kt) * P
                            ins = pe.matmul(accs[t % 4][:, i * P:(i + 1) * P], inner[:, h % 2, o:o + P],
                                            tv[:, kt, h * P:(h + 1) * P], start=(kt == 0), stop=(kt == i))
                    ins.then_inc(acc_done, 1)

                def ret_turn(h):
                    t = aux_at["rt", h]
                    aux_free(pe, t)
                    pe.wait_ge(acc_drained, a0 + B_R + h + 1)
                    for i in range(TT):
                        ins = pe.transpose(auxs[t % 4][:, i * P:(i + 1) * P], tmp[:, h % 2, i * P:(i + 1) * P],
                                           ident[:, :])
                    ins.then_inc(aux_done, 1)

                def start_out(j):
                    out_unit(u0 + U_OUT1, a0 + B_OUT1, j, 0, KT // 2)

                def turn_and_start(h):
                    ret_turn(h)
                    for j in {1: (0,), 2: (1, 2)}.get(h, ()):
                        start_out(j)

                order_ret(ret_scores, ret_values, turn_and_start)
                out_proj(u0 + U_OUT1, a0 + B_OUT1, lambda k: pe.wait_ge(y_ready, 4 + k - 3))

            cross_attention(0)
            ffn(0)
            odd_mixer()
            cross_attention(1)
            ffn(1)
            turn_out(KT - 1)
            mean(6)


def rotary_tables(dims, half, theta, order):
    inv = (1.0 / np.power(np.float32(theta), np.arange(half, dtype=np.float32) / np.float32(half))).astype(np.float32)
    ang = (np.arange(S, dtype=np.float32)[:, None] * inv[None, :]).astype(np.float32).astype(np.float64)
    cs = np.zeros((dims, 2, S))
    cs[:, 0] = 1.0
    for f in range(2 * half):
        cs[f, 0], cs[f, 1] = np.cos(ang[:, f % half]), np.sin(ang[:, f % half]) * (-1.0 if f < half else 1.0)
    return cs[order].astype(np.float32)


DIL_ORDER = np.concatenate([np.arange(0, 8), np.arange(16, 40), np.arange(8, 16), np.arange(40, DH)])


def constants():
    cs64 = rotary_tables(DH, 8, 500000.0, DIL_ORDER)
    cs_r = rotary_tables(P, 64, 10000.0, np.arange(P))
    dist = np.arange(P)[:, None] - np.arange(S)[None, :] + (S - P)
    past = dist >= 0
    count = (past & (dist <= 128)).astype(int) + (past & (dist % 4 == 0)) + (past & (dist % 16 == 0))
    band = np.where(count > 0, np.log(np.maximum(count, 1)), NEG).astype(np.float32)
    rel = np.arange(S)[None, :] - np.arange(P)[:, None]
    decay = np.stack([np.where(rel >= 0, (1 - 2.0 ** (-5 - h)) ** np.maximum(rel, 0), 0.0) * P ** -0.5
                      for h in range(RET_H)], axis=1).astype(np.float32)
    inv = np.stack([1.0 / np.minimum(np.arange(PAD) + 1, w) for w in WINDOWS]).astype(np.float32)
    return {
        "ident": np.eye(P, dtype=np.float32),
        "cs_d": np.ascontiguousarray(np.concatenate([cs64, cs64])),
        "cs_r": cs_r,
        "band": band,
        "decay": np.ascontiguousarray(decay),
        "invcnt": np.ascontiguousarray(np.broadcast_to(inv.reshape(1, -1), (P, 4 * PAD))),
    }


def weight_units(w):
    def rows(a):
        k, m = a.shape[0] // P, a.shape[1] // P
        return a.reshape(k, P, m, P).transpose(2, 1, 0, 3).reshape(m, P, k * P)

    def cols(a):
        c = a.shape[1] // 512
        return a.reshape(4, 2, P, c, 512).transpose(3, 0, 2, 1, 4).reshape(4 * c, P, UW)

    out = np.zeros((UNITS, P, UW), np.float32)
    n = [0]

    def put(u):
        out[n[0]:n[0] + len(u), :, 0:u.shape[2]] = u
        n[0] += len(u)

    even, odd = w["even_w_in"][0], w["odd_w_in"][0]
    def put_kv(layer):
        put(rows(w["xattn_wkv"][layer][:, 0:D]))
        put(cols(w["xattn_wkv"][layer][:, D:]))

    for layer in range(LAYERS):
        if layer == 0:
            put_kv(0)
            put(cols(even[:, 1024:1536]))
            put(rows(even[:, 0:1024]))
            put(rows(w["even_w_out"][0]))
        else:
            put(cols(odd[:, 1024:1536]))
            put(rows(odd[:, 0:1024].reshape(D, -1, DH)[:, :, DIL_ORDER].reshape(D, 1024)))
            put(cols(odd[:, 2560:3072]))
            put(rows(odd[:, 1536:2560]))
            put(rows(odd[:, 3072:3584]))
            put(rows(w["odd_w_out"][0]))
            put_kv(1)
        put(rows(w["xattn_wq"][layer]))
        put(rows(w["xattn_wo"][layer]))
        gu = rows(w["ffn_w_gate_up"][layer])
        put(gu.reshape(2, FT, P, UW).transpose(1, 0, 2, 3).reshape(2 * FT, P, UW))
        down = rows(w["ffn_w_down"][layer])
        for j in range(KT):
            for e in range(3):
                put(down[j:j + 1, :, e * UW:min((e + 1) * UW, DFF)])
    assert n[0] == UNITS
    return out


def kernel(**inputs):
    import concourse.bacc as bacc
    from concourse.bass_utils import run_bass_kernel_spmd

    w = {k: np.asarray(v) for k, v in inputs.items()}

    def columns(v):
        return v.reshape(-1, P).T

    arrays = dict(constants())
    arrays["x"] = np.ascontiguousarray(w["x"])
    arrays["mem"] = np.ascontiguousarray(w["mem"])
    arrays["weights"] = weight_units(w)
    arrays["vecs"] = np.ascontiguousarray(np.concatenate(
        [columns(w[k]) for k in ("even_mix_norm", "odd_mix_norm", "xattn_norm", "ffn_norm", "mem_norm", "pool_scale")],
        axis=1))
    arrays["ws_t"] = np.ascontiguousarray(w["sgu_w"][0].transpose(2, 0, 1))
    arrays["pool_w"] = np.ascontiguousarray(w["pool_w"][0].transpose(1, 0, 2))
    arrays["sgu_b"] = np.ascontiguousarray(np.broadcast_to(w["sgu_b"][0].reshape(1, -1), (P, 4 * P)))
    arrays["sgu_g"] = np.ascontiguousarray(np.broadcast_to(w["sgu_norm"][0][None], (P, S)))
    arrays["final_g"] = np.ascontiguousarray(np.broadcast_to(w["final_norm"][None], (P, D)))

    nc = bacc.Bacc("TRN2", target_bir_lowering=False, num_devices=1)
    named = {f"in_{k}": a for k, a in arrays.items()}
    d = {k: nc.dram_tensor(f"in_{k}", a.shape, F32, kind="ExternalInput").ap() for k, a in arrays.items()}
    d["out"] = nc.dram_tensor("out_h", (1, S, D), F32, kind="ExternalOutput").ap()
    program(nc, d)
    r = run_bass_kernel_spmd(nc, [named], core_ids=[0])
    return r.results[0]["out_h"]
```
